# Optimizing a Trainium2 kernel written in Bass

```python
import jax, jax.numpy as jnp
from jax import lax
import numpy as np
import math

D_MODEL = 1024
BATCH = 1
SEQ = 256
DEPTH = 1

MLA_HEADS = 8
MLA_NOPE = 64
MLA_ROPE = 32
MLA_QK = MLA_NOPE + MLA_ROPE
MLA_V = 64
MLA_W = MLA_HEADS * MLA_V
MLA_Q_RANK = 256
MLA_KV_RANK = 128
ROPE_THETA = 10000.0
Q_BLOCK = 128

RWKV_HEADS = 8
RWKV_N = 64
RWKV_W = RWKV_HEADS * RWKV_N
DECAY_LORA = 64
AAA_LORA = 64
GATE_LORA = 128

MIX_W = MLA_W + RWKV_W
MLA_IN = MLA_Q_RANK + MLA_KV_RANK + MLA_ROPE
RWKV_IN = 3 * RWKV_W + DECAY_LORA + AAA_LORA + GATE_LORA
IN_W = MLA_IN + RWKV_IN

N_GROUPS = 4
EXPERTS_PER_GROUP = 8
N_EXPERTS = N_GROUPS * EXPERTS_PER_GROUP
TOP_K = 2
D_EXPERT = 256

NORM_EPS = 1e-6
LNX_EPS = 64e-5


def rms_norm(x, g, eps=NORM_EPS):
    xf = x.astype(jnp.float32)
    y = xf * lax.rsqrt(jnp.mean(xf * xf, axis=-1, keepdims=True) + eps)
    return (y * g.astype(jnp.float32)).astype(x.dtype)

def rope_tables(positions):
    half = MLA_ROPE // 2
    inv_freq = 1.0 / (ROPE_THETA ** (jnp.arange(half, dtype=jnp.float32) / half))
    ang = positions.astype(jnp.float32)[..., None] * inv_freq
    return jnp.cos(ang)[:, :, None, :], jnp.sin(ang)[:, :, None, :]

def apply_rope(x, cos, sin):
    half = MLA_ROPE // 2
    xf = x.astype(jnp.float32)
    x1, x2 = xf[..., :half], xf[..., half:]
    return jnp.concatenate([x1 * cos - x2 * sin, x2 * cos + x1 * sin], axis=-1).astype(x.dtype)

def mla_group(c_q, c_kv, k_rope, positions, g_cq, w_uq, g_ckv, w_uk, w_uv, g_qn, g_kn):
    bsz, s, _ = c_q.shape
    q = jnp.einsum('bsr,rhd->bshd', rms_norm(c_q, g_cq), w_uq)
    ckv = rms_norm(c_kv, g_ckv)
    k_nope = jnp.einsum('bsr,rhd->bshd', ckv, w_uk)
    v = jnp.einsum('bsr,rhd->bshd', ckv, w_uv)
    k_rope_h = jnp.broadcast_to(k_rope[:, :, None, :], (bsz, s, MLA_HEADS, MLA_ROPE))
    k = jnp.concatenate([k_nope, k_rope_h], axis=-1)
    q = rms_norm(q, g_qn)
    k = rms_norm(k, g_kn)
    cos, sin = rope_tables(positions)
    q = jnp.concatenate([q[..., :MLA_NOPE], apply_rope(q[..., MLA_NOPE:], cos, sin)], axis=-1)
    k = jnp.concatenate([k[..., :MLA_NOPE], apply_rope(k[..., MLA_NOPE:], cos, sin)], axis=-1)
    scale = MLA_QK ** -0.5
    outs = []
    for blk in range(s // Q_BLOCK):
        q0 = blk * Q_BLOCK
        kend = q0 + Q_BLOCK
        scores = jnp.einsum('bqhd,bkhd->bhqk', q[:, q0:kend], k[:, :kend]).astype(jnp.float32) * scale
        causal = (q0 + jnp.arange(Q_BLOCK))[:, None] >= jnp.arange(kend)[None, :]
        scores = jnp.where(causal, scores, -jnp.inf)
        probs = jax.nn.softmax(scores, axis=-1).astype(v.dtype)
        outs.append(jnp.einsum('bhqk,bkhd->bqhd', probs, v[:, :kend]))
    return jnp.concatenate(outs, axis=1).reshape(bsz, s, MLA_W)

def rwkv7_group(feat, mu, w0, w2, a0, a2, g2, k_k, k_a, r_k, lnx_g, lnx_b):
    bsz, s, _ = feat.shape
    prev = jnp.pad(feat, ((0, 0), (1, 0), (0, 0)))[:, :-1]
    feat = feat + (prev - feat) * mu
    splits = np.cumsum([RWKV_W, RWKV_W, RWKV_W, DECAY_LORA, AAA_LORA]).tolist()
    r, k, v, wl, al, gl = jnp.split(feat, splits, axis=-1)
    w = -jax.nn.softplus(-(w0 + jnp.tanh(wl) @ w2)) - 0.5
    a = jax.nn.sigmoid(a0 + al @ a2)
    g = jax.nn.sigmoid(gl) @ g2
    heads = lambda t: t.reshape(bsz, s, RWKV_HEADS, RWKV_N).astype(jnp.float32)
    kk = heads(k * k_k)
    kk = kk * lax.rsqrt(jnp.sum(kk * kk, axis=-1, keepdims=True) + 1e-12)
    k = k * (1.0 + (a - 1.0) * k_a)
    rh, kh, vh, ah = heads(r), heads(k), heads(v), heads(a)
    decay = jnp.exp(-jnp.exp(heads(w)))

    def step(state, inp):
        r_t, k_t, v_t, kk_t, b_t, d_t = inp
        sa = jnp.einsum('bhvk,bhk->bhv', state, -kk_t)
        state = (state * d_t[:, :, None, :] + sa[..., None] * b_t[:, :, None, :]
                 + v_t[..., None] * k_t[:, :, None, :])
        return state, jnp.einsum('bhvk,bhk->bhv', state, r_t)

    tm = lambda t: jnp.swapaxes(t, 0, 1)
    state0 = jnp.zeros((bsz, RWKV_HEADS, RWKV_N, RWKV_N), jnp.float32)
    _, y = lax.scan(step, state0, (tm(rh), tm(kh), tm(vh), tm(kk), tm(kk * ah), tm(decay)))
    y = tm(y)
    mean = jnp.mean(y, axis=-1, keepdims=True)
    var = jnp.mean(jnp.square(y - mean), axis=-1, keepdims=True)
    y = ((y - mean) * lax.rsqrt(var + LNX_EPS)).reshape(bsz, s, RWKV_W)
    y = y * lnx_g.astype(jnp.float32) + lnx_b.astype(jnp.float32)
    bonus = jnp.sum(rh * kh * r_k.astype(jnp.float32), axis=-1, keepdims=True) * vh
    y = y + bonus.reshape(bsz, s, RWKV_W)
    return (y * g.astype(jnp.float32)).astype(feat.dtype)

def hier_moe(h, w_group, b_group, w_expert, b_expert, w_gate, w_up, w_down):
    bsz, s, d = h.shape
    t = h.reshape(bsz * s, d)
    n = t.shape[0]
    rows = jnp.arange(n)
    group_logits = (t @ w_group).astype(jnp.float32) + b_group.astype(jnp.float32)
    group_probs = jax.nn.softmax(group_logits, axis=-1)
    _, gsel = lax.top_k(group_logits, 1)
    gsel = gsel[:, 0]
    expert_logits = ((t @ w_expert).astype(jnp.float32) + b_expert.astype(jnp.float32)).reshape(
        n, N_GROUPS, EXPERTS_PER_GROUP)
    in_group = expert_logits[rows, gsel]
    top_vals, top_idx = lax.top_k(in_group, TOP_K)
    weights = jax.nn.softmax(top_vals, axis=-1) * group_probs[rows, gsel][:, None]
    expert_ids = gsel[:, None] * EXPERTS_PER_GROUP + top_idx
    combine = jnp.sum(jax.nn.one_hot(expert_ids, N_EXPERTS, dtype=jnp.float32) * weights[..., None],
                      axis=1).astype(t.dtype)
    y = jnp.zeros_like(t)
    for e in range(N_EXPERTS):
        hidden = jax.nn.silu(t @ w_gate[e]) * (t @ w_up[e])
        y = y + combine[:, e:e + 1] * (hidden @ w_down[e])
    return y.reshape(bsz, s, d)

def hybrid_layer(x, positions, g_mix, w_in, g_cq, w_uq, g_ckv, w_uk, w_uv, g_qn, g_kn, g_mla_out,
                 rw_mu, rw_w0, rw_w2, rw_a0, rw_a2, rw_g2, rw_k_k, rw_k_a, rw_r_k, rw_lnx_g, rw_lnx_b,
                 w_o, g_ffn, w_group, b_group, w_expert, b_expert, w_gate, w_up, w_down):
    h = rms_norm(x, g_mix)
    proj = h @ w_in
    c_q = proj[..., :MLA_Q_RANK]
    c_kv = proj[..., MLA_Q_RANK:MLA_Q_RANK + MLA_KV_RANK]
    k_rope = proj[..., MLA_Q_RANK + MLA_KV_RANK:MLA_IN]
    feat = proj[..., MLA_IN:]
    mla_out = rms_norm(mla_group(c_q, c_kv, k_rope, positions, g_cq, w_uq, g_ckv, w_uk, w_uv, g_qn, g_kn),
                       g_mla_out)
    rw_out = rwkv7_group(feat, rw_mu, rw_w0, rw_w2, rw_a0, rw_a2, rw_g2, rw_k_k, rw_k_a, rw_r_k,
                         rw_lnx_g, rw_lnx_b)
    x = x + jnp.concatenate([mla_out, rw_out], axis=-1) @ w_o
    x = x + hier_moe(rms_norm(x, g_ffn), w_group, b_group, w_expert, b_expert, w_gate, w_up, w_down)
    return x

def first_inputs(seed: int = 0) -> dict:
    key = jax.random.key(seed)
    ks = iter(jax.random.split(key, 40))
    L = DEPTH

    def nrm(shape, scale):
        return jax.random.normal(next(ks), shape, jnp.float32) * scale

    def gain(shape):
        return 1.0 + nrm(shape, 0.02)

    x = nrm((BATCH, SEQ, D_MODEL), 1.0)
    positions = (jnp.arange(SEQ, dtype=jnp.int32)[None, :]
                 + jax.random.randint(next(ks), (BATCH, 1), 0, 1024, jnp.int32))
    return {
        'x': x,
        'positions': positions,
        'g_mix': gain((L, D_MODEL)),
        'w_in': nrm((L, D_MODEL, IN_W), D_MODEL ** -0.5),
        'g_cq': gain((L, MLA_Q_RANK)),
        'w_uq': nrm((L, MLA_Q_RANK, MLA_HEADS, MLA_QK), MLA_Q_RANK ** -0.5),
        'g_ckv': gain((L, MLA_KV_RANK)),
        'w_uk': nrm((L, MLA_KV_RANK, MLA_HEADS, MLA_NOPE), MLA_KV_RANK ** -0.5),
        'w_uv': nrm((L, MLA_KV_RANK, MLA_HEADS, MLA_V), MLA_KV_RANK ** -0.5),
        'g_qn': gain((L, MLA_QK)),
        'g_kn': gain((L, MLA_QK)),
        'g_mla_out': gain((L, MLA_W)),
        'rw_mu': jax.random.uniform(next(ks), (L, RWKV_IN), jnp.float32, 0.0, 1.0),
        'rw_w0': jax.random.uniform(next(ks), (L, RWKV_W), jnp.float32, -4.0, 2.0),
        'rw_w2': nrm((L, DECAY_LORA, RWKV_W), 0.5 * DECAY_LORA ** -0.5),
        'rw_a0': nrm((L, RWKV_W), 0.1),
        'rw_a2': nrm((L, AAA_LORA, RWKV_W), 0.5 * AAA_LORA ** -0.5),
        'rw_g2': nrm((L, GATE_LORA, RWKV_W), GATE_LORA ** -0.5),
        'rw_k_k': 0.85 + nrm((L, RWKV_W), 0.02),
        'rw_k_a': 1.0 + nrm((L, RWKV_W), 0.02),
        'rw_r_k': nrm((L, RWKV_HEADS, RWKV_N), 0.1),
        'rw_lnx_g': gain((L, RWKV_W)),
        'rw_lnx_b': nrm((L, RWKV_W), 0.01),
        'w_o': nrm((L, MIX_W, D_MODEL), MIX_W ** -0.5),
        'g_ffn': gain((L, D_MODEL)),
        'w_group': nrm((L, D_MODEL, N_GROUPS), D_MODEL ** -0.5),
        'b_group': nrm((L, N_GROUPS), 0.01),
        'w_expert': nrm((L, D_MODEL, N_EXPERTS), D_MODEL ** -0.5),
        'b_expert': nrm((L, N_EXPERTS), 0.01),
        'w_gate': nrm((L, N_EXPERTS, D_MODEL, D_EXPERT), D_MODEL ** -0.5),
        'w_up': nrm((L, N_EXPERTS, D_MODEL, D_EXPERT), D_MODEL ** -0.5),
        'w_down': nrm((L, N_EXPERTS, D_EXPERT, D_MODEL), D_EXPERT ** -0.5),
    }

def first_block(x, positions, g_mix, w_in, g_cq, w_uq, g_ckv, w_uk, w_uv, g_qn, g_kn, g_mla_out,
              rw_mu, rw_w0, rw_w2, rw_a0, rw_a2, rw_g2, rw_k_k, rw_k_a, rw_r_k, rw_lnx_g, rw_lnx_b,
              w_o, g_ffn, w_group, b_group, w_expert, b_expert, w_gate, w_up, w_down):
    for l in range(DEPTH):
        x = hybrid_layer(x, positions, g_mix[l], w_in[l], g_cq[l], w_uq[l], g_ckv[l], w_uk[l], w_uv[l],
                         g_qn[l], g_kn[l], g_mla_out[l], rw_mu[l], rw_w0[l], rw_w2[l], rw_a0[l],
                         rw_a2[l], rw_g2[l], rw_k_k[l], rw_k_a[l], rw_r_k[l], rw_lnx_g[l], rw_lnx_b[l],
                         w_o[l], g_ffn[l], w_group[l], b_group[l], w_expert[l], b_expert[l],
                         w_gate[l], w_up[l], w_down[l])
    return x


DEPTH_2 = 2

D_PLE = 256
D_POOL = 512
D_CONV = D_MODEL - D_POOL
POOL_WINDOWS = (2, 4, 8, 16)
N_POOL_GROUPS = len(POOL_WINDOWS)
POOL_GROUP_DIM = D_POOL // N_POOL_GROUPS
CONV_WIDTH = 31
D_IN_PROJ = D_POOL + 2 * D_CONV
D_FF_DENSE = 2816
N_EXPERTS_2 = 8
D_FF_EXPERT = 3584
N_DENSE = (DEPTH_2 + 1) // 2
N_MOE = DEPTH_2 // 2
DEEPNORM_ALPHA = (2.0 * DEPTH_2) ** 0.25
DEEPNORM_BETA = (8.0 * DEPTH_2) ** -0.25
LN_EPS = 1e-5


def layer_norm(x, g, b):
    xf = x.astype(jnp.float32)
    mu = jnp.mean(xf, axis=-1, keepdims=True)
    var = jnp.mean(jnp.square(xf - mu), axis=-1, keepdims=True)
    y = (xf - mu) * lax.rsqrt(var + LN_EPS)
    return (y * g.astype(jnp.float32) + b.astype(jnp.float32)).astype(x.dtype)

def causal_multiscale_pool(u):
    B, S, _ = u.shape
    uf = u.astype(jnp.float32).reshape(B, S, N_POOL_GROUPS, POOL_GROUP_DIM)
    cs = jnp.cumsum(uf, axis=1)
    pos = jnp.arange(S, dtype=jnp.float32)[None, :, None]
    outs = []
    for gi, w in enumerate(POOL_WINDOWS):
        c = cs[:, :, gi]
        prev = jnp.pad(c, ((0, 0), (w, 0), (0, 0)))[:, :S]
        count = jnp.minimum(pos + 1.0, float(w))
        outs.append((c - prev) / count - uf[:, :, gi])
    return jnp.stack(outs, axis=2).astype(u.dtype)

def pool_mixer(u, w_grp, scale):
    d = causal_multiscale_pool(u)
    y = jnp.einsum('bsgc,gcd->bsgd', d, w_grp)
    return y.reshape(u.shape) * scale

def conformer_conv(a, gate, w_dw, b_dw, g_ln, b_ln, w_pw):
    v = a * jax.nn.sigmoid(gate)
    vp = jnp.pad(v, ((0, 0), (CONV_WIDTH - 1, 0), (0, 0)))
    y = lax.conv_general_dilated(
        vp, w_dw[:, None, :].astype(v.dtype), window_strides=(1,), padding='VALID',
        dimension_numbers=('NWC', 'WIO', 'NWC'), feature_group_count=D_CONV) + b_dw
    y = jax.nn.silu(layer_norm(y, g_ln, b_ln))
    return y @ w_pw

def swiglu(h, w1, w3, w2):
    return (jax.nn.silu(h @ w1) * (h @ w3)) @ w2

def moe_swiglu(h, w_router, w1, w3, w2):
    B, S, D = h.shape
    t = h.reshape(B * S, D)
    logits = (t @ w_router).astype(jnp.float32)
    top_vals, top_idx = lax.top_k(logits, TOP_K)
    top_w = jax.nn.softmax(top_vals, axis=-1)
    gates = jnp.sum(jax.nn.one_hot(top_idx, N_EXPERTS_2, dtype=jnp.float32) * top_w[..., None],
                    axis=1).astype(h.dtype)
    out = jnp.zeros_like(t)
    for e in range(N_EXPERTS_2):
        out = out + gates[:, e:e + 1] * swiglu(t, w1[e], w3[e], w2[e])
    return out.reshape(B, S, D)

def second_inputs(seed: int = 0) -> dict:
    key = jax.random.key(seed)
    ks = iter(jax.random.split(key, 32))
    f32 = jnp.float32

    def nrm(shape, scale):
        return jax.random.normal(next(ks), shape, f32) * scale

    def gain(shape):
        return 1.0 + nrm(shape, 0.02)

    L = DEPTH_2
    return {
        "x": nrm((BATCH, SEQ, D_MODEL), 1.0),
        "p": nrm((DEPTH_2, BATCH, SEQ, D_PLE), 1.0),
        "w_in": nrm((L, D_MODEL, D_IN_PROJ), D_MODEL ** -0.5),
        "pool_w": nrm((L, N_POOL_GROUPS, POOL_GROUP_DIM, POOL_GROUP_DIM), POOL_GROUP_DIM ** -0.5),
        "pool_scale": gain((L, D_POOL)),
        "conv_w": nrm((L, CONV_WIDTH, D_CONV), CONV_WIDTH ** -0.5),
        "conv_b": nrm((L, D_CONV), 0.02),
        "conv_ln_g": gain((L, D_CONV)),
        "conv_ln_b": nrm((L, D_CONV), 0.02),
        "conv_pw": nrm((L, D_CONV, D_CONV), D_CONV ** -0.5),
        "w_out": nrm((L, D_MODEL, D_MODEL), DEEPNORM_BETA * D_MODEL ** -0.5),
        "ln1_g": gain((L, D_MODEL)),
        "ln1_b": nrm((L, D_MODEL), 0.02),
        "dense_w1": nrm((N_DENSE, D_MODEL, D_FF_DENSE), D_MODEL ** -0.5),
        "dense_w3": nrm((N_DENSE, D_MODEL, D_FF_DENSE), D_MODEL ** -0.5),
        "dense_w2": nrm((N_DENSE, D_FF_DENSE, D_MODEL), DEEPNORM_BETA * D_FF_DENSE ** -0.5),
        "router_w": nrm((N_MOE, D_MODEL, N_EXPERTS_2), D_MODEL ** -0.5),
        "exp_w1": nrm((N_MOE, N_EXPERTS_2, D_MODEL, D_FF_EXPERT), D_MODEL ** -0.5),
        "exp_w3": nrm((N_MOE, N_EXPERTS_2, D_MODEL, D_FF_EXPERT), D_MODEL ** -0.5),
        "exp_w2": nrm((N_MOE, N_EXPERTS_2, D_FF_EXPERT, D_MODEL), DEEPNORM_BETA * D_FF_EXPERT ** -0.5),
        "ln2_g": gain((L, D_MODEL)),
        "ln2_b": nrm((L, D_MODEL), 0.02),
        "ple_gate_w": nrm((L, D_MODEL, D_MODEL), D_MODEL ** -0.5),
        "ple_w": nrm((L, D_PLE, D_MODEL), DEEPNORM_BETA * D_PLE ** -0.5),
    }

def second_block(x, p, w_in, pool_w, pool_scale, conv_w, conv_b, conv_ln_g, conv_ln_b, conv_pw,
              w_out, ln1_g, ln1_b, dense_w1, dense_w3, dense_w2, router_w, exp_w1, exp_w3,
              exp_w2, ln2_g, ln2_b, ple_gate_w, ple_w):
    for i in range(DEPTH_2):
        u = x @ w_in[i]
        u_pool = u[..., :D_POOL]
        u_val = u[..., D_POOL:D_POOL + D_CONV]
        u_gate = u[..., D_POOL + D_CONV:]
        y_pool = pool_mixer(u_pool, pool_w[i], pool_scale[i])
        y_conv = conformer_conv(u_val, u_gate, conv_w[i], conv_b[i],
                                conv_ln_g[i], conv_ln_b[i], conv_pw[i])
        mix = jnp.concatenate([y_pool, y_conv], axis=-1) @ w_out[i]
        x = layer_norm(DEEPNORM_ALPHA * x + mix, ln1_g[i], ln1_b[i])
        j = i // 2
        if i % 2 == 0:
            f = swiglu(x, dense_w1[j], dense_w3[j], dense_w2[j])
        else:
            f = moe_swiglu(x, router_w[j], exp_w1[j], exp_w3[j], exp_w2[j])
        x = layer_norm(DEEPNORM_ALPHA * x + f, ln2_g[i], ln2_b[i])
        x = x + jax.nn.sigmoid(x @ ple_gate_w[i]) * (p[i] @ ple_w[i])
    return x


def setup_inputs(seed=0):
    out = dict(first_inputs(seed))
    for name, value in second_inputs(seed + 1).items():
        if name != "x":
            out[name + "_2"] = value
    return out


def reference(
    x, positions, g_mix, w_in, g_cq, w_uq, g_ckv, w_uk, w_uv, g_qn, g_kn, g_mla_out, rw_mu,
    rw_w0, rw_w2, rw_a0, rw_a2, rw_g2, rw_k_k, rw_k_a, rw_r_k, rw_lnx_g, rw_lnx_b, w_o, g_ffn,
    w_group, b_group, w_expert, b_expert, w_gate, w_up, w_down, p_2, w_in_2, pool_w_2,
    pool_scale_2, conv_w_2, conv_b_2, conv_ln_g_2, conv_ln_b_2, conv_pw_2, w_out_2, ln1_g_2,
    ln1_b_2, dense_w1_2, dense_w3_2, dense_w2_2, router_w_2, exp_w1_2, exp_w3_2, exp_w2_2,
    ln2_g_2, ln2_b_2, ple_gate_w_2, ple_w_2,
):
    x = first_block(
        x, positions, g_mix, w_in, g_cq, w_uq, g_ckv, w_uk, w_uv, g_qn, g_kn, g_mla_out, rw_mu,
        rw_w0, rw_w2, rw_a0, rw_a2, rw_g2, rw_k_k, rw_k_a, rw_r_k, rw_lnx_g, rw_lnx_b, w_o,
        g_ffn, w_group, b_group, w_expert, b_expert, w_gate, w_up, w_down,
    )
    return second_block(
        x, p_2, w_in_2, pool_w_2, pool_scale_2, conv_w_2, conv_b_2, conv_ln_g_2, conv_ln_b_2,
        conv_pw_2, w_out_2, ln1_g_2, ln1_b_2, dense_w1_2, dense_w3_2, dense_w2_2, router_w_2,
        exp_w1_2, exp_w3_2, exp_w2_2, ln2_g_2, ln2_b_2, ple_gate_w_2, ple_w_2,
    )


_drawn_inputs = setup_inputs


def setup_inputs(seed=0):
    import zlib

    import numpy as np

    out = dict(_drawn_inputs(seed))
    spreads = {}
    factors = {'g_cq': 39.512,
     'rw_k_k': 44.671,
     'rw_k_a': 3.895,
     'rw_lnx_g': 7.944,
     'rw_lnx_b': 34.814,
     'b_group': 39.959,
     'b_expert': 22.173,
     'pool_scale_2': 5.848,
     'conv_b_2': 6.229,
     'conv_ln_g_2': 21.887,
     'conv_ln_b_2': 24.998,
     'g_kn': 16.512,
     'g_ckv': 3.293,
     'g_qn': 3.153,
     'g_mla_out': 6.902,
     'g_ffn': 4.526}
    for name, (base, spread) in spreads.items():
        noise = np.random.default_rng([zlib.crc32(name.encode()), seed]).standard_normal(out[name].shape)
        drawn = base * np.exp(spread * noise) if base else spread * noise
        out[name] = __import__('jax').numpy.asarray(drawn.astype(out[name].dtype))
    for name, factor in factors.items():
        out[name] = (out[name] * factor).astype(out[name].dtype)
    return out
```

```python
from contextlib import ExitStack

import numpy as np

import concourse.bass as bass
from concourse import mybir

F32 = mybir.dt.float32
I32 = mybir.dt.int32
U32 = mybir.dt.uint32
ALU = mybir.AluOpType
ACT = mybir.ActivationFunctionType
AX_X = mybir.AxisListType.X
RMAX = bass.bass_isa.ReduceOp.max

P = 128
D = 1024
S = 256
TT = S // P
KD = D // P
EPS = 1e-6

H, NOPE, ROPE, VD = 8, 64, 32, 64
QK = NOPE + ROPE
HALF = ROPE // 2
Q_RANK, KV_RANK = 256, 128
C_W = Q_RANK + KV_RANK + ROPE
ROPE_THETA = 10000.0
TWO_PI = 6.283185307179586
NEG = -1.0e30

RW = 512
N = 64
J = RW // P
NCH = S // N
NF = 14
LVL = (1, 2, 4, 8, 16, 32)
DECAY = 0.6065306597126334
LNX_EPS = 64e-5
IN_W = C_W + NF * P

NG, EG, E1, F1 = 4, 8, 32, 256
CAP1 = 32
L2 = 2
D_POOL, D_CONV, CW = 512, 512, 31
IN2 = D_POOL + 2 * D_CONV
NPC = D_POOL // P
WINDOWS = (2, 4, 8, 16)
D_PLE = 256
FD = 2816
E2, F2 = 8, 3584
CAP2 = 128
SMALL = CAP2 // 2
ALPHA = float((2.0 * L2) ** 0.25)
LN_EPS = 1e-5

ROWS = {}
_at = 0
for _name, _n in (("mu", NF), ("w0", J), ("a0", J), ("k_k", J), ("k_a", J), ("r_k", J), ("g_cq", 2), ("g_ckv", 1),
                  ("g_mla", J), ("pool_scale", L2 * NPC), ("conv_b", L2 * NPC), ("ln_g", L2 * NPC), ("ln_b", L2 * NPC)):
    ROWS[_name] = _at
    _at += _n
NROWS = _at

PLACE = 4096
PLACES = 7
HALFP = PLACE // 2
HALVES = 12


class Steps:

    def __init__(self, sem, names):
        self.sem = sem
        self.value = {name: n + 1 for n, name in enumerate(names)}
        self.raised = 0

    def raise_by(self, instruction, name):
        self.raised += 1
        assert self.value[name] == self.raised, (name, self.raised)
        instruction.then_inc(self.sem, 1)

    def __call__(self, name):
        return self.sem, self.value[name]


STEPS = {
    "consts": [
        "ident", "all",
    ],
    "pe_front": [
        "cols", "xT 0 0", "xT 0 1", "xT 1 0", "xT 1 1", "c 0", "c 1", "feat 0", "feat 1", "feat 2", "feat 3", "feat 4",
        "feat 5", "feat 6", "projected", "qkv 0", "qkv 1", "qkT 0", "qkT 1", "qkT 2", "qkT 3", "qkT 4", "qkT 5",
        "qkT 6", "qkT 7", "scores 0", "scores 1", "pT 0", "pT 1", "pv", "mlaT", "low rank", "kk sums", "turned 0 0",
        "turned 0 1", "bonus", "turned 1 0", "turned 1 1", "turned 2 0", "turned 2 1", "gram 0 0", "gram 0 1",
        "gram 1 0", "gram 1 1", "lx 0 0", "lx 0 1", "lx 1 0", "lx 1 1", "xlxT 1 0", "xlx 1 0", "xlxT 1 1", "xlx 1 1",
        "lx 2 0", "lx 2 1", "xlxT 2 0", "xlx 2 0", "xlxT 2 1", "xlx 2 1", "lx 3 0", "lx 3 1", "xlxT 3 0", "xlx 3 0",
        "xlxT 3 1", "xlx 3 1", "lx 4 0", "lx 4 1", "xlxT 4 0", "xlx 4 0", "xlxT 4 1", "xlx 4 1", "lx 5 0", "lx 5 1",
        "xlxT 5 0", "xlxT 5 1", "akv 0", "akv 1", "u 0", "state 0", "y 0", "kk s 1", "r s 1", "u 1", "state 1", "y 1",
        "kk s 2", "r s 2", "u 2", "state 2", "y 2", "kk s 3", "r s 3", "u 3", "y 3", "g", "yT", "w_o 0", "w_o 1",
    ],
    "act_front": [
        "x squares 0", "x squares 1", "x std", "c 0", "c 1", "raw 0", "raw 1", "raw 2", "raw 3", "raw 4", "raw 5",
        "raw 6", "c squares", "c std", "qk squares 0", "v 0", "qk squares 1", "v 1", "k rope squares", "qk std", "trig",
        "qkT 0", "qkT 1", "qkT 2", "qkT 3", "probs 0", "probs 1", "pT0", "pT1", "mla squares", "mla std", "tanh",
        "sig w", "sig a", "kk std", "d inv", "d inc", "d ex", "turned 0 0", "turned 0 1", "turned 1 0", "turned 1 1",
        "turned 2 0", "turned 2 1", "lx 1 0", "lx 1 1", "lx 2 0", "lx 2 1", "lx 3 0", "lx 3 1", "lx 4 0", "lx 4 1",
        "lx 5 0", "lx 5 1", "u 0", "u 1", "u 2", "u 3", "g", "y std",
    ],
    "dve_front": [
        "x var", "xn 0", "xn 1", "xT 0 0", "xT 0 1", "xT 1 0", "xT 1 1", "cols", "c var", "c normed", "mixed", "cT",
        "qk var", "angles", "qk", "qkT 4", "qkT 5", "qkT 6", "qkT 7", "max 0", "max 1", "pT1", "mla", "mla var",
        "mla normed", "kk squares", "kk var", "cum", "tilde", "bonus", "low 0 0", "low 0 1", "inv 0 0", "invT 0 0",
        "inv 0 1", "invT 0 1", "low 1 0", "low 1 1", "inv 1 0", "invT 1 0", "inv 1 1", "invT 1 1", "low 2 0", "low 2 1",
        "inv 2 0", "invT 2 0", "inv 2 1", "invT 2 1", "low 3 0", "low 3 1", "inv 3 0", "invT 3 0", "inv 3 1",
        "invT 3 1", "low 4 0", "low 4 1", "inv 4 0", "invT 4 0", "inv 4 1", "invT 4 1", "low 5 0", "low 5 1",
        "invT 5 0", "invT 5 1", "rn 0", "state 0", "y 0", "rn 1", "state 1", "y 1", "rn 2", "state 2", "y 2", "rn 3",
        "y 3", "y var", "y gated", "mixT", "x1 0", "x1 1",
    ],
    "moe1_pe": [
        "xT 0", "xT 1", "xT 2", "xT 3", "logits", "places",
    ],
    "moe1_act": [
        "squares 0", "squares 1", "std", "exp",
    ],
    "moe1_dve": [
        "var", "xn 0", "xn 1", "xT 0", "xT 1", "xT 2", "xT 3", "diffs", "mask", "over", "done",
    ],
    "block2_pe": [
        "xT mix 0 0", "xT mix 0 1", "xT mix 0 2", "xT mix 0 3", "taps 0", "pool 0", "conv sum 0", "conv squares 0",
        "mix 0", "xT ffn 0 0", "xT ffn 0 1", "xT ffn 0 2", "xT ffn 0 3", "up 0", "hT 0 0", "hT 0 1", "up 1", "hT 1 0",
        "hT 1 1", "up 2", "hT 2 0", "hT 2 1", "up 3", "hT 3 0", "hT 3 1", "up 4", "hT 4 0", "hT 4 1", "up 5", "hT 5 0",
        "hT 5 1", "xT ple 0 0", "xT ple 0 1", "xT ple 0 2", "xT ple 0 3", "pT 0", "ple gate 0 0", "ple 0 0",
        "xT mix 1 0", "xT mix 1 1", "xT mix 1 2", "xT mix 1 3", "taps 1", "pool 1", "conv sum 1", "conv squares 1",
        "mix 1", "xT ffn 1 0", "xT ffn 1 1", "xT ffn 1 2", "xT ffn 1 3", "logits", "places", "xT ple 1 0", "xT ple 1 1",
        "xT ple 1 2", "xT ple 1 3", "pT 1", "ple gate 1 0", "ple gate 1 1", "ple 1 0", "ple 1 1",
    ],
    "block2_act": [
        "xT mix 0 0", "xT mix 0 1", "xT mix 0 2", "xT mix 0 3", "pool in 0", "gate 0", "squares 0", "conv std 0",
        "silu 0", "conv out 0", "ln1 std 0", "xT ffn 0 0", "xT ffn 0 1", "xT ffn 0 2", "xT ffn 0 3", "silu 0 0",
        "silu 0 1", "silu 1 0", "silu 1 1", "silu 2 0", "silu 2 1", "silu 3 0", "silu 3 1", "silu 4 0", "silu 4 1",
        "silu 5 0", "silu 5 1", "ln2 std 0", "xT ple 0 0", "xT ple 0 1", "xT ple 0 2", "xT ple 0 3", "pT 0",
        "ple gate 0 0", "ple gate 0 1", "xT mix 1 0", "xT mix 1 1", "xT mix 1 2", "xT mix 1 3", "pool in 1", "gate 1",
        "squares 1", "conv std 1", "silu 1", "conv out 1", "ln1 std 1", "xT ffn 1 0", "xT ffn 1 1", "xT ffn 1 2",
        "xT ffn 1 3", "x kept 0", "x kept 1", "exp", "ln2 std 1", "xT ple 1 0", "xT ple 1 1", "xT ple 1 2",
        "xT ple 1 3", "pT 1", "ple gate 1 0", "ple gate 1 1",
    ],
    "block2_dve": [
        "pads 0", "pooled 0", "conv 0", "pool out 0", "centred 0", "conv var 0", "conv normed 0", "ln1 var 0", "ln1 0",
        "hidden 0 0", "hT 0 0", "hidden 0 1", "hT 0 1", "hidden 1 0", "hT 1 0", "hidden 1 1", "hT 1 1", "hidden 2 0",
        "hT 2 0", "hidden 2 1", "hT 2 1", "hidden 3 0", "hT 3 0", "hidden 3 1", "hT 3 1", "hidden 4 0", "hT 4 0",
        "hidden 4 1", "hT 4 1", "hidden 5 0", "hT 5 0", "hidden 5 1", "hT 5 1", "ffn 0", "ln2 var 0", "ln2 0", "x 0",
        "pads 1", "pooled 1", "conv 1", "pool out 1", "centred 1", "conv var 1", "conv normed 1", "ln1 var 1", "ln1 1",
        "diffs", "mask", "over", "ffn 1", "ln2 var 1", "ln2 1", "out 0", "out 1",
    ],
}

def build(nc, x, positions, g_mix, w_in, g_cq, w_uq, g_ckv, w_uk, w_uv, g_qn, g_kn, g_mla_out, rw_mu, rw_w0, rw_w2,
          rw_a0, rw_a2, rw_g2, rw_k_k, rw_k_a, rw_r_k, rw_lnx_g, rw_lnx_b, w_o, g_ffn, w_group, b_group, w_expert,
          b_expert, w_gate, w_up, w_down, p_2, w_in_2, pool_w_2, pool_scale_2, conv_w_2, conv_b_2, conv_ln_g_2,
          conv_ln_b_2, conv_pw_2, w_out_2, ln1_g_2, ln1_b_2, dense_w1_2, dense_w3_2, dense_w2_2, router_w_2,
          exp_w1_2, exp_w3_2, exp_w2_2, ln2_g_2, ln2_b_2, ple_gate_w_2, ple_w_2, out):
    with ExitStack() as ctx:
        def sb(name, shape, dtype=F32):
            return ctx.enter_context(nc.sbuf_tensor(name, shape, dtype))

        def sem(name):
            return ctx.enter_context(nc.semaphore(name))

        def steps(name):
            return Steps(sem(name), STEPS[name])

        ring = sb("ring", [P, PLACES * PLACE])
        x_sb = sb("x_sb", [P, TT, D])
        xn = sb("xn", [P, TT, D])
        xT = sb("xT", [P, KD, S])
        work = sb("work", [P, 14368])
        c_sb = sb("c_sb", [P, TT, C_W])
        ident = sb("ident", [P, P])
        ones = sb("ones", [P, P])
        before = sb("before", [P, P])
        iota = sb("iota", [P, P])
        iota_q = sb("iota_q", [P, P])
        zero = sb("zero", [P, P // 2])
        thr = sb("thr", [P, 8])
        rows = sb("rows", [P, P])
        cols = sb("cols", [P, NROWS])
        sg = sb("sg", [P, S])
        st = sb("st", [P, J, N])
        st2 = sb("st2", [P, J, N])
        small = sb("small", [P, 512])
        pos_i = sb("pos_i", [P, TT], I32)
        gcol = sb("gcol", [P, 2, KD])
        ps = ctx.enter_context(nc.psum_tensor("ps", [P, 8, 512], F32))

        def cut(base, at, *shape):
            n = int(np.prod(shape))
            v = base[:, at:at + n]
            names = "abcde"[:len(shape)]
            if len(shape) == 1:
                return v
            return v.rearrange(f"p ({' '.join(names)}) -> p {' '.join(names)}", **dict(zip(names[1:], shape[1:])))

        def spread(v, axis, n):
            v = v.unsqueeze(axis)
            return v.to_broadcast([*v.shape[:axis], n, *v.shape[axis + 1:]])

        FC = 10 * HALFP
        w2a2 = cut(ring, FC, RW)
        g2w = cut(ring, FC + 512, RW)
        lnx = cut(ring, FC + 1024, 2, RW)
        cmask = cut(ring, FC + 2048, S)
        gqk = cut(ring, FC + 2304, 2, QK)
        lvl = cut(ring, FC + 2496, len(LVL), N)
        rst = cut(ring, FC + 2880, S)
        blk = cut(ring, FC + 3136, P)
        m_lt = cut(ring, FC + 3264, N)
        m_le = cut(ring, FC + 3328, N)
        idh = cut(ring, FC + 3392, N)
        hsel = cut(ring, FC + 3456, 2)
        w_in_sb = cut(ring, 0, KD, IN_W)
        w_uq_sb = cut(ring, 17664, 2, H * QK)
        w_uk_sb = cut(ring, 19200, H * NOPE)
        w_uv_sb = cut(ring, 19712, H * VD)
        w_o_a = cut(ring, 0, 4, D)
        w_o_b = cut(ring, 6 * PLACE, 4, D)

        raw = cut(work, 0, NF, S + 1)
        feat = cut(work, 3600, NF, S)
        cT = cut(work, 0, 3, S)
        sq = cut(work, 7184, TT, H * QK + H * NOPE)
        qkT = cut(work, 7184, 2 * H, S)
        qk = cut(work, 11280, TT, 2 * H, QK)
        probs0 = cut(work, 11280, H, P)
        probs1 = cut(work, 12304, H, S)
        pT0 = cut(work, 0, H, P)
        pT1 = cut(work, 1024, 2 * H, P)
        mla = cut(work, 7184, TT, RW)
        vt = cut(xn[:, 0, :], 0, TT, H * VD)
        rope_t = cut(xn[:, 1, :], 0, 4, 512 // 2)
        r_f, k_f, v_f = (cut(work, 3600 + 1024 * n, J, S) for n in range(3))
        wa_f = cut(work, 3600 + 12 * S, S)
        gl_f = cut(work, 3600 + 13 * S, S)
        a_f = cut(work, 7184, J, S)
        sig_f = cut(work, 8208, J, S)
        cum = cut(work, 9232, J, S)
        d_inc = cut(work, 10256, J, S)
        d_inv = cut(work, 11280, J, S)
        d_ex = cut(work, 12304, J, S)
        tmp_f = cut(work, 13328, J, S)
        kk_f = cut(xn[:, 1, :], 0, J, S)
        bt_f, kt_f, rt_f = (cut(work, 1024 * n, J, S) for n in range(3))
        rk_f = a_f
        v_t, b_t, k_t = (cut(work, at, TT, RW) for at in (8208, 9232, 7184))
        gram = cut(work, 10256, TT, 2, 2, 2 * J * N)
        inv = cut(work, 3600, TT, 2 * J, N)
        invT = cut(work, 4624, TT, 2 * J, N)
        yy = cut(work, 5648, TT, 2 * J, N)
        low = cut(xn[:, 0, :], 0, TT, 2 * J, N)
        akv = yy
        u_t = inv
        rn = cut(xn[:, 0, :], 0, 2 * J, N)
        y_t = cut(work, 0, TT, RW)
        y_q = cut(work, 1024, TT, RW)
        gl_t = cut(work, 2048, TT, RW)
        mixT = xT
        at_small = [0]

        def tiny(*shape):
            at = at_small[0]
            at_small[0] += int(np.prod(shape))
            return cut(small, at, *shape)

        ss_x, rs_x = tiny(2), tiny(2)
        ss_c, rs_c = tiny(2, 2), tiny(2, 2)
        ss_qk, rs_qk, ss_kr = tiny(2, 16), tiny(2, 16), tiny(2)
        inv_freq, posf = tiny(HALF), tiny(2)
        ang, turn, trig = tiny(2, HALF), tiny(2, 2, HALF), tiny(2, 2, HALF)
        mx, den = tiny(2, H), tiny(2, H)
        bonus, d_end = tiny(2, H), tiny(J, NCH)
        mean, var = tiny(16), tiny(16)

        ld_x, ld_win, ld_rows, ld_front = sem("ld_x"), sem("ld_win"), sem("ld_rows"), sem("ld_front")
        ld_uq, ld_woa, ld_wob = sem("ld_uq"), sem("ld_woa"), sem("ld_wob")
        out_written = sem("out_written")
        pool_step, act_step, dve_step = sem("pool_step"), sem("act_step"), sem("dve_step")
        consts = steps("consts")
        pe_f, act_f, dve_f = steps("pe_front"), steps("act_front"), steps("dve_front")

        ga_sel = cut(work, 0, TT, P)
        sc_sel = cut(work, 256, TT, P)
        sc_T = cut(work, 512, TT, P)
        xg = cut(work, 768, KD, P)
        hs = cut(work, 1792, 2, 512)
        hh = cut(work, 2816, 2, 512)
        hT = cut(work, 3840, 4, P)
        yg = cut(work, 4352, D)
        RT = 7480
        at_rt = [RT]

        def rt(*shape):
            at = at_rt[0]
            at_rt[0] += int(np.prod(shape))
            return cut(work, at, *shape)

        glog, elog, gtop, etop = rt(2, 8), rt(2, E1), rt(2, 8), rt(2, 8)
        gtop_i, etop_i = rt(2, 8), rt(2, 8)
        gsel, esel = rt(2), rt(2, 2)
        g_one, e_one = rt(2, NG), rt(2, 2, 8)
        in_group, spread_g = rt(2, 8), rt(2, NG, 8)
        diffs, w2 = rt(2, 5), rt(2, 2)
        gp = rt(2)
        comb8, mask8 = rt(2, 8), rt(2, 8)
        comb, mask, slot = rt(2, E1), rt(2, E1), rt(2, E1)
        over, over8 = rt(1), rt(8)
        small_e = rt(E2)
        slot_hi = rt(2, E2 + 1)
        over_i = sb("over_i", [P, 1], I32)
        small_i = sb("small_i", [P, E2], I32)
        rtr = sb("rtr", [P, KD * (NG + E1) + NG + E1 + KD * E2])
        wg_sb = cut(rtr, 0, KD, NG)
        we_sb = cut(rtr, KD * NG, KD, E1)
        bg_sb = cut(rtr, KD * (NG + E1), NG)
        be_sb = cut(rtr, KD * (NG + E1) + NG, E1)
        w_router = cut(rtr, KD * (NG + E1) + NG + E1, KD, E2)

        up = cut(work, 0, NPC, 16 + S)
        sum_a = cut(work, 1088, NPC, 16 + S)
        sum_b = cut(work, 2176, NPC, 16 + S)
        pooled = cut(work, 3264, NPC, S)
        vp = cut(work, 4288, NPC, CW - 1 + S)
        yv = cut(work, 5432, NPC, S)
        sv = cut(work, 6456, NPC, S)
        mT = cut(work, 7480, KD, S)
        mean_b = cut(work, 9528, S)
        rstd_b = cut(work, 9784, S)
        lnp = cut(work, 10040, 4, D)
        c_flat = c_sb[:, :, :].rearrange("p t n -> p (t n)")
        conv_rows = cut(c_flat, 0, L2, P)
        cw = cut(c_flat, 2 * P, CW, NPC)
        rc = cut(c_flat, 2 * P + CW * NPC, NPC, 16)
        p_sb = cut(work, 4352, TT, D_PLE)
        pT = cut(work, 4864, 2, S)
        gate_s = cut(work, 0, TT, D)
        stats = cut(small, 300, TT, 2, 6)
        mv = cut(small, 324, TT, 2)
        rstd = cut(small, 328, TT)

        ld_rtr, ld_conv, ld_pool, ld_lnp, ld_p = sem("ld_rtr"), sem("ld_conv"), sem("ld_pool"), sem("ld_lnp"), sem("ld_p")
        m1 = {k: steps(f"moe1_{k}") for k in ("pe", "act", "dve")}
        piece1 = [sem(f"piece1_{n}") for n in range(HALVES)]
        used1 = sem("used1")
        q_sel, q_gath, q_xg, q_scT, q_silu, q_hid, q_hT, q_hTs, q_yg, q_scat, q_add, q_turn = (
            sem("q_" + n) for n in ("sel", "gathered", "xg", "scT", "silu", "hidden", "hT", "hTs", "yg", "scattered", "added",
                                    "turned"))
        landed = [sem(f"landed_{n}") for n in range(PLACES)]
        used = sem("used")
        bl = {k: steps(f"block2_{k}") for k in ("pe", "act", "dve")}
        e_sel, e_gath, e_xg, e_scT, e_turn, e_silu, e_hid, e_hT, e_hTs, e_yg, e_scat, e_add = (
            sem("e_" + n) for n in ("sel", "gathered", "xg", "scT", "turned", "silu", "hidden", "hT", "hTs", "yg", "scattered", "added"))
        more_done1, more_done2 = sem("more_done1"), sem("more_done2")
        q_sel_w, q_shift, e_sel_w, e_shift = sem("q_sel_w"), sem("q_shift"), sem("e_sel_w"), sem("e_shift")
        ld_last = sem("ld_last")

        NQ = E1 // 4
        UNITS = F2 // 512
        UD = [512] * (FD // 512) + [FD % 512]

        def half_place(i):
            return (i + 2) % HALVES

        def place(n):
            at = (n + 1) % PLACES * PLACE
            return ring[:, at:at + PLACE]

        def chunked(v, width):
            return v[:, 0:KD * width].rearrange("p (k n) -> p k n", k=KD)

        def ffn_order(units):
            order = []
            for u in range(units):
                order += [("w1", u), ("w3", u)] + ([("w2", u - 1)] if u else [])
            return order + [("w2", units - 1)]

        MIX = [("in", 0), ("in", 1), ("in", 2), ("pw", 0), ("out", 0), ("out", 1)]
        PLE = [("pg", 0), ("pg", 1), ("ple", 0)]
        DENSE = [(what, u) for u in range(len(UD)) for what in ("w1", "w3", "w2")]
        MOE = ffn_order(UNITS)
        MIX0, DENSE0 = 0, len(MIX)
        PLE0 = DENSE0 + len(DENSE)
        MIX1 = PLE0 + len(PLE)
        MOE0 = MIX1 + len(MIX)
        PLE1 = MOE0 + E2 * len(MOE)

        def read(n):
            return used, n + 1

        def read_moe(what, u):
            return MOE0 + MOE.index((what, u)) + 1

        def read_dense(what, u):
            return read(DENSE0 + DENSE.index((what, u)))

        assert len(MOE) % PLACES == 0 and len(MOE) == 3 * UNITS

        block = ctx.enter_context(nc.Block())

        def row(v, n):
            return v.rearrange("(a n) -> a n", a=1).to_broadcast([P, n])

        @block.sync
        def _(sp):
            for t in range(TT):
                sp.dma_start(x_sb[:, t, :], x[0, t * P:(t + 1) * P, :]).then_inc(ld_x, 16)
            for k in range(KD):
                sp.dma_start(w_in_sb[:, k, :], w_in[0].rearrange("(p k) n -> p k n", k=KD)[:, k, :]).then_inc(ld_win, 16)
            sp.dma_start(w_uq_sb, w_uq[0].rearrange("(k p) h d -> p k (h d)", p=P)).then_inc(ld_uq, 16)
            sp.dma_start(w_uk_sb, w_uk[0].rearrange("p h d -> p (h d)")).then_inc(ld_uq, 16)
            sp.dma_start(w_uv_sb, w_uv[0].rearrange("p h d -> p (h d)")).then_inc(ld_uq, 16)
            wo_rows = w_o[0].rearrange("(k p) n -> p k n", p=P)
            sp.dma_start(w_o_b, wo_rows[:, 4:8, :]).then_inc(ld_wob, 16)
            sp.wait_ge(*pe_f("projected"))
            sp.dma_start(w_o_a, wo_rows[:, 0:4, :]).then_inc(ld_woa, 16)
            def quad(q, first, it):
                for i in range(HALVES):
                    j = i % 4
                    at = half_place(i) * HALFP
                    dst = ring[:, at:at + HALFP]
                    src = (w_gate, w_up, w_down)[i // 4]
                    src = src[0][bass.ds(q * 4 + j, 1)] if not first else src[0][j:j + 1]
                    if first:
                        if i == 6:
                            sp.wait_ge(*pe_f("qkv 1"))
                        if i == 8:
                            sp.wait_ge(*dve_f("y gated"))
                            sp.wait_ge(*pe_f("g"))
                        if i == 10:
                            sp.wait_ge(*pe_f("w_o 1"))
                    else:
                        sp.wait_ge(used1, (it - 1) * HALVES + i + 1)
                    src = src.rearrange("a (p k) n -> p (a k n)", p=P)
                    sp.dma_start(dst, src).then_inc(piece1[half_place(i)], 16)

            quad(0, True, 0)
            with sp.Fori(1, NQ) as q:
                quad(q, False, q)
            sp.wait_ge(*m1["dve"]("over"))
            extra = sp.value_load(over_i[0:1, 0:1], min_val=0, max_val=S // CAP1 - 1)
            with sp.If(extra > 0):
                with sp.Fori(1, extra + 1) as r:
                    with sp.Fori(0, NQ) as q:
                        quad(q, False, r * NQ + q)
                sp.wait_ge(more_done1, 1)

            def piece(n, src, slot_free=True):
                if n >= PLACES:
                    sp.wait_ge(used, n - PLACES + 1)
                elif (n + 1) % PLACES == 6:
                    sp.wait_ge(*pe_f("w_o 1"))
                else:
                    sp.wait_ge(used1, (NQ - 1) * HALVES + min(HALVES, 4 * (n // 2 + 1)))
                dst = place(n)
                dst = dst[:, 0:int(np.prod(src.shape[1:]))]
                if len(src.shape) == 3:
                    dst = dst.rearrange("p (a b) -> p a b", a=src.shape[1])
                sp.dma_start(dst, src).then_inc(landed[(n + 1) % PLACES], 16)

            def mixer_pieces(l, n0):
                w_i = w_in_2[l].rearrange("(p k) n -> p k n", k=KD)
                w_u = w_out_2[l].rearrange("(k p) n -> p k n", p=P)
                for n, (what, a) in enumerate(MIX):
                    if what == "in":
                        src = w_i[:, :, a * 512:(a + 1) * 512]
                    elif what == "pw":
                        src = conv_pw_2[l].rearrange("(k p) n -> p k n", p=P)
                    else:
                        src = w_u[:, 4 * a:4 * a + 4, :]
                    piece(n0 + n, src)
                    if what == "pw":
                        sp.dma_start(place(n0 + n)[:, 4 * 512:5 * 512].rearrange("p (g d) -> p g d", g=NPC),
                                     pool_w_2[l].rearrange("g c d -> c g d")).then_inc(ld_pool, 16)

            def ple_pieces(l, n0):
                w_g = ple_gate_w_2[l].rearrange("(p k) n -> p k n", k=KD)
                piece(n0, w_g[:, 0:4, :])
                piece(n0 + 1, w_g[:, 4:8, :])
                piece(n0 + 2, ple_w_2[l].rearrange("(k p) n -> p k n", p=P))

            mixer_pieces(0, MIX0)
            for n, (what, u) in enumerate(DENSE):
                f0, f = 512 * u, UD[u]
                if what == "w2":
                    src = dense_w2_2[0][f0:f0 + f, :].rearrange("(p c) n -> p c n", p=P)
                else:
                    src = (dense_w1_2 if what == "w1" else dense_w3_2)[0].rearrange("(p k) f -> p k f", k=KD)[:, :, f0:f0 + f]
                piece(DENSE0 + n, src)
            ple_pieces(0, PLE0)
            mixer_pieces(1, MIX1)

            def expert_pieces(e, it):
                for i, (what, u) in enumerate(MOE):
                    n = MOE0 + i
                    sp.wait_ge(used, it * len(MOE) + (n - PLACES + 1))
                    dst = place(n)
                    if what == "w2":
                        src = exp_w2_2[0][bass.ds(e, 1), u * 512:(u + 1) * 512, :].rearrange("a (p c) n -> p (a c n)", p=P)
                    else:
                        src = (exp_w1_2 if what == "w1" else exp_w3_2)[0][bass.ds(e, 1)]
                        src = src.rearrange("a (p k) f -> p (a k) f", k=KD)[:, :, u * 512:(u + 1) * 512]
                        dst = chunked(dst, 512)
                    sp.dma_start(dst, src).then_inc(landed[(n + 1) % PLACES], 16)

            with sp.Fori(0, E2) as e:
                expert_pieces(e, e)
            sp.wait_ge(*bl["dve"]("over"))
            extra2 = sp.value_load(over_i[0:1, 0:1], min_val=0, max_val=S // CAP2 - 1)
            with sp.If(extra2 > 0):
                with sp.Fori(E2, 2 * E2) as e:
                    expert_pieces(e - E2, e)
                sp.wait_ge(more_done2, 1)
            ple_last = (("pg", 0), ("pg", 1), ("ple", 0))
            w_g = ple_gate_w_2[1].rearrange("(p k) n -> p k n", k=KD)
            for a in range(3):
                n = PLE1 + a
                sp.wait_ge(used, n - PLACES + 1)
                src = w_g[:, 4 * a:4 * a + 4, :] if a < 2 else ple_w_2[1].rearrange("(k p) n -> p k n", p=P)
                dst = place(n)[:, 0:src.shape[1] * D].rearrange("p (a b) -> p a b", b=D)
                sp.dma_start(dst, src).then_inc(ld_last, 16)
            for t in range(TT):
                sp.wait_ge(*bl["dve"](f"out {t}"))
                sp.dma_start(out[0, t * P:(t + 1) * P, :], x_sb[:, t, :]).then_inc(out_written, 16)
            sp.wait_ge(out_written, 16 * TT)

        @block.gpsimd
        def _(pool):
            count = [0]

            def link(ins):
                count[0] += 1
                ins.then_inc(pool_step, 1)
                pool.wait_ge(pool_step, count[0])

            link(pool.memset(ident[:, :], 0.0))
            consts.raise_by(pool.affine_select(out=ident[:, :], in_=ident[:, :], compare_op=ALU.not_equal, fill=1.0, base=0,
                                               pattern=[[-1, P]], channel_multiplier=1), "ident")
            link(pool.memset(ones[:, :], 1.0))
            link(pool.memset(zero[:, :], 0.0))
            link(pool.memset(raw[:, :, 0:1], 0.0))
            for n in range(HALF):
                f = float(np.float32(1.0) / np.float32(ROPE_THETA ** (n / HALF)))
                link(pool.memset(inv_freq[:, n:n + 1], f))
            link(pool.memset(cmask, 0.0))
            link(pool.affine_select(out=cmask[:, P:S], in_=cmask[:, P:S], compare_op=ALU.is_ge, fill=NEG, base=0,
                                    pattern=[[-1, P]], channel_multiplier=1))
            link(pool.affine_select(out=before[:, :], in_=ones[:, :], compare_op=ALU.is_gt, fill=0.0, base=0,
                                    pattern=[[1, P]], channel_multiplier=-1))
            link(pool.memset(blk, 0.0))
            link(pool.memset(hsel, 0.0))
            for h in range(2):
                half = slice(N * h, N * h + N)
                link(pool.memset(blk[half, N * h:N * h + N], 1.0))
                link(pool.memset(hsel[half, h:h + 1], 1.0))
            link(pool.memset(rst, 1.0))
            link(pool.memset(rst.rearrange("p (c t) -> p c t", t=N)[:, :, 0:1], 0.0))
            for h in range(2):
                half = slice(N * h, N * h + N)
                link(pool.affine_select(out=m_lt[half, :], in_=ones[half, 0:N], compare_op=ALU.is_gt, fill=0.0, base=0,
                                        pattern=[[1, N]], channel_multiplier=-1))
                link(pool.affine_select(out=m_le[half, :], in_=ones[half, 0:N], compare_op=ALU.is_ge, fill=0.0, base=0,
                                        pattern=[[1, N]], channel_multiplier=-1))
                link(pool.affine_select(out=idh[half, :], in_=ones[half, 0:N], compare_op=ALU.is_equal, fill=0.0, base=0,
                                        pattern=[[1, N]], channel_multiplier=-1))
            for n, m in enumerate(LVL):
                nb = N // (2 * m)
                for h in range(2):
                    half = slice(N * h, N * h + N)
                    v = lvl[half, n, :].rearrange("p (b u i) -> p b u i", u=2, i=m)
                    link(pool.memset(lvl[half, n, :], 0.0))
                    link(pool.memset(v[:, :, 1, :], 1.0))
                    link(pool.affine_select(out=v[:, :, 1, :], in_=v[:, :, 1, :], compare_op=ALU.is_ge, fill=0.0, base=0,
                                            pattern=[[-2 * m, nb], [0, m]], channel_multiplier=1))
                    link(pool.affine_select(out=v[:, :, 1, :], in_=v[:, :, 1, :], compare_op=ALU.is_gt, fill=0.0, base=m,
                                            pattern=[[2 * m, nb], [0, m]], channel_multiplier=-1))
            link(pool.iota(iota[:, :], pattern=[[1, P]], base=0, channel_multiplier=0,
                           allow_small_or_imprecise_dtypes=True))
            link(pool.iota(iota_q[:, :], pattern=[[0, 4], [1, CAP1]], base=0, channel_multiplier=0,
                           allow_small_or_imprecise_dtypes=True))
            consts.raise_by(pool.iota(thr[:, :], pattern=[[1, 8]], base=1, channel_multiplier=0,
                                      allow_small_or_imprecise_dtypes=True), "all")
            for dst, src in ((wg_sb, w_group[0].rearrange("(p k) n -> p k n", k=KD)),
                             (we_sb, w_expert[0].rearrange("(p k) n -> p k n", k=KD)),
                             (bg_sb, row(b_group[0], NG)), (be_sb, row(b_expert[0], E1)),
                             (w_router, router_w_2[0].rearrange("(p k) n -> p k n", k=KD))):
                pool.dma_start(dst, src).then_inc(ld_rtr, 16)
            pool.wait_ge(*dve_f("qk"))
            pool.wait_ge(*act_f("k rope squares"))
            pool.dma_start(conv_rows[0:CW * NPC], conv_w_2.rearrange("l j (c b) -> (j c) l b", b=P)).then_inc(ld_conv, 16)
            pool.wait_ge(*dve_f("x1 1"))
            for l in range(L2):
                if l == 1:
                    pool.wait_ge(*bl["dve"]("ln2 0"))
                for n, v in enumerate((ln1_g_2, ln1_b_2, ln2_g_2, ln2_b_2)):
                    pool.dma_start(lnp[:, n, :], row(v[l], D)).then_inc(ld_lnp, 16)
                pool.wait_ge(*bl["dve"](f"ffn {l}"))
                pool.dma_start(p_sb, p_2[l, 0].rearrange("(t p) n -> p t n", p=P)).then_inc(ld_p, 16)

        @block.scalar
        def _(act):
            count = [0]

            def link(ins):
                count[0] += 1
                ins.then_inc(act_step, 1)
                act.wait_ge(act_step, count[0])

            def rowload(name, src, n):
                act.dma_start(rows[ROWS[name]:ROWS[name] + n, :], src).then_inc(ld_rows, 16)

            rowload("mu", rw_mu[0].rearrange("(a b) -> a b", b=P), NF)
            for name, v in (("w0", rw_w0), ("a0", rw_a0), ("k_k", rw_k_k), ("k_a", rw_k_a)):
                rowload(name, v[0].rearrange("(a b) -> a b", b=P), J)
            rowload("r_k", rw_r_k[0].rearrange("(a h) n -> a (h n)", h=2), J)
            rowload("g_cq", g_cq[0].rearrange("(a b) -> a b", b=P), 2)
            rowload("g_ckv", g_ckv[0].rearrange("(a b) -> a b", b=P), 1)
            rowload("g_mla", g_mla_out[0].rearrange("(a b) -> a b", b=P), J)
            for name, v in (("pool_scale", pool_scale_2), ("conv_b", conv_b_2), ("ln_g", conv_ln_g_2), ("ln_b", conv_ln_b_2)):
                rowload(name, v.rearrange("l (a b) -> (l a) b", b=P), L2 * NPC)
            front = [
                (gcol[:, 0, :], g_mix[0].rearrange("(p k) -> p k", k=KD)), (gcol[:, 1, :], g_ffn[0].rearrange("(p k) -> p k", k=KD)),
                (w2a2[0:N, :], rw_w2[0]), (w2a2[N:P, :], rw_a2[0]), (g2w, rw_g2[0]),
                (lnx[:, 0, :], row(rw_lnx_g[0], RW)), (lnx[:, 1, :], row(rw_lnx_b[0], RW)),
                (gqk[:, 0, :], row(g_qn[0], QK)), (gqk[:, 1, :], row(g_kn[0], QK)),
                (pos_i[:, 0:1], positions[0, 0:P].rearrange("(p a) -> p a", a=1)),
                (pos_i[:, 1:2], positions[0, P:S].rearrange("(p a) -> p a", a=1)),
            ]
            for dst, src in front:
                act.dma_start(dst, src).then_inc(ld_front, 16)

            for t in range(TT):
                act.wait_ge(ld_x, 16 * TT)
                act_f.raise_by(act.activation(xn[:, t, :], x_sb[:, t, :], ACT.Square, accum_out=ss_x[:, t:t + 1]), f"x squares {t}")
            act.wait_ge(*dve_f("x var"))
            act_f.raise_by(act.activation(rs_x, ss_x, ACT.Sqrt), "x std")

            for t in range(TT):
                act.wait_ge(*pe_f(f"c {t}"))
                act_f.raise_by(act.activation(c_sb[:, t, :], ps[:, t, 0:C_W], ACT.Copy), f"c {t}")
            act.wait_ge(*consts("all"))
            for i in range(NF // 2):
                act.wait_ge(*pe_f(f"feat {i}"))
                act_f.raise_by(act.activation(raw[:, 2 * i:2 * i + 2, 1:S + 1],
                                              ps[:, (2 + i) % 8, :].rearrange("p (a t) -> p a t", a=2), ACT.Copy), f"raw {i}")
            act.wait_ge(*act_f("c 1"))
            for t in range(TT):
                act.activation(qkT[:, 0, :], c_sb[:, t, 0:Q_RANK], ACT.Square, accum_out=ss_c[:, t, 0:1]).then_inc(act_step, 1)
                count[0] += 1
                ins = act.activation(qkT[:, 1, 0:KV_RANK], c_sb[:, t, Q_RANK:Q_RANK + KV_RANK], ACT.Square,
                                     accum_out=ss_c[:, t, 1:2])
                if t == 0:
                    link(ins)
            act_f.raise_by(ins, "c squares")
            act.wait_ge(*dve_f("c var"))
            act_f.raise_by(act.activation(rs_c, ss_c, ACT.Sqrt), "c std")

            act.wait_ge(act_step, count[0])
            for t in range(TT):
                act.wait_ge(*pe_f(f"qkv {t}"))
                link(act.activation(sq[:, t, 0:H * QK].rearrange("p (a n) -> p a n", a=2), ps[:, 4 * t:4 * t + 2, 0:384],
                                    ACT.Square))
                act_f.raise_by(act.activation(sq[:, t, H * QK:], ps[:, 4 * t + 2, :], ACT.Square), f"qk squares {t}")
                act_f.raise_by(act.activation(vt[:, t, :], ps[:, 4 * t + 3, :], ACT.Copy), f"v {t}")
            for t in range(TT):
                ins = act.activation(trig[:, 0, t, :], c_sb[:, t, Q_RANK + KV_RANK:Q_RANK + KV_RANK + HALF], ACT.Copy)
                link(ins)
            link(act.activation(rope_t[:, 0, 0:ROPE], c_sb[:, 0, Q_RANK + KV_RANK:], ACT.Square, accum_out=ss_kr[:, 0:1]))
            act_f.raise_by(act.activation(rope_t[:, 0, 0:ROPE], c_sb[:, 1, Q_RANK + KV_RANK:], ACT.Square,
                                          accum_out=ss_kr[:, 1:2]), "k rope squares")
            act.wait_ge(*dve_f("qk var"))
            act_f.raise_by(act.activation(rs_qk, ss_qk, ACT.Sqrt), "qk std")
            act.wait_ge(*dve_f("angles"))
            act_f.raise_by(act.activation(trig, turn, ACT.Sin), "trig")

            for g in range(4):
                act.wait_ge(*pe_f(f"qkT {g}"))
                act_f.raise_by(act.activation(qkT[0:QK, 4 * g:4 * g + 4, 0:P],
                                              ps[0:QK, g, :].rearrange("p (a t) -> p a t", a=4), ACT.Copy), f"qkT {g}")
            for t, pr in ((0, probs0), (1, probs1)):
                act.wait_ge(*dve_f(f"max {t}"))
                for h in range(H):
                    ins = act.activation(pr[:, h, :], pr[:, h, :], ACT.Exp, bias=mx[:, t, h:h + 1], scale=QK ** -0.5,
                                         accum_out=den[:, t, h:h + 1])
                    if h < H - 1:
                        ins.then_inc(act_step, 1)
                        count[0] += 1
                act_f.raise_by(ins, f"probs {t}")
            act.wait_ge(*pe_f("pT 0"))
            act_f.raise_by(act.activation(pT0, ps[:, 6:8, :].rearrange("p b (a t) -> p (b a) t", a=4), ACT.Copy), "pT0")
            act.wait_ge(*pe_f("pT 1"))
            act_f.raise_by(act.activation(pT1[:, 0:8, :], ps[:, 0:2, :].rearrange("p b (a t) -> p (b a) t", a=4), ACT.Copy),
                           "pT1")
            act.wait_ge(*dve_f("mla"))
            link(act.activation(probs1[:, 0:2, :].rearrange("p a t -> p (a t)"), mla[:, 0, :], ACT.Square,
                                accum_out=ss_x[:, 0:1]))
            act_f.raise_by(act.activation(probs1[:, 0:2, :].rearrange("p a t -> p (a t)"), mla[:, 1, :], ACT.Square,
                                          accum_out=ss_x[:, 1:2]), "mla squares")
            act.wait_ge(*dve_f("mla var"))
            act_f.raise_by(act.activation(rs_x, ss_x, ACT.Sqrt), "mla std")

            act.wait_ge(*dve_f("mixed"))
            link(act.activation(sg[:, :], gl_f, ACT.Sigmoid))
            act_f.raise_by(act.activation(wa_f[0:N, :], wa_f[0:N, :], ACT.Tanh), "tanh")
            act.wait_ge(*pe_f("low rank"))
            act.wait_ge(*pe_f("mlaT"))
            for j in range(J):
                link(act.activation(sig_f[:, j, :], ps[:, j // 2, (j % 2) * S:(j % 2) * S + S], ACT.Sigmoid,
                                    bias=cols[:, ROWS["w0"] + j:ROWS["w0"] + j + 1]))
            act_f.raise_by(act.activation(a_f[:, 0, :], ps[:, 2, 0:S], ACT.Sigmoid, bias=cols[:, ROWS["a0"]:ROWS["a0"] + 1]),
                           "sig w")
            for j in range(1, J):
                ins = act.activation(a_f[:, j, :], ps[:, 2 + j // 2, (j % 2) * S:(j % 2) * S + S], ACT.Sigmoid,
                                     bias=cols[:, ROWS["a0"] + j:ROWS["a0"] + j + 1])
                if j < J - 1:
                    link(ins)
            act_f.raise_by(ins, "sig a")
            act.wait_ge(*dve_f("kk var"))
            act_f.raise_by(act.activation(tmp_f, tmp_f, ACT.Sqrt), "kk std")
            act.wait_ge(*dve_f("cum"))
            act_f.raise_by(act.activation(d_inv, cum, ACT.Exp, scale=DECAY), "d inv")
            act_f.raise_by(act.activation(d_inc, cum, ACT.Exp, scale=-DECAY), "d inc")
            act_f.raise_by(act.activation(d_ex, d_ex, ACT.Exp, scale=-DECAY), "d ex")
            for n, dst in enumerate((v_t, b_t, k_t)):
                for t in range(TT):
                    act.wait_ge(*pe_f(f"turned {n} {t}"))
                    act_f.raise_by(act.activation(dst[:, t, :], ps[:, 2 * n + t, :], ACT.Copy), f"turned {n} {t}")
            for n in range(1, len(LVL)):
                for t in range(TT):
                    act.wait_ge(*pe_f(f"lx {n} {t}"))
                    act_f.raise_by(act.activation(yy[:, t].rearrange("p h n -> p (h n)"), ps[:, 4 * t, :], ACT.Copy), f"lx {n} {t}")
            for c in range(NCH):
                half = slice(N * (c % 2), N * (c % 2) + N)
                act.wait_ge(*pe_f(f"u {c}"))
                act_f.raise_by(act.activation(u_t[half, c // 2].rearrange("p h n -> p (h n)"), ps[half, 2, :], ACT.Copy), f"u {c}")
            act.wait_ge(*pe_f("g"))
            act_f.raise_by(act.activation(gl_t, ps[:, 0:2, :], ACT.Copy), "g")
            act.wait_ge(*dve_f("y var"))
            act_f.raise_by(act.activation(var, var, ACT.Sqrt), "y std")
            m1a, m1d, m1p = m1["act"], m1["dve"], m1["pe"]
            ba, bd, bp = bl["act"], bl["dve"], bl["pe"]
            for t in range(TT):
                act.wait_ge(*dve_f("x1 1"))
                m1a.raise_by(act.activation(xn[:, t, :], x_sb[:, t, :], ACT.Square, accum_out=ss_x[:, t:t + 1]), f"squares {t}")
            act.wait_ge(*m1d("var"))
            m1a.raise_by(act.activation(rs_x, ss_x, ACT.Sqrt), "std")
            act.wait_ge(*m1d("diffs"))
            m1a.raise_by(act.activation(diffs, diffs, ACT.Exp), "exp")

            def quad_act(it):
                act.wait_ge(q_turn, it + 1)
                act.activation(sc_T, ps[:, 3, 256:512].rearrange("p (t n) -> p t n", t=TT), ACT.Copy).then_inc(q_scT, 1)
                act.wait_ge(used1, it * HALVES + 8)
                act.activation(hs[:, 0, 0:F1], ps[:, 2, 0:F1], ACT.Silu).then_inc(q_silu, 1)
                act.wait_ge(used1, it * HALVES + 12)
                act.activation(yg.rearrange("p (b n) -> p b n", b=2), ps[:, 4:6, :], ACT.Copy).then_inc(q_yg, 1)

            with act.Fori(0, NQ) as q:
                quad_act(q)
            extra = act.value_load(over_i[0:1, 0:1], min_val=0, max_val=S // CAP1 - 1)
            with act.If(extra > 0):
                with act.Fori(1, extra + 1) as r:
                    with act.Fori(0, NQ) as q:
                        quad_act(r * NQ + q)

            def turned_x(l, when):
                for b in range(4):
                    act.wait_ge(*bp(f"xT {when} {b}"))
                    t, g = b // 2, b % 2
                    ba.raise_by(act.activation(xT[:, 4 * g:4 * g + 4, t * P:(t + 1) * P],
                                               ps[:, b, :].rearrange("p (k t) -> p k t", k=4), ACT.Copy), f"xT {when} {b}")

            def mixer_act(l):
                turned_x(l, f"mix {l}")
                act.wait_ge(*read((MIX0, MIX1)[l]))
                act.wait_ge(*bd(f"pads {l}"))
                ba.raise_by(act.activation(up[:, :, 16:].rearrange("p (b a) t -> p b a t", b=2),
                                           ps[:, 4:6, :].rearrange("p b (a t) -> p b a t", a=2), ACT.Copy), f"pool in {l}")
                act.wait_ge(*read((MIX0, MIX1)[l] + 2))
                ba.raise_by(act.activation(sv.rearrange("p (b a) t -> p b (a t)", b=2), ps[:, 0:2, :], ACT.Sigmoid), f"gate {l}")
                act.wait_ge(*bd(f"centred {l}"))
                ba.raise_by(act.activation(sv, yv, ACT.Square), f"squares {l}")
                act.wait_ge(*bd(f"conv var {l}"))
                ba.raise_by(act.activation(rstd_b, rstd_b, ACT.Sqrt), f"conv std {l}")
                act.wait_ge(*bd(f"conv normed {l}"))
                for j in range(NPC):
                    g, b = ROWS["ln_g"] + l * NPC + j, ROWS["ln_b"] + l * NPC + j
                    ins = act.activation(sv[:, j, :], yv[:, j, :], ACT.Silu, bias=cols[:, b:b + 1], scale=cols[:, g:g + 1])
                    if j < NPC - 1:
                        link(ins)
                ba.raise_by(ins, f"silu {l}")
                act.wait_ge(*read((MIX0, MIX1)[l] + 3))
                ba.raise_by(act.activation(mT[:, 4:8, :].rearrange("p (b a) t -> p b (a t)", b=2), ps[:, 2:4, :], ACT.Copy),
                            f"conv out {l}")
                act.wait_ge(*bd(f"ln1 var {l}"))
                ba.raise_by(act.activation(rstd, rstd, ACT.Sqrt), f"ln1 std {l}")

            def tail_act(l):
                act.wait_ge(*bd(f"ln2 var {l}"))
                ba.raise_by(act.activation(rstd, rstd, ACT.Sqrt), f"ln2 std {l}")
                turned_x(l, f"ple {l}")
                act.wait_ge(*bp(f"pT {l}"))
                ba.raise_by(act.activation(pT, ps[:, 4, :].rearrange("p (k t) -> p k t", k=2), ACT.Copy), f"pT {l}")
                for t in range(TT):
                    act.wait_ge(*(read(PLE0 + 1) if (l, t) == (0, 1) else bp(f"ple gate {l} {t}")))
                    ba.raise_by(act.activation(gate_s[:, t, :].rearrange("p (b n) -> p b n", b=2), ps[:, 2 * t:2 * t + 2, :],
                                               ACT.Sigmoid), f"ple gate {l} {t}")

            mixer_act(0)
            turned_x(0, "ffn 0")
            for u in range(len(UD)):
                for t in range(TT):
                    act.wait_ge(*(bp(f"up {u}") if t == 0 else read_dense("w3", u)))
                    if u > 0:
                        act.wait_ge(*bd(f"hidden {u - 1} {t}"))
                    ba.raise_by(act.activation(hs[:, t, 0:UD[u]], ps[:, t, 0:UD[u]], ACT.Silu), f"silu {u} {t}")
            tail_act(0)
            mixer_act(1)
            turned_x(1, "ffn 1")
            for t in range(TT):
                ba.raise_by(act.activation(xn[:, t, :], x_sb[:, t, :], ACT.Copy), f"x kept {t}")
            act.wait_ge(*bd("diffs"))
            ba.raise_by(act.activation(diffs, diffs, ACT.Exp), "exp")

            def expert_act(e, r):
                it = e + r * E2
                for u in range(UNITS):
                    b = u % 2
                    act.wait_ge(used, it * len(MOE) + read_moe("w1", u))
                    if u >= 2:
                        act.wait_ge(e_hid, it * UNITS + (u - 1))
                    act.activation(hs[:, b, :], ps[:, b, :], ACT.Silu).then_inc(e_silu, 1)
                    if u == 2:
                        act.wait_ge(e_turn, it + 1)
                        act.activation(sc_T, ps[:, 6, 0:2 * P].rearrange("p (t n) -> p t n", t=TT), ACT.Copy).then_inc(e_scT, 1)
                act.wait_ge(used, it * len(MOE) + read_moe("w2", UNITS - 1))
                act.activation(yg.rearrange("p (b n) -> p b n", b=2), ps[:, 4:6, :], ACT.Copy).then_inc(e_yg, 1)

            def pass_act(r):
                with act.Fori(0, E2) as e:
                    expert_act(e, r)

            pass_act(0)
            extra2 = act.value_load(over_i[0:1, 0:1], min_val=0, max_val=S // CAP2 - 1)
            with act.If(extra2 > 0):
                pass_act(1)
            tail_act(1)

        @block.tensor
        def _(pe):
            mm, turn_ = pe.matmul, pe.transpose

            pe.wait_ge(*consts("ident"))
            pe.wait_ge(ld_rows, 16 * 13)
            pe_f.raise_by(turn_(ps[:, 7, 0:NROWS], rows[0:NROWS, :], ident[0:NROWS, 0:NROWS]), "cols")
            for t in range(TT):
                pe.wait_ge(*dve_f(f"xn {t}"))
                for g in range(2):
                    for k in range(4):
                        ins = turn_(ps[:, 2 * t + g, k * P:(k + 1) * P],
                                    xn[:, t, :].rearrange("p (q k) -> p k q", k=KD)[:, 4 * g + k, :], ident[:, :])
                    pe_f.raise_by(ins, f"xT {t} {g}")
            pe.wait_ge(ld_win, 16 * KD)
            pe.wait_ge(*dve_f("xT 1 1"))
            for t in range(TT):
                for k in range(KD):
                    ins = mm(ps[:, t, 0:C_W], xT[:, k, t * P:(t + 1) * P], w_in_sb[:, k, 0:C_W], start=(k == 0), stop=(k == KD - 1))
                pe_f.raise_by(ins, f"c {t}")
            pe.wait_ge(*dve_f("cols"))
            for i in range(NF // 2):
                if i == 6:
                    pe.wait_ge(*act_f("c 0"))
                for u in range(2):
                    f0 = C_W + (2 * i + u) * P
                    for k in range(KD):
                        ins = mm(ps[:, (2 + i) % 8, u * S:(u + 1) * S], w_in_sb[:, k, f0:f0 + P], xT[:, k, :],
                                 start=(k == 0), stop=(k == KD - 1))
                pe_f.raise_by(ins, f"feat {i}")

            pe.wait_ge(*dve_f("c normed"))
            pe.wait_ge(*act_f("raw 6"))
            pe.wait_ge(*act_f("c 1"))
            for t in range(TT):
                for i in range(3):
                    at = (i % 2) * S + t * P
                    ins = turn_(ps[:, i // 2, at:at + P], c_sb[:, t, i * P:(i + 1) * P], ident[:, :])
            pe_f.raise_by(ins, "projected")
            pe.wait_ge(ld_uq, 48)
            pe.wait_ge(*dve_f("cT"))
            for t in range(TT):
                for a in range(2):
                    for k in range(2):
                        mm(ps[:, 4 * t + a, 0:384], cT[:, k, t * P:(t + 1) * P], w_uq_sb[:, k, 384 * a:384 * a + 384],
                           start=(k == 0), stop=(k == 1))
                mm(ps[:, 4 * t + 2, :], cT[:, 2, t * P:(t + 1) * P], w_uk_sb, start=True, stop=True)
                pe_f.raise_by(mm(ps[:, 4 * t + 3, :], cT[:, 2, t * P:(t + 1) * P], w_uv_sb, start=True, stop=True), f"qkv {t}")
            pe.wait_ge(*dve_f("qk"))
            pe.wait_ge(*act_f("v 1"))
            for t in range(TT):
                for g in range(4):
                    for a in range(4):
                        ins = turn_(ps[0:QK, 4 * t + g, a * P:(a + 1) * P], qk[:, t, 4 * g + a, :], ident[:, :])
                    pe_f.raise_by(ins, f"qkT {4 * t + g}")
            pe.wait_ge(*act_f("qkT 3"))
            pe.wait_ge(*dve_f("qkT 7"))
            for h in range(H):
                ins = mm(ps[:, h // 4, (h % 4) * P:(h % 4 + 1) * P], qkT[0:QK, h, 0:P], qkT[0:QK, H + h, 0:P], start=True, stop=True)
            pe_f.raise_by(ins, "scores 0")
            for h in range(H):
                ins = mm(ps[:, 2 + h // 2, (h % 2) * S:(h % 2 + 1) * S], qkT[0:QK, h, P:S], qkT[0:QK, H + h, :], start=True, stop=True)
            pe_f.raise_by(ins, "scores 1")
            pe.wait_ge(*act_f("probs 0"))
            for h in range(H):
                ins = turn_(ps[:, 6 + h // 4, (h % 4) * P:(h % 4 + 1) * P], probs0[:, h, :], ident[:, :])
            pe_f.raise_by(ins, "pT 0")
            pe.wait_ge(*act_f("probs 1"))
            for h in range(H):
                for b in range(2):
                    i = 2 * h + b
                    ins = turn_(ps[:, i // 4, (i % 4) * P:(i % 4 + 1) * P], probs1[:, h, b * P:(b + 1) * P], ident[:, :])
            pe_f.raise_by(ins, "pT 1")
            pe.wait_ge(*act_f("pT0"))
            for h in range(H):
                ins = mm(ps[:, 4, h * VD:(h + 1) * VD], pT0[:, h, :], vt[:, 0, h * VD:(h + 1) * VD], start=True, stop=True)
            pe.wait_ge(*act_f("pT1"))
            pe.wait_ge(*dve_f("pT1"))
            for h in range(H):
                for b in range(2):
                    ins = mm(ps[:, 5, h * VD:(h + 1) * VD], pT1[:, 2 * h + b, :], vt[:, b, h * VD:(h + 1) * VD],
                             start=(b == 0), stop=(b == 1))
            pe_f.raise_by(ins, "pv")
            pe.wait_ge(*dve_f("mla normed"))
            for t in range(TT):
                for j in range(J):
                    ins = turn_(ps[:, 6 + j // 2, (j % 2) * S + t * P:(j % 2) * S + (t + 1) * P], mla[:, t, j * P:(j + 1) * P],
                                ident[:, :])
            pe_f.raise_by(ins, "mlaT")

            pe.wait_ge(ld_front, 16 * 11)
            pe.wait_ge(*act_f("tanh"))
            for j in range(J):
                for n, half in enumerate((slice(0, N), slice(N, P))):
                    ins = mm(ps[:, 2 * n + j // 2, (j % 2) * S:(j % 2 + 1) * S], w2a2[half, j * P:(j + 1) * P], wa_f[half, :],
                             start=True, stop=True)
            pe_f.raise_by(ins, "low rank")
            pe.wait_ge(*dve_f("kk squares"))
            for b in range(2):
                ins = mm(ps[:, 4 + b, :], blk, tmp_f[:, 2 * b:2 * b + 2, :].rearrange("p a t -> p (a t)"), start=True, stop=True)
            pe_f.raise_by(ins, "kk sums")
            pe.wait_ge(*act_f("sig a"))
            pe.wait_ge(*dve_f("tilde"))
            for n, src in enumerate((v_f, bt_f, kt_f)):
                if n == 2:
                    pe.wait_ge(*dve_f("kk var"))
                for t in range(TT):
                    for j in range(J):
                        ins = turn_(ps[:, 2 * n + t, j * P:(j + 1) * P], src[:, j, t * P:(t + 1) * P], ident[:, :])
                    pe_f.raise_by(ins, f"turned {n} {t}")
                if n == 0:
                    for tt in range(TT):
                        for j in range(J):
                            ins = mm(ps[:, 6, tt * H + 2 * j:tt * H + 2 * j + 2], rk_f[:, j, tt * P:(tt + 1) * P], hsel,
                                     start=True, stop=True)
                    pe_f.raise_by(ins, "bonus")
            for t in range(TT):
                for m, rhs in enumerate((kk_f, rt_f)):
                    if t == 0 and m == 0:
                        pe.wait_ge(*act_f("turned 0 1"))
                    if t == 0 and m == 1:
                        pe.wait_ge(*act_f("turned 1 1"))
                    if t == 1 and m == 0:
                        pe.wait_ge(*act_f("turned 2 1"))
                    if t == 1 and m == 1:
                        pe.wait_ge(*dve_f("bonus"))
                    for h in range(H):
                        j, par = h // 2, h % 2
                        rows_h = slice(N * par, N * par + N)
                        for n, lhs in enumerate((bt_f, kt_f)):
                            for c in range(2):
                                tok = slice(t * P + c * N, t * P + c * N + N)
                                ins = mm(ps[c * N:(c + 1) * N, 4 * t + 2 * m + par, (n * J + j) * N:(n * J + j + 1) * N],
                                         lhs[rows_h, j, tok], rhs[rows_h, j, tok], start=True, stop=True)
                    pe_f.raise_by(ins, f"gram {t} {m}")

            def per_head(t, bank, left, right, **kw):
                for c in range(2):
                    half = slice(N * c, N * c + N)
                    for h in range(2 * J):
                        ins = mm(ps[half, bank, h * N:(h + 1) * N], left(half, h), right(half, h), **kw)
                return ins

            def natural(h):
                return slice((2 * (h % J) + h // J) * N, (2 * (h % J) + h // J + 1) * N)

            for n in range(len(LVL)):
                for t in range(TT):
                    pe.wait_ge(*dve_f(f"low {n} {t}"))
                    if n == 0:
                        pe_f.raise_by(per_head(t, 4 * t, lambda p_, h: low[p_, t, h, :], lambda p_, h: idh[p_, :], start=True,
                                               stop=True), f"lx {n} {t}")
                        continue
                    pe.wait_ge(*dve_f(f"inv {n - 1} {t}"))
                    pe_f.raise_by(per_head(t, 4 * t, lambda p_, h: low[p_, t, h, :], lambda p_, h: inv[p_, t, h, :], start=True,
                                           stop=True), f"lx {n} {t}")
                if n == 0:
                    continue
                for t in range(TT):
                    pe.wait_ge(*act_f(f"lx {n} {t}"))
                    pe.wait_ge(*dve_f(f"invT {n - 1} {t}"))
                    pe_f.raise_by(per_head(t, 4 * t + 2, lambda p_, h: yy[p_, t, h, :], lambda p_, h: invT[p_, t, h, :], start=True,
                                           stop=True), f"xlxT {n} {t}")
                    if n < len(LVL) - 1:
                        pe_f.raise_by(per_head(t, 4 * t + 1, lambda p_, h: invT[p_, t, h, :], lambda p_, h: yy[p_, t, h, :],
                                               start=True, stop=True), f"xlx {n} {t}")
            pe.wait_ge(*dve_f("invT 5 1"))
            for t in range(TT):
                pe_f.raise_by(per_head(t, 6 + t, lambda p_, h: gram[p_, t, 0, h // J, (J + h % J) * N:(J + h % J + 1) * N],
                                       lambda p_, h: v_t[p_, t, natural(h)], start=True, stop=True), f"akv {t}")

            for c in range(NCH):
                t, half = c // 2, slice(N * (c % 2), N * (c % 2) + N)
                tok = slice(c * N, c * N + N)
                if c > 0:
                    pe.wait_ge(*dve_f(f"state {c - 1}"))
                    for src, bank in ((kk_f, 0), (rt_f, 4)):
                        if bank == 4 and c >= 2:
                            pe.wait_ge(*dve_f(f"y {c - 1}"))
                        for h in range(2 * J):
                            par, j = h // J, h % J
                            rows_h = slice(N * par, N * par + N)
                            ins = mm(ps[half, bank + par, j * N:(j + 1) * N], src[rows_h, j, tok], st[rows_h, j, :], start=True,
                                     stop=True)
                        pe_f.raise_by(ins, f"kk s {c}" if bank == 0 else f"r s {c}")
                pe.wait_ge(*dve_f(f"rn {c}"))
                for h in range(2 * J):
                    ins = mm(ps[half, 2, h * N:(h + 1) * N], invT[half, t, h, :], rn[half, h, :], start=True, stop=True)
                pe_f.raise_by(ins, f"u {c}")
                pe.wait_ge(*act_f(f"u {c}"))
                if c < NCH - 1:
                    for h in range(2 * J):
                        par, j = h // J, h % J
                        o = ps[N * par:N * par + N, 3, j * N:(j + 1) * N]
                        mm(o, b_t[half, t, natural(h)], u_t[half, t, h, :], start=True, stop=False)
                        ins = mm(o, k_t[half, t, natural(h)], v_t[half, t, natural(h)], start=False, stop=True)
                    pe_f.raise_by(ins, f"state {c}")
                for h in range(2 * J):
                    par, j = h // J, h % J
                    o = ps[half, 6, h * N:(h + 1) * N]
                    mm(o, gram[half, t, 1, par, j * N:(j + 1) * N], u_t[half, t, h, :], start=True, stop=False)
                    ins = mm(o, gram[half, t, 1, par, (J + j) * N:(J + j + 1) * N], v_t[half, t, natural(h)], start=False,
                             stop=True)
                pe_f.raise_by(ins, f"y {c}")
            pe.wait_ge(*dve_f("rn 3"))
            for t in range(TT):
                ins = mm(ps[:, t, :], sg[:, t * P:(t + 1) * P], g2w, start=True, stop=True)
            pe_f.raise_by(ins, "g")
            pe.wait_ge(*dve_f("y gated"))
            for t in range(TT):
                for j in range(J):
                    ins = turn_(ps[:, 6 + j // 2, (j % 2) * S + t * P:(j % 2) * S + (t + 1) * P], y_t[:, t, j * P:(j + 1) * P],
                                ident[:, :])
            pe_f.raise_by(ins, "yT")
            pe.wait_ge(ld_woa, 16)
            pe.wait_ge(ld_wob, 16)
            pe.wait_ge(*dve_f("mixT"))
            for t in range(TT):
                for n in range(2):
                    for k in range(KD):
                        w = (w_o_a if k < 4 else w_o_b)[:, k % 4, n * 512:(n + 1) * 512]
                        ins = mm(ps[:, 2 * t + n, :], mixT[:, k, t * P:(t + 1) * P], w, start=(k == 0), stop=(k == KD - 1))
                pe_f.raise_by(ins, f"w_o {t}")
            m1a, m1d, m1p = m1["act"], m1["dve"], m1["pe"]
            ba, bd, bp = bl["act"], bl["dve"], bl["pe"]

            def by8(v):
                return v.rearrange("p (q k) -> p k q", k=KD)

            def turn_x(src, stage, name, waits):
                for t in range(TT):
                    for g in range(2):
                        for w in waits(t):
                            pe.wait_ge(*w)
                        for k in range(4):
                            ins = turn_(ps[:, 2 * t + g, k * P:(k + 1) * P], by8(src[:, t, :])[:, 4 * g + k, :], ident[:, :])
                        stage.raise_by(ins, f"{name} {2 * t + g}")

            def logits(experts, w, at):
                for t in range(TT):
                    for k in range(KD):
                        ins = mm(ps[:, 4 + t, at:at + experts], xT[:, k, t * P:(t + 1) * P], w[:, k, :], start=(k == 0),
                                 stop=(k == KD - 1))
                return ins

            def places(stage, n):
                mm(ps[:, 6, 0:n], before[:, :], mask[:, 0, 0:n], start=True, stop=True)
                mm(ps[:, 6, n:2 * n], ones[:, :], mask[:, 0, 0:n], start=True, stop=False)
                mm(ps[:, 6, n:2 * n], before[:, :], mask[:, 1, 0:n], start=False, stop=True)
                mm(ps[:, 6, 2 * n:3 * n], ones[:, :], mask[:, 0, 0:n], start=True, stop=False)
                stage.raise_by(mm(ps[:, 6, 2 * n:3 * n], ones[:, :], mask[:, 1, 0:n], start=False, stop=True), "places")

            turn_x(xn, m1p, "xT", lambda t: [m1d(f"xn {t}"), dve_f("x1 1")])
            pe.wait_ge(ld_rtr, 16 * 5)
            pe.wait_ge(*m1d("xT 3"))
            logits(NG, wg_sb, 0)
            m1p.raise_by(logits(E1, we_sb, 8), "logits")
            pe.wait_ge(*m1d("mask"))
            places(m1p, E1)

            def quad_pe(it):
                pe.wait_ge(q_sel, it + 1)
                for k in range(KD):
                    for t in range(TT):
                        ins = mm(ps[:, k // 4, (k % 4) * P:(k % 4 + 1) * P], by8(xn[:, t, :])[:, k, :], ga_sel[:, t, :],
                                 start=(t == 0), stop=(t == TT - 1))
                ins.then_inc(q_gath, 1)
                for t in range(TT):
                    ins = turn_(ps[:, 3, 256 + t * P:256 + (t + 1) * P], sc_sel[:, t, :], ident[:, :])
                ins.then_inc(q_turn, 1)
                pe.wait_ge(q_xg, it + 1)
                for n in range(2):
                    for j in range(4):
                        pe.wait_ge(piece1[half_place(4 * n + j)], (it + 1) * 16)
                    for k in range(KD):
                        for j in range(4):
                            at = half_place(4 * n + j) * HALFP
                            ins = mm(ps[32 * j:32 * j + 32, 2, n * F1:(n + 1) * F1], xg[:, k, 32 * j:32 * j + 32],
                                     ring[:, at + k * F1:at + (k + 1) * F1], start=(k == 0), stop=(k == KD - 1),
                                     tile_position=(0, 32 * j))
                    ins.then_inc(used1, 4)
                pe.wait_ge(q_hid, it + 1)
                for c in range(2):
                    ins = turn_(ps[:, 3, c * P:(c + 1) * P], hh[:, 0, 0:F1].rearrange("p (q c) -> p c q", c=2)[:, c, :], ident[:, :])
                ins.then_inc(q_hT, 1)
                pe.wait_ge(q_hTs, it + 1)
                for j in range(4):
                    pe.wait_ge(piece1[half_place(8 + j)], (it + 1) * 16)
                for n in range(2):
                    for c in range(2):
                        for j in range(4):
                            at = half_place(8 + j) * HALFP + c * D + n * 512
                            ins = mm(ps[32 * j:32 * j + 32, 4 + n, :], hT[:, c, 32 * j:32 * j + 32], ring[:, at:at + 512],
                                     start=(c == 0), stop=(c == 1), tile_position=(0, 32 * j))
                ins.then_inc(used1, 4)
                pe.wait_ge(q_yg, it + 1)
                pe.wait_ge(q_scT, it + 1)
                for t in range(TT):
                    if t == 1:
                        pe.wait_ge(q_add, 2 * it + 2)
                    for n in range(2):
                        ins = mm(ps[:, 6 + n, :], sc_T[:, t, :], yg[:, n * 512:(n + 1) * 512], start=True, stop=True)
                    ins.then_inc(q_scat, 1)

            with pe.Fori(0, NQ) as q:
                quad_pe(q)
            extra = pe.value_load(over_i[0:1, 0:1], min_val=0, max_val=S // CAP1 - 1)
            with pe.If(extra > 0):
                with pe.Fori(1, extra + 1) as r:
                    with pe.Fori(0, NQ) as q:
                        quad_pe(r * NQ + q)
                pe.drain().then_inc(more_done1, 1)

            def has(n):
                pe.wait_ge(landed[(n + 1) % PLACES], 16 * (n // PLACES + 1))

            def mixer_pe(l, n0):
                turn_x(x_sb, bp, f"xT mix {l}", lambda t: [m1d("done") if l == 0 else bd("x 0")])
                for n, (bank, a) in enumerate(((4, 0), (2, 1), (0, 2))):
                    has(n0 + n)
                    w = chunked(place(n0 + n), 512)
                    if n == 0:
                        pe.wait_ge(*ba(f"xT mix {l} 3"))
                    for i in range(4):
                        for k in range(KD):
                            ins = mm(ps[:, bank + i // 2, (i % 2) * S:(i % 2 + 1) * S], w[:, k, i * P:(i + 1) * P], xT[:, k, :],
                                     start=(k == 0), stop=(k == KD - 1))
                        if i == 3:
                            ins.then_inc(used, 1)
                if l == 0:
                    pe.wait_ge(ld_conv, 16)
                pe.wait_ge(*ba(f"pool in {l}"))
                ins = turn_(ps[:, 4, 0:CW * NPC], conv_rows[0:CW * NPC, l, :], ident[0:CW * NPC, 0:CW * NPC])
                bp.raise_by(ins, f"taps {l}")
                has(n0 + 3)
                pe.wait_ge(ld_pool, 16 * (l + 1))
                pe.wait_ge(*bd(f"pooled {l}"))
                for g in range(NPC):
                    w = place(n0 + 3)[:, 4 * 512 + g * P:4 * 512 + (g + 1) * P]
                    ins = mm(ps[:, 6 + g // 2, (g % 2) * S:(g % 2 + 1) * S], w, pooled[:, g, :], start=True, stop=True)
                bp.raise_by(ins, f"pool {l}")
                pe.wait_ge(*bd(f"conv {l}"))
                for j in range(NPC):
                    ins = mm(ps[:, 5, 0:S], ones[:, :], yv[:, j, :], start=(j == 0), stop=(j == NPC - 1))
                bp.raise_by(ins, f"conv sum {l}")
                pe.wait_ge(*ba(f"squares {l}"))
                for j in range(NPC):
                    ins = mm(ps[:, 5, S:2 * S], ones[:, :], sv[:, j, :], start=(j == 0), stop=(j == NPC - 1))
                bp.raise_by(ins, f"conv squares {l}")
                pe.wait_ge(*ba(f"silu {l}"))
                pw = place(n0 + 3)[:, 0:4 * 512].rearrange("p (k n) -> p k n", k=4)
                for j in range(NPC):
                    for k in range(NPC):
                        ins = mm(ps[:, 2 + j // 2, (j % 2) * S:(j % 2 + 1) * S], pw[:, k, j * P:(j + 1) * P], sv[:, k, :],
                                 start=(k == 0), stop=(k == NPC - 1))
                ins.then_inc(used, 1)
                pe.wait_ge(*bd(f"pool out {l}"))
                pe.wait_ge(*ba(f"conv out {l}"))
                has(n0 + 4)
                has(n0 + 5)
                wo = [place(n0 + 4 + a).rearrange("p (k n) -> p k n", k=4) for a in range(2)]
                for t in range(TT):
                    for n in range(2):
                        for k in range(KD):
                            ins = mm(ps[:, 4 * (1 - t) + n, :], mT[:, k, t * P:(t + 1) * P],
                                     wo[k // 4][:, k % 4, n * 512:(n + 1) * 512], start=(k == 0), stop=(k == KD - 1))
                    if t == 0:
                        bp.raise_by(ins, f"mix {l}")
                    else:
                        ins.then_inc(used, 2)

            def ple_pe(l, n0, last):
                turn_x(x_sb, bp, f"xT ple {l}", lambda t: [bd(f"ln2 {l}")])
                pe.wait_ge(ld_p, 16 * (l + 1))
                for k in range(2):
                    for t in range(TT):
                        ins = turn_(ps[:, 4, k * S + t * P:k * S + (t + 1) * P], p_sb[:, t, k * P:(k + 1) * P], ident[:, :])
                bp.raise_by(ins, f"pT {l}")
                pe.wait_ge(*ba(f"xT ple {l} 3"))
                if last:
                    pe.wait_ge(ld_last, 16 * 3)
                else:
                    for a in range(3):
                        has(n0 + a)
                wg = [place(n0 + a).rearrange("p (k n) -> p k n", k=4) for a in range(2)]
                for t in range(TT):
                    for n in range(2):
                        for k in range(KD):
                            ins = mm(ps[:, 2 * t + n, :], xT[:, k, t * P:(t + 1) * P], wg[k // 4][:, k % 4, n * 512:(n + 1) * 512],
                                     start=(k == 0), stop=(k == KD - 1))
                    if last or t == 0:
                        bp.raise_by(ins, f"ple gate {l} {t}")
                    else:
                        ins.then_inc(used, 2)
                wp = place(n0 + 2)[:, 0:2 * D].rearrange("p (k n) -> p k n", k=2)
                pe.wait_ge(*ba(f"pT {l}"))
                for t in range(TT):
                    for n in range(2):
                        for k in range(2):
                            ins = mm(ps[:, 4 + 2 * t + n, :], pT[:, k, t * P:(t + 1) * P], wp[:, k, n * 512:(n + 1) * 512],
                                     start=(k == 0), stop=(k == 1))
                    if last or t == 0:
                        bp.raise_by(ins, f"ple {l} {t}")
                    else:
                        ins.then_inc(used, 1)

            mixer_pe(0, MIX0)
            turn_x(x_sb, bp, "xT ffn 0", lambda t: [bd("ln1 0")])
            pe.wait_ge(*ba("xT ffn 0 3"))

            def dense_down(u, t):
                n_c = UD[u] // P
                n2 = DENSE0 + DENSE.index(("w2", u))
                if t == 0:
                    has(n2)
                pe.wait_ge(*bd(f"hT {u} {t}"))
                w = place(n2)[:, 0:n_c * D].rearrange("p (c n) -> p c n", c=n_c)
                for n in range(2):
                    for c in range(n_c):
                        ins = mm(ps[:, 4 + 2 * t + n, :], hT[:, c, :], w[:, c, n * 512:(n + 1) * 512], start=(u == 0 and c == 0),
                                 stop=(u == len(UD) - 1 and c == n_c - 1))
                if t == 1:
                    ins.then_inc(used, 1)

            def dense_turn(u, t):
                n_c = UD[u] // P
                pe.wait_ge(*bd(f"hidden {u} {t}"))
                v = hh[:, t, 0:UD[u]].rearrange("p (q c) -> p c q", c=n_c)
                for c in range(n_c):
                    ins = turn_(ps[:, 3, c * P:(c + 1) * P], v[:, c, :], ident[:, :])
                bp.raise_by(ins, f"hT {u} {t}")

            before_ = None
            for u in range(len(UD)):
                n1, n3 = DENSE0 + DENSE.index(("w1", u)), DENSE0 + DENSE.index(("w3", u))
                has(n1)
                has(n3)
                for t in range(TT):
                    if u > 0:
                        pe.wait_ge(*ba(f"silu {u - 1} {t}"))
                    for k in range(KD):
                        ins = mm(ps[:, t, 0:UD[u]], xT[:, k, t * P:(t + 1) * P], chunked(place(n1), UD[u])[:, k, :],
                                 start=(k == 0), stop=(k == KD - 1))
                    if t == 1:
                        ins.then_inc(used, 1)
                    if before_:
                        dense_turn(*before_)
                    for k in range(KD):
                        ins = mm(ps[:, 2, 0:UD[u]], xT[:, k, t * P:(t + 1) * P], chunked(place(n3), UD[u])[:, k, :],
                                 start=(k == 0), stop=(k == KD - 1))
                    if t == 0:
                        bp.raise_by(ins, f"up {u}")
                    else:
                        ins.then_inc(used, 1)
                    if before_:
                        dense_down(*before_)
                    before_ = (u, t)
            dense_turn(*before_)
            dense_down(*before_)
            ple_pe(0, PLE0, False)
            mixer_pe(1, MIX1)
            turn_x(x_sb, bp, "xT ffn 1", lambda t: [bd("ln1 1")])
            pe.wait_ge(*ba("xT ffn 1 3"))
            bp.raise_by(logits(E2, w_router, 8), "logits")
            pe.wait_ge(*bd("mask"))
            places(bp, E2)

            def gather(n):
                pe.wait_ge(e_sel, n)
                for k in range(KD):
                    for t in range(TT):
                        ins = mm(ps[:, 6 + k // 4, (k % 4) * P:(k % 4 + 1) * P], by8(xn[:, t, :])[:, k, :], ga_sel[:, t, :],
                                 start=(t == 0), stop=(t == TT - 1))
                ins.then_inc(e_gath, 1)

            def scatter(n, t):
                if t == 0:
                    pe.wait_ge(e_scT, n)
                    pe.wait_ge(e_yg, n)
                else:
                    pe.wait_ge(e_add, 2 * n)
                for h in range(2):
                    ins = mm(ps[:, 6 + h, :], sc_T[:, t, :], yg[:, h * 512:(h + 1) * 512], start=True, stop=True)
                ins.then_inc(e_scat, 1)

            def expert_pe(e, r, halves):
                it, n9 = e + r * E2, e + (r * (E2 + 1) + 1)
                fh, slots_h = 512 // halves, P // halves
                pe.wait_ge(e_xg, n9)

                def has_piece(what, u):
                    n = MOE0 + MOE.index((what, u))
                    pe.wait_ge(landed[(n + 1) % PLACES], it * (16 * len(MOE) // PLACES) + 16 * (n // PLACES + 1))
                    return place(n)

                def side(j):
                    return slice(slots_h * j, slots_h * (j + 1)), dict(tile_position=(0, slots_h * j)) if halves > 1 else {}

                def rows_of(what, u, bank):
                    w = chunked(has_piece(what, u), 512)
                    w = w.rearrange("p k (q c) -> p k q c", c=4)
                    n_c = 4 // halves
                    for k in range(KD):
                        for j in range(halves):
                            cols_j, tile = side(j)
                            ins = mm(ps[cols_j, bank, 0:fh], xg[:, k, cols_j], w[:, k, :, n_c * j:n_c * (j + 1)], start=(k == 0),
                                     stop=(k == KD - 1), **tile)
                    ins.then_inc(used, 1)

                def turn_hidden(u):
                    pe.wait_ge(e_hid, it * UNITS + (u + 1))
                    v = hh[:, u % 2, 0:fh].rearrange("p (q c) -> p c q", q=P)
                    for c in range(4 // halves):
                        ins = turn_(ps[:, 3, c * P:(c + 1) * P], v[:, c, :], ident[:, :])
                    ins.then_inc(e_hT, 1)

                def down(u):
                    w = has_piece("w2", u).rearrange("p (c n) -> p c n", c=4)
                    pe.wait_ge(e_hTs, it * UNITS + (u + 1))
                    first, final = u == 0, u == UNITS - 1
                    if halves == 1:
                        for n in range(2):
                            for c in range(4):
                                ins = mm(ps[:, 4 + n, :], hT[:, c, :], w[:, c, n * 512:(n + 1) * 512], start=(first and c == 0),
                                         stop=(final and c == 3))
                    else:
                        for c in range(4):
                            for n in range(2):
                                rows_n, tile = side(n)
                                ins = mm(ps[rows_n, 4 + n, :], hT[:, c % 2, side(c // 2)[0]], w[:, c, n * 512:(n + 1) * 512],
                                         start=(first and c == 0), stop=(final and c == 3), **tile)
                    ins.then_inc(used, 1)

                for u in range(UNITS):
                    rows_of("w1", u, u % 2)
                    if u > 0:
                        turn_hidden(u - 1)
                    if u == 1:
                        scatter(n9, 1)
                    rows_of("w3", u, 2)
                    if u == 0:
                        scatter(n9, 0)
                        if halves > 1:
                            for n in range(2):
                                rows_n, tile = side(1 - n)
                                mm(ps[rows_n, 4 + n, :], zero[:, 0:slots_h], spread(ones[:, :], 1, 4), start=True, stop=True, **tile)
                    if u > 0:
                        down(u - 1)
                    if u == 2:
                        pe.wait_ge(e_add, 2 * n9 + 1)
                        for t in range(TT):
                            ins = turn_(ps[:, 6, t * P:(t + 1) * P], sc_sel[:, t, :], ident[:, :])
                        ins.then_inc(e_turn, 1)
                gather(n9 + 1)
                turn_hidden(UNITS - 1)
                down(UNITS - 1)

            def pass_end(r):
                n = (r + 1) * (E2 + 1)
                pe.wait_ge(e_xg, n)
                for t in range(TT):
                    scatter(n, t)

            gather(1)
            with pe.Fori(0, E2) as e:
                small_one = pe.value_load(small_i[0:1, bass.ds(e, 1)], min_val=0, max_val=1)
                with pe.If(small_one > 0):
                    expert_pe(e, 0, 2)
                with pe.If(small_one < 1):
                    expert_pe(e, 0, 1)
            pass_end(0)
            extra2 = pe.value_load(over_i[0:1, 0:1], min_val=0, max_val=S // CAP2 - 1)
            with pe.If(extra2 > 0):
                gather(E2 + 2)
                with pe.Fori(0, E2) as e:
                    expert_pe(e, 1, 1)
                pass_end(1)
                pe.drain().then_inc(more_done2, 1)
            ple_pe(1, PLE1, True)

        @block.vector
        def _(dve):
            count = [0]
            tt, ts, stt, red, rec, cp = (dve.tensor_tensor, dve.tensor_scalar, dve.scalar_tensor_tensor, dve.tensor_reduce,
                                         dve.reciprocal, dve.tensor_copy)

            def link(ins):
                count[0] += 1
                ins.then_inc(dve_step, 1)
                dve.wait_ge(dve_step, count[0])

            def mark(stage, ins, name):
                stage.raise_by(ins, name)
                dve.wait_ge(*stage(name))

            dve.wait_ge(*act_f("x squares 1"))
            mark(dve_f, ts(ss_x, ss_x, 1.0 / D, EPS, ALU.mult, ALU.add), "x var")
            dve.wait_ge(*act_f("x std"))
            link(rec(rs_x, rs_x))
            for t in range(TT):
                mark(dve_f, ts(xn[:, t, :], x_sb[:, t, :], rs_x[:, t:t + 1], None, ALU.mult), f"xn {t}")
            dve.wait_ge(ld_front, 16 * 11)
            for t in range(TT):
                for g in range(2):
                    dve.wait_ge(*pe_f(f"xT {t} {g}"))
                    mark(dve_f, tt(xT[:, 4 * g:4 * g + 4, t * P:(t + 1) * P], ps[:, 2 * t + g, :].rearrange("p (k t) -> p k t", k=4),
                                   spread(gcol[:, 0, 4 * g:4 * g + 4], 2, P), ALU.mult), f"xT {t} {g}")
            mark(dve_f, cp(cols[:, :], ps[:, 7, 0:NROWS]), "cols")
            link(cp(posf, pos_i[:, :]))
            dve.wait_ge(*consts("all"))
            link(tt(ang, spread(inv_freq, 1, 2), spread(posf, 2, HALF), ALU.mult))
            magic = 12582912.0
            for n in range(2):
                link(ts(turn[:, n], ang, 1.0 / TWO_PI, 0.25 * n, ALU.mult, ALU.add))
                link(ts(turn[:, n], turn[:, n], magic, None, ALU.add))
                link(ts(trig[:, n], turn[:, n], -magic, None, ALU.add))
                link(stt(turn[:, n], trig[:, n], -6.28125, ang, ALU.mult, ALU.add))
                link(stt(turn[:, n], trig[:, n], -0.0019350051879882812, turn[:, n], ALU.mult, ALU.add))
                link(stt(turn[:, n], trig[:, n], -(TWO_PI - 6.28125 - 0.0019350051879882812), turn[:, n], ALU.mult, ALU.add))
                if n == 1:
                    link(ts(turn[:, n], turn[:, n], TWO_PI / 4, None, ALU.add))
                link(ts(turn[:, n], turn[:, n], 3.1415925, -3.1415925, ALU.min, ALU.max))
            dve.wait_ge(*act_f("c squares"))
            link(ts(ss_c[:, :, 0:1], ss_c[:, :, 0:1], 1.0 / Q_RANK, EPS, ALU.mult, ALU.add))
            mark(dve_f, ts(ss_c[:, :, 1:2], ss_c[:, :, 1:2], 1.0 / KV_RANK, EPS, ALU.mult, ALU.add), "c var")
            dve.wait_ge(*act_f("c std"))
            link(rec(rs_c, rs_c))
            for t in range(TT):
                link(ts(c_sb[:, t, 0:Q_RANK], c_sb[:, t, 0:Q_RANK], rs_c[:, t, 0:1], None, ALU.mult))
                ins = ts(c_sb[:, t, Q_RANK:Q_RANK + KV_RANK], c_sb[:, t, Q_RANK:Q_RANK + KV_RANK], rs_c[:, t, 1:2], None, ALU.mult)
                if t == 0:
                    link(ins)
            mark(dve_f, ins, "c normed")
            dve.wait_ge(*act_f("raw 6"))
            for f in range(NF):
                link(tt(feat[:, f, :], raw[:, f, 0:S], raw[:, f, 1:S + 1], ALU.subtract))
                ins = stt(feat[:, f, :], feat[:, f, :], cols[:, ROWS["mu"] + f:ROWS["mu"] + f + 1], raw[:, f, 1:S + 1],
                          ALU.mult, ALU.add)
                if f < NF - 1:
                    link(ins)
            mark(dve_f, ins, "mixed")
            dve.wait_ge(*pe_f("projected"))
            for i in range(3):
                g = ROWS["g_cq"] + i
                ins = ts(cT[:, i, :], ps[:, i // 2, (i % 2) * S:(i % 2 + 1) * S], cols[:, g:g + 1], None, ALU.mult)
                if i < 2:
                    link(ins)
            mark(dve_f, ins, "cT")
            for t in range(TT):
                dve.wait_ge(*act_f(f"qk squares {t}"))
                link(red(ss_qk[:, t, 0:H], sq[:, t, 0:H * QK].rearrange("p (h d) -> p h d", h=H), AX_X, ALU.add))
                link(red(ss_qk[:, t, H:], sq[:, t, H * QK:].rearrange("p (h d) -> p h d", h=H), AX_X, ALU.add))
            dve.wait_ge(*act_f("k rope squares"))
            for t in range(TT):
                link(ts(ss_qk[:, t, H:], ss_qk[:, t, H:], ss_kr[:, t:t + 1], None, ALU.add))
            mark(dve_f, ts(ss_qk, ss_qk, 1.0 / QK, EPS, ALU.mult, ALU.add), "qk var")
            mark(dve_f, cp(posf, posf), "angles")
            dve.wait_ge(*act_f("qk std"))
            link(rec(rs_qk, rs_qk))
            for t in range(TT):
                dve.wait_ge(*pe_f(f"qkv {t}"))
                heads = rs_qk[:, t, 0:H].rearrange("p (a b) -> p a b", a=2)
                link(tt(qk[:, t, 0:H, :].rearrange("p (a b) d -> p a b d", a=2),
                        ps[:, 4 * t:4 * t + 2, 0:384].rearrange("p a (b d) -> p a b d", b=4), spread(heads, 3, QK), ALU.mult))
                link(tt(qk[:, t, H:, 0:NOPE], ps[:, 4 * t + 2, :].rearrange("p (h d) -> p h d", h=H),
                        spread(rs_qk[:, t, H:], 2, NOPE), ALU.mult))
                link(tt(qk[:, t, H:, NOPE:], spread(c_sb[:, t, Q_RANK + KV_RANK:], 1, H), spread(rs_qk[:, t, H:], 2, ROPE),
                        ALU.mult))
                link(tt(qk[:, t].rearrange("p (a h) d -> p a h d", a=2), qk[:, t].rearrange("p (a h) d -> p a h d", a=2),
                        spread(gqk, 2, H), ALU.mult))
            dve.wait_ge(*act_f("trig"))
            for t in range(TT):
                x1, x2 = qk[:, t, :, NOPE:NOPE + HALF], qk[:, t, :, NOPE + HALF:]
                prod = [rope_t[:, n, :].rearrange("p (h d) -> p h d", h=2 * H) for n in range(4)]
                sin, cos = spread(trig[:, 0, t, :], 1, 2 * H), spread(trig[:, 1, t, :], 1, 2 * H)
                link(tt(prod[0], x1, cos, ALU.mult))
                link(tt(prod[1], x2, sin, ALU.mult))
                link(tt(prod[2], x2, cos, ALU.mult))
                link(tt(prod[3], x1, sin, ALU.mult))
                link(tt(x1, prod[0], prod[1], ALU.subtract))
                ins = tt(x2, prod[2], prod[3], ALU.add)
                if t == 0:
                    link(ins)
            mark(dve_f, ins, "qk")
            for g in range(4, 8):
                dve.wait_ge(*pe_f(f"qkT {g}"))
                mark(dve_f, cp(qkT[0:QK, 4 * (g - 4):4 * (g - 4) + 4, P:S], ps[0:QK, g, :].rearrange("p (a t) -> p a t", a=4)),
                     f"qkT {g}")
            for t, pr, banks in ((0, probs0, ps[:, 0:2, :]), (1, probs1, ps[:, 2:6, :])):
                n = P * (t + 1)
                dve.wait_ge(*pe_f(f"scores {t}"))
                link(tt(pr, banks.rearrange("p b (a k) -> p (b a) k", k=n), spread(cmask[:, S - n:], 1, H), ALU.add))
                link(red(mx[:, t, :], pr, AX_X, ALU.max))
                mark(dve_f, ts(mx[:, t, :], mx[:, t, :], -(QK ** -0.5), None, ALU.mult), f"max {t}")
            dve.wait_ge(*act_f("probs 1"))
            link(rec(den, den))
            dve.wait_ge(*pe_f("pT 1"))
            mark(dve_f, cp(pT1[:, 8:16, :], ps[:, 2:4, :].rearrange("p b (a t) -> p (b a) t", a=4)), "pT1")
            dve.wait_ge(*pe_f("pv"))
            mark(dve_f, tt(mla.rearrange("p t (h d) -> p t h d", h=H), ps[:, 4:6, :].rearrange("p t (h d) -> p t h d", h=H),
                           spread(den, 3, VD), ALU.mult), "mla")
            dve.wait_ge(*act_f("mla squares"))
            mark(dve_f, ts(ss_x, ss_x, 1.0 / RW, EPS, ALU.mult, ALU.add), "mla var")
            dve.wait_ge(*act_f("mla std"))
            link(rec(rs_x, rs_x))
            link(ts(mla[:, 0, :], mla[:, 0, :], rs_x[:, 0:1], None, ALU.mult))
            mark(dve_f, ts(mla[:, 1, :], mla[:, 1, :], rs_x[:, 1:2], None, ALU.mult), "mla normed")
            dve.wait_ge(*pe_f("mlaT"))
            for b in range(2):
                g = ROWS["g_mla"] + 2 * b
                link(tt(mixT[:, 2 * b:2 * b + 2, :], ps[:, 6 + b, :].rearrange("p (a t) -> p a t", a=2),
                        spread(cols[:, g:g + 2], 2, S), ALU.mult))

            def col(name):
                return cols[:, ROWS[name]:ROWS[name] + J]

            link(tt(kk_f, k_f, spread(col("k_k"), 2, S), ALU.mult))
            mark(dve_f, tt(tmp_f, kk_f, kk_f, ALU.mult), "kk squares")
            dve.wait_ge(*pe_f("kk sums"))
            mark(dve_f, ts(tmp_f.rearrange("p (b a) t -> p b (a t)", b=2), ps[:, 4:6, :], 1e-12, None, ALU.add), "kk var")
            dve.wait_ge(*act_f("sig w"))
            for j in range(J):
                link(dve.tensor_tensor_scan(cum[:, j, :], rst, sig_f[:, j, :], 0.0, ALU.mult, ALU.add))
            mark(dve_f, tt(d_ex, cum, sig_f, ALU.subtract), "cum")
            dve.wait_ge(*act_f("kk std"))
            link(rec(tmp_f, tmp_f))
            link(tt(kk_f, kk_f, tmp_f, ALU.mult))
            dve.wait_ge(*act_f("sig a"))
            link(stt(tmp_f, a_f, -1.0, spread(col("k_a"), 2, S), ALU.add, ALU.mult))
            link(stt(k_f, tmp_f, 1.0, k_f, ALU.add, ALU.mult))
            link(tt(tmp_f, kk_f, a_f, ALU.mult))
            link(tt(rk_f, r_f, k_f, ALU.mult))
            link(tt(rk_f, rk_f, spread(col("r_k"), 2, S), ALU.mult))
            dve.wait_ge(*act_f("d inv"))
            link(tt(bt_f, tmp_f, d_inv, ALU.mult))
            link(tt(kt_f, k_f, d_inv, ALU.mult))
            dve.wait_ge(*act_f("d inc"))
            link(tt(rt_f, r_f, d_inc, ALU.mult))
            link(cp(d_end, d_inc.rearrange("p j (c t) -> p j c t", t=N)[:, :, :, N - 1]))
            dve.wait_ge(*act_f("d ex"))
            mark(dve_f, tt(kk_f, kk_f, d_ex, ALU.mult), "tilde")
            dve.wait_ge(*pe_f("bonus"))
            mark(dve_f, cp(bonus, ps[:, 6, 0:2 * H].rearrange("p (t h) -> p t h", t=2)), "bonus")
            for t in range(TT):
                for m, kept in enumerate((m_lt, m_le)):
                    dve.wait_ge(*pe_f(f"gram {t} {m}"))
                    link(tt(gram[:, t, m].rearrange("p a (h n) -> p a h n", n=N),
                            ps[:, 4 * t + 2 * m:4 * t + 2 * m + 2, :].rearrange("p a (h n) -> p a h n", n=N),
                            spread(spread(kept, 1, 2 * J), 1, 2), ALU.mult))

            def a_part(t):
                return gram[:, t, 0, :, 0:J * N].rearrange("p a (j n) -> p a j n", n=N)

            def parity(v):
                return v.rearrange("p (a j) n -> p a j n", a=2)

            def flat(v):
                return v.rearrange("p h n -> p (h n)")

            dve.wait_ge(*act_f("turned 2 1"))
            for n in range(len(LVL)):
                for t in range(TT):
                    if n > 0:
                        dve.wait_ge(*pe_f(f"lx {n - 1} {t}"))
                    mark(dve_f, tt(parity(low[:, t]), a_part(t), spread(spread(lvl[:, n, :], 1, J), 1, 2), ALU.mult), f"low {n} {t}")
                if n == 0:
                    for t in range(TT):
                        dve.wait_ge(*pe_f(f"lx 0 {t}"))
                        mark(dve_f, stt(inv[:, t], ps[:, 4 * t, :].rearrange("p (h n) -> p h n", n=N), -1.0,
                                        spread(idh, 1, 2 * J), ALU.mult, ALU.add), f"inv 0 {t}")
                        mark(dve_f, stt(invT[:, t], low[:, t], -1.0, spread(idh, 1, 2 * J), ALU.mult, ALU.add), f"invT 0 {t}")
                    continue
                for t in range(TT):
                    if n < len(LVL) - 1:
                        dve.wait_ge(*pe_f(f"xlx {n} {t}"))
                        mark(dve_f, tt(flat(inv[:, t]), flat(inv[:, t]), ps[:, 4 * t + 1, :], ALU.subtract), f"inv {n} {t}")
                    dve.wait_ge(*pe_f(f"xlxT {n} {t}"))
                    mark(dve_f, tt(flat(invT[:, t]), flat(invT[:, t]), ps[:, 4 * t + 2, :], ALU.subtract), f"invT {n} {t}")
            for t in range(TT):
                dve.wait_ge(*pe_f(f"akv {t}"))
                link(cp(flat(akv[:, t]), ps[:, 6 + t, :]))
            for c in range(NCH):
                t, half = c // 2, slice(N * (c % 2), N * (c % 2) + N)
                if c == 0:
                    mark(dve_f, ts(rn[half], akv[half, t], -1.0, None, ALU.mult), "rn 0")
                else:
                    dve.wait_ge(*pe_f(f"kk s {c}"))
                    mark(dve_f, stt(rn[half].rearrange("p (a j) n -> p a (j n)", a=2), ps[half, 0:2, 0:J * N], -1.0,
                                    akv[half, t].rearrange("p (a j) n -> p a (j n)", a=2), ALU.mult, ALU.subtract), f"rn {c}")
                if c < NCH - 1:
                    dve.wait_ge(*pe_f(f"state {c}"))
                    new = ps[:, 3, 0:J * N].rearrange("p (j n) -> p j n", n=N)
                    end = spread(d_end[:, :, c], 2, N)
                    if c == 0:
                        mark(dve_f, tt(st[:, :, :], new, end, ALU.mult), "state 0")
                    else:
                        link(tt(st2[:, :, :], new, st[:, :, :], ALU.add))
                        dve.wait_ge(*pe_f(f"r s {c}"))
                        mark(dve_f, tt(st[:, :, :], st2[:, :, :], end, ALU.mult), f"state {c}")
                dve.wait_ge(*pe_f(f"y {c}"))
                y_c = y_t[half, t].rearrange("p (j a n) -> p a j n", j=J, a=2)
                ins = cp(y_c, ps[half, 6, :].rearrange("p (a j n) -> p a j n", a=2, n=N))
                if c > 0:
                    link(ins)
                    dve.wait_ge(*pe_f(f"r s {c}"))
                    ins = tt(y_c, y_c, ps[half, 4:6, 0:J * N].rearrange("p a (j n) -> p a j n", n=N), ALU.add)
                mark(dve_f, ins, f"y {c}")
            y_h = y_t.rearrange("p t (h n) -> p (t h) n", n=N)
            q_h = y_q.rearrange("p t (h n) -> p (t h) n", n=N)
            link(red(mean, y_h, AX_X, ALU.add))
            link(ts(mean, mean, 1.0 / N, None, ALU.mult))
            link(tt(y_h, y_h, spread(mean, 2, N), ALU.subtract))
            link(tt(q_h, y_h, y_h, ALU.mult))
            link(red(var, q_h, AX_X, ALU.add))
            mark(dve_f, ts(var, var, 1.0 / N, LNX_EPS, ALU.mult, ALU.add), "y var")
            link(tt(q_h, v_t.rearrange("p t (h n) -> p (t h) n", n=N), spread(bonus.rearrange("p t h -> p (t h)"), 2, N), ALU.mult))
            dve.wait_ge(*act_f("y std"))
            link(rec(var, var))
            link(tt(y_h, y_h, spread(var, 2, N), ALU.mult))
            link(tt(y_t, y_t, spread(lnx[:, 0, :], 1, TT), ALU.mult))
            link(tt(y_t, y_t, spread(lnx[:, 1, :], 1, TT), ALU.add))
            link(tt(y_t, y_t, y_q, ALU.add))
            dve.wait_ge(*act_f("g"))
            mark(dve_f, tt(y_t, y_t, gl_t, ALU.mult), "y gated")
            dve.wait_ge(*pe_f("yT"))
            mark(dve_f, cp(mixT[:, 4:8, :].rearrange("p (b a) t -> p b (a t)", b=2), ps[:, 6:8, :]), "mixT")
            for t in range(TT):
                dve.wait_ge(*pe_f(f"w_o {t}"))
                x_t = x_sb[:, t, :].rearrange("p (b n) -> p b n", b=2)
                mark(dve_f, tt(x_t, x_t, ps[:, 2 * t:2 * t + 2, :], ALU.add), f"x1 {t}")
            m1a, m1d, m1p = m1["act"], m1["dve"], m1["pe"]
            ba, bd, bp = bl["act"], bl["dve"], bl["pe"]

            def top_two(stage, acts, values, n_pad):
                for t in range(TT):
                    link(dve.max(etop[:, t, :], values[:, t, :]))
                    link(dve.max_index(etop_i[:, t, :].bitcast(U32), etop[:, t, :], values[:, t, :]))
                link(cp(esel, etop_i.bitcast(U32)[:, :, 0:2]))
                mark(stage, tt(diffs[:, :, 4:5], etop[:, :, 1:2], etop[:, :, 0:1], ALU.subtract), "diffs")
                dve.wait_ge(*acts("exp"))
                link(ts(w2[:, :, 0:1], diffs[:, :, 4:5], 1.0, None, ALU.add))
                link(rec(w2[:, :, 0:1], w2[:, :, 0:1]))
                link(tt(w2[:, :, 1:2], diffs[:, :, 4:5], w2[:, :, 0:1], ALU.mult))
                link(tt(e_one, spread(spread(iota[:, 0:8], 1, 2), 1, TT), spread(esel, 3, 8), ALU.is_equal))

            def slots(stage, n, cap):
                link(stt(slot[:, :, 0:n], stage_ps(n), 1.0, mask[:, :, 0:n], ALU.add, ALU.mult))
                link(ts(slot[:, :, 0:n], slot[:, :, 0:n], -1.0, None, ALU.add))
                link(red(over, ps[:, 6, 2 * n:3 * n], AX_X, ALU.max))
                link(ts(over8, thr[:, :], float(cap), over, ALU.mult, ALU.is_lt))
                link(red(over, over8, AX_X, ALU.add))
                mark(stage, cp(over_i[:, :], over), "over")

            def stage_ps(n):
                return ps[:, 6, 0:2 * n].rearrange("p (t e) -> p t e", t=TT)

            dve.wait_ge(*m1a("squares 1"))
            mark(m1d, ts(ss_x, ss_x, 1.0 / D, EPS, ALU.mult, ALU.add), "var")
            dve.wait_ge(*m1a("std"))
            link(rec(rs_x, rs_x))
            for t in range(TT):
                mark(m1d, ts(xn[:, t, :], x_sb[:, t, :], rs_x[:, t:t + 1], None, ALU.mult), f"xn {t}")
            for b in range(4):
                t, g = b // 2, b % 2
                dve.wait_ge(*m1p(f"xT {b}"))
                mark(m1d, tt(xT[:, 4 * g:4 * g + 4, t * P:(t + 1) * P], ps[:, b, :].rearrange("p (k t) -> p k t", k=4),
                             spread(gcol[:, 1, 4 * g:4 * g + 4], 2, P), ALU.mult), f"xT {b}")
            link(dve.memset(glog, 2 * NEG))
            dve.wait_ge(*m1p("logits"))
            dve.wait_ge(ld_rtr, 16 * 5)
            link(tt(glog[:, :, 0:NG], ps[:, 4:6, 0:NG], spread(bg_sb, 1, TT), ALU.add))
            link(tt(elog, ps[:, 4:6, 8:8 + E1], spread(be_sb, 1, TT), ALU.add))
            for t in range(TT):
                link(dve.max(gtop[:, t, :], glog[:, t, :]))
                link(dve.max_index(gtop_i[:, t, :].bitcast(U32), gtop[:, t, :], glog[:, t, :]))
            link(cp(gsel, gtop_i.bitcast(U32)[:, :, 0]))
            link(tt(g_one, spread(iota[:, 0:NG], 1, TT), spread(gsel, 2, NG), ALU.is_equal))
            link(tt(spread_g, elog.rearrange("p t (g e) -> p t g e", g=NG), spread(g_one, 3, EG), ALU.mult))
            link(red(in_group, spread_g.rearrange("p t g e -> p t e g"), AX_X, ALU.add))
            link(tt(diffs[:, :, 0:NG], glog[:, :, 0:NG], gtop[:, :, 0:1].to_broadcast([P, TT, NG]), ALU.subtract))
            top_two(m1d, m1a, in_group, 0)
            link(red(gp, diffs[:, :, 0:NG], AX_X, ALU.add))
            link(rec(gp, gp))
            link(tt(w2, w2, spread(gp, 2, 2), ALU.mult))
            link(tt(mask8, e_one[:, :, 0, :], e_one[:, :, 1, :], ALU.add))
            link(tt(e_one, e_one, spread(w2, 3, 8), ALU.mult))
            link(tt(comb8, e_one[:, :, 0, :], e_one[:, :, 1, :], ALU.add))
            link(tt(comb.rearrange("p t (g e) -> p t g e", g=NG), spread(g_one, 3, EG), spread(comb8, 2, NG), ALU.mult))
            mark(m1d, tt(mask.rearrange("p t (g e) -> p t g e", g=NG), spread(g_one, 3, EG), spread(mask8, 2, NG), ALU.mult), "mask")
            dve.wait_ge(*m1p("places"))
            slots(m1d, E1, CAP1)
            dve.memset(over8, 0.0).then_inc(q_add, 1)

            def quad_dve(q, it, shifted=None):
                k4 = bass.ds(dve.snap(q * 4), 4)
                dve.wait_ge(q_add, it * 2 + 1)
                if shifted is not None:
                    dve.wait_ge(q_shift, shifted)
                sel4 = ga_sel.rearrange("p t (j s) -> p t j s", j=4)
                dve.tensor_tensor(sel4, spread(iota_q[:, :].rearrange("p (j s) -> p j s", j=4), 1, TT),
                                  spread(slot[:, :, k4], 3, CAP1), ALU.is_equal).then_inc(q_sel_w, 1)
                dve.wait_ge(q_sel_w, it + 1)
                dve.tensor_tensor(sc_sel.rearrange("p t (j s) -> p t j s", j=4), sel4, spread(comb[:, :, k4], 3, CAP1),
                                  ALU.mult).then_inc(q_sel, 1)
                dve.wait_ge(q_gath, it + 1)
                dve.tensor_tensor(xg[:, :, :], ps[:, 0:2, :].rearrange("p b (k s) -> p (b k) s", k=4), spread(gcol[:, 1, :], 2, P),
                                  ALU.mult).then_inc(q_xg, 1)
                dve.wait_ge(q_silu, it + 1)
                dve.tensor_tensor(hh[:, 0, 0:F1], hs[:, 0, 0:F1], ps[:, 2, F1:2 * F1], ALU.mult).then_inc(q_hid, 1)
                dve.wait_ge(q_hT, it + 1)
                dve.tensor_copy(hT[:, 0:2, :], ps[:, 3, 0:2 * P].rearrange("p (c s) -> p c s", c=2)).then_inc(q_hTs, 1)
                for t in range(TT):
                    dve.wait_ge(q_scat, it * 2 + (t + 1))
                    x_t = x_sb[:, t, :].rearrange("p (b n) -> p b n", b=2)
                    dve.tensor_tensor(x_t, x_t, ps[:, 6:8, :], ALU.add).then_inc(q_add, 1)

            with dve.Fori(0, NQ) as q:
                quad_dve(q, q)
            extra = dve.value_load(over_i[0:1, 0:1], min_val=0, max_val=S // CAP1 - 1)
            with dve.If(extra > 0):
                with dve.Fori(1, extra + 1) as r:
                    dve.tensor_scalar(slot[:, :, :], slot[:, :, :], -float(CAP1), None, ALU.add).then_inc(q_shift, 1)
                    with dve.Fori(0, NQ) as q:
                        quad_dve(q, r * NQ + q, r)
            dve.wait_ge(q_add, 2 * NQ + 1)
            for g, w in enumerate(WINDOWS):
                link(ts(rc[:, g, :], iota[:, 0:16], 1.0, float(w), ALU.add, ALU.min))
            link(rec(rc, rc))
            mark(m1d, dve.memset(up[:, :, 0:16], 0.0), "done")

            def layer_norm(l, which, gain, bias, last):
                for t in range(TT):
                    for b in range(2):
                        link(dve.bn_stats(stats[:, t, b, :], x_sb[:, t, b * 512:(b + 1) * 512]))
                    link(dve.bn_aggr(mv[:, t, :], stats[:, t].rearrange("p b n -> p (b n)")))
                mark(bd, ts(rstd, mv[:, :, 1], LN_EPS, None, ALU.add), f"{which} var {l}")
                dve.wait_ge(*ba(f"{which} std {l}"))
                link(rec(rstd, rstd))
                dve.wait_ge(ld_lnp, 16 * 4 * (l + 1))
                for t in range(TT):
                    link(ts(x_sb[:, t, :], x_sb[:, t, :], mv[:, t, 0:1], rstd[:, t:t + 1], ALU.subtract, ALU.mult))
                link(tt(x_sb[:, :, :], x_sb[:, :, :], spread(lnp[:, gain, :], 1, TT), ALU.mult))
                mark(bd, tt(x_sb[:, :, :], x_sb[:, :, :], spread(lnp[:, gain + 1, :], 1, TT), ALU.add), f"{which} {l}")

            def mixer_dve(l):
                if l > 0:
                    link(dve.memset(up[:, :, 0:16], 0.0))
                mark(bd, dve.memset(vp[:, :, 0:CW - 1], 0.0), f"pads {l}")
                dve.wait_ge(*read((MIX0, MIX1)[l] + 1))
                dve.wait_ge(*ba(f"gate {l}"))
                link(tt(vp[:, :, CW - 1:].rearrange("p (b a) t -> p b a t", b=2), sv.rearrange("p (b a) t -> p b a t", b=2),
                        ps[:, 2:4, :].rearrange("p b (a t) -> p b a t", a=2), ALU.mult))
                dve.wait_ge(*ba(f"pool in {l}"))
                W = 16 + S
                link(tt(sum_a[:, :, 1:W], up[:, :, 1:W], up[:, :, 0:W - 1], ALU.add))
                link(tt(sum_b[:, 1:, 3:W], sum_a[:, 1:, 3:W], sum_a[:, 1:, 1:W - 2], ALU.add))
                link(tt(sum_a[:, 2:, 7:W], sum_b[:, 2:, 7:W], sum_b[:, 2:, 3:W - 4], ALU.add))
                link(tt(sum_b[:, 3:, 15:W], sum_a[:, 3:, 15:W], sum_a[:, 3:, 7:W - 8], ALU.add))
                for g, (w, src) in enumerate(zip(WINDOWS, (sum_a, sum_b, sum_a, sum_b))):
                    link(stt(pooled[:, g, 16:], src[:, g, 32:], 1.0 / w, up[:, g, 32:], ALU.mult, ALU.subtract))
                    link(tt(pooled[:, g, 0:16], src[:, g, 16:32], rc[:, g, :], ALU.mult))
                mark(bd, tt(pooled[:, :, 0:16], pooled[:, :, 0:16], up[:, :, 16:32], ALU.subtract), f"pooled {l}")
                dve.wait_ge(*bp(f"taps {l}"))
                link(cp(cw.rearrange("p j c -> p (j c)"), ps[:, 4, 0:CW * NPC]))
                for j in range(NPC):
                    b = ROWS["conv_b"] + l * NPC + j
                    link(ts(yv[:, j, :], vp[:, j, 0:S], cw[:, 0, j:j + 1], cols[:, b:b + 1], ALU.mult, ALU.add))
                for tap in range(1, CW):
                    for j in range(NPC):
                        ins = stt(yv[:, j, :], vp[:, j, tap:tap + S], cw[:, tap, j:j + 1], yv[:, j, :], ALU.mult, ALU.add)
                        if j == NPC - 1:
                            if tap < CW - 1:
                                link(ins)
                            else:
                                mark(bd, ins, f"conv {l}")
                        else:
                            ins.then_inc(dve_step, 1)
                            count[0] += 1
                dve.wait_ge(*bp(f"pool {l}"))
                g = ROWS["pool_scale"] + l * NPC
                mark(bd, tt(mT[:, 0:4, :].rearrange("p (b a) t -> p b a t", b=2), ps[:, 6:8, :].rearrange("p b (a t) -> p b a t", a=2),
                            spread(cols[:, g:g + 4].rearrange("p (b a) -> p b a", b=2), 3, S), ALU.mult), f"pool out {l}")
                dve.wait_ge(*bp(f"conv sum {l}"))
                link(ts(mean_b, ps[:, 5, 0:S], 1.0 / D_CONV, None, ALU.mult))
                mark(bd, tt(yv, yv, spread(mean_b, 1, NPC), ALU.subtract), f"centred {l}")
                dve.wait_ge(*bp(f"conv squares {l}"))
                mark(bd, ts(rstd_b, ps[:, 5, S:2 * S], 1.0 / D_CONV, LN_EPS, ALU.mult, ALU.add), f"conv var {l}")
                dve.wait_ge(*ba(f"conv std {l}"))
                link(rec(rstd_b, rstd_b))
                mark(bd, tt(yv, yv, spread(rstd_b, 1, NPC), ALU.mult), f"conv normed {l}")
                for t in range(TT):
                    dve.wait_ge(*(bp(f"mix {l}") if t == 0 else read((MIX0, MIX1)[l] + 5)))
                    b = 4 * (1 - t)
                    x_t = x_sb[:, t, :].rearrange("p (b n) -> p b n", b=2)
                    link(stt(x_t, x_t, ALPHA, ps[:, b:b + 2, :], ALU.mult, ALU.add))
                layer_norm(l, "ln1", 0, 1, False)

            def tail_dve(l):
                layer_norm(l, "ln2", 2, 3, True)
                for t in range(TT):
                    dve.wait_ge(*ba(f"ple gate {l} {t}"))
                    dve.wait_ge(*(read(PLE0 + 2) if (l, t) == (0, 1) else bp(f"ple {l} {t}")))
                    g_t = gate_s[:, t, :].rearrange("p (b n) -> p b n", b=2)
                    link(tt(g_t, g_t, ps[:, 4 + 2 * t:6 + 2 * t, :], ALU.mult))
                    ins = tt(x_sb[:, t, :], x_sb[:, t, :], gate_s[:, t, :], ALU.add)
                    if l == L2 - 1:
                        mark(bd, ins, f"out {t}")
                    elif t == 0:
                        link(ins)
                    else:
                        mark(bd, ins, f"x {l}")

            mixer_dve(0)
            for u in range(len(UD)):
                for t in range(TT):
                    dve.wait_ge(*ba(f"silu {u} {t}"))
                    mark(bd, tt(hh[:, t, 0:UD[u]], hs[:, t, 0:UD[u]], ps[:, 2, 0:UD[u]], ALU.mult), f"hidden {u} {t}")
                    dve.wait_ge(*bp(f"hT {u} {t}"))
                    n_c = UD[u] // P
                    mark(bd, cp(hT[:, 0:n_c, :].rearrange("p c s -> p (c s)"), ps[:, 3, 0:UD[u]]), f"hT {u} {t}")
            dve.wait_ge(*read_dense("w2", len(UD) - 1))
            for t in range(TT):
                x_t = x_sb[:, t, :].rearrange("p (b n) -> p b n", b=2)
                ins = stt(x_t, x_t, ALPHA, ps[:, 4 + 2 * t:6 + 2 * t, :], ALU.mult, ALU.add)
                if t == 0:
                    link(ins)
            mark(bd, ins, "ffn 0")
            tail_dve(0)
            mixer_dve(1)
            dve.wait_ge(*bp("logits"))
            link(cp(in_group, ps[:, 4:6, 8:8 + E2]))
            link(dve.memset(diffs[:, :, 0:4], 0.0))
            top_two(bd, ba, in_group, 0)
            mark(bd, tt(mask[:, :, 0:E2], e_one[:, :, 0, :], e_one[:, :, 1, :], ALU.add), "mask")
            link(tt(e_one, e_one, spread(w2, 3, 8), ALU.mult))
            link(tt(comb[:, :, 0:E2], e_one[:, :, 0, :], e_one[:, :, 1, :], ALU.add))
            dve.wait_ge(*bp("places"))
            slots(bd, E2, CAP2)
            link(ts(small_e, ps[:, 6, 2 * E2:3 * E2], float(SMALL), None, ALU.is_le))
            link(cp(small_i[:, :], small_e))
            link(dve.memset(slot[:, :, E2:E2 + 1], -1.0))
            link(dve.memset(comb[:, :, E2:E2 + 1], 0.0))
            link(dve.memset(slot_hi, -1.0))
            link(stt(slot_hi[:, :, 0:E2], spread(small_e, 1, TT), float(SMALL), slot[:, :, 0:E2], ALU.mult, ALU.add))
            dve.wait_ge(*ba("x kept 1"))
            ts(x_sb[:, :, :], x_sb[:, :, :], ALPHA, None, ALU.mult).then_inc(e_add, 1)

            def select(k, n):
                for half, of in ((slice(0, SMALL), slot), (slice(SMALL, P), slot_hi)):
                    dve.tensor_tensor(ga_sel[:, :, half], spread(iota[:, half], 1, TT),
                                      of[:, :, k].to_broadcast([P, TT, SMALL]), ALU.is_equal).then_inc(e_sel_w, 1)
                dve.wait_ge(e_sel_w, 2 * n)
                dve.tensor_tensor(sc_sel, ga_sel, comb[:, :, k].to_broadcast([P, TT, P]), ALU.mult).then_inc(e_sel, 1)

            def take_x(n):
                dve.wait_ge(e_gath, n)
                dve.tensor_copy(xg[:, :, :].rearrange("p (b k) s -> p b (k s)", b=2), ps[:, 6:8, :]).then_inc(e_xg, 1)

            def add_y(n, t):
                dve.wait_ge(e_scat, 2 * n + (t - 1))
                x_t = x_sb[:, t, :].rearrange("p (b n) -> p b n", b=2)
                dve.tensor_tensor(x_t, x_t, ps[:, 6:8, :], ALU.add).then_inc(e_add, 1)

            def expert_dve(e, r):
                it, n9 = e + r * E2, e + (r * (E2 + 1) + 1)
                k_next = bass.ds(dve.snap(e + 1), 1)
                for u in range(UNITS):
                    b = u % 2
                    dve.wait_ge(used, it * len(MOE) + read_moe("w3", u))
                    dve.wait_ge(e_silu, it * UNITS + (u + 1))
                    dve.tensor_tensor(hh[:, b, :], hs[:, b, :], ps[:, 2, :], ALU.mult).then_inc(e_hid, 1)
                    if u == 0:
                        add_y(n9, 0)
                    if u == UNITS - 1:
                        take_x(n9 + 1)
                    dve.wait_ge(e_hT, it * UNITS + (u + 1))
                    dve.tensor_copy(hT[:, :, :].rearrange("p c s -> p (c s)"), ps[:, 3, :]).then_inc(e_hTs, 1)
                    if u == 0:
                        add_y(n9, 1)
                    if u == 3:
                        dve.wait_ge(e_turn, it + 1)
                        select(k_next, n9 + 1)

            def pass_dve(r):
                dve.memset(sc_T, 0.0).then_inc(e_scT, 1)
                dve.memset(yg, 0.0).then_inc(e_yg, 1)
                select(slice(0, 1), r * (E2 + 1) + 1)
                take_x(r * (E2 + 1) + 1)
                with dve.Fori(0, E2) as e:
                    expert_dve(e, r)
                for t in range(TT):
                    add_y((r + 1) * (E2 + 1), t)

            pass_dve(0)
            extra2 = dve.value_load(over_i[0:1, 0:1], min_val=0, max_val=S // CAP2 - 1)
            with dve.If(extra2 > 0):
                for shifted in (slot_hi, slot):
                    dve.tensor_scalar(shifted[:, :, 0:E2], slot[:, :, 0:E2], -float(CAP2), None, ALU.add).then_inc(e_shift, 1)
                dve.wait_ge(e_shift, 2)
                dve.wait_ge(e_add, 2 * (E2 + 1) + 1)
                pass_dve(1)
            dve.wait_ge(e_add, 2 * (E2 + 1) + 1)
            mark(bd, dve.memset(stats, 0.0), "ffn 1")
            tail_dve(1)


INPUTS = ["x", "positions", "g_mix", "w_in", "g_cq", "w_uq", "g_ckv", "w_uk", "w_uv", "g_qn", "g_kn", "g_mla_out", "rw_mu",
          "rw_w0", "rw_w2", "rw_a0", "rw_a2", "rw_g2", "rw_k_k", "rw_k_a", "rw_r_k", "rw_lnx_g", "rw_lnx_b", "w_o", "g_ffn",
          "w_group", "b_group", "w_expert", "b_expert", "w_gate", "w_up", "w_down", "p_2", "w_in_2", "pool_w_2",
          "pool_scale_2", "conv_w_2", "conv_b_2", "conv_ln_g_2", "conv_ln_b_2", "conv_pw_2", "w_out_2", "ln1_g_2", "ln1_b_2",
          "dense_w1_2", "dense_w3_2", "dense_w2_2", "router_w_2", "exp_w1_2", "exp_w3_2", "exp_w2_2", "ln2_g_2", "ln2_b_2",
          "ple_gate_w_2", "ple_w_2"]


def kernel(**inputs):
    import concourse.bacc as bacc
    from concourse.bass_utils import run_bass_kernel_spmd

    nc = bacc.Bacc("TRN2", target_bir_lowering=False, num_devices=1)
    arrays, args = {}, {}
    for name in INPUTS:
        a = np.ascontiguousarray(inputs[name])
        arrays[f"in_{name}"] = a
        args[name] = nc.dram_tensor(f"in_{name}", a.shape, mybir.dt.from_np(a.dtype), kind="ExternalInput").ap()
    out = nc.dram_tensor("out_0", (1, S, D), F32, kind="ExternalOutput").ap()
    build(nc, out=out, **args)
    r = run_bass_kernel_spmd(nc, [arrays], core_ids=[0])
    return r.results[0]["out_0"]
```

```python
from contextlib import ExitStack

import numpy as np

import concourse.bass as bass
from concourse import mybir

F32 = mybir.dt.float32
I32 = mybir.dt.int32
U32 = mybir.dt.uint32
ALU = mybir.AluOpType
ACT = mybir.ActivationFunctionType
AX_X = mybir.AxisListType.X
RMAX = bass.bass_isa.ReduceOp.max

P = 128
D = 1024
S = 256
TT = S // P
KD = D // P
EPS = 1e-6

H, NOPE, ROPE, VD = 8, 64, 32, 64
QK = NOPE + ROPE
HALF = ROPE // 2
Q_RANK, KV_RANK = 256, 128
C_W = Q_RANK + KV_RANK + ROPE
ROPE_THETA = 10000.0
TWO_PI = 6.283185307179586
NEG = -1.0e30

RW = 512
N = 64
J = RW // P
NCH = S // N
NF = 14
LVL = (1, 2, 4, 8, 16, 32)
DECAY = 0.6065306597126334
LNX_EPS = 64e-5
IN_W = C_W + NF * P

NG, EG, E1, F1 = 4, 8, 32, 256
CAP1 = 32
L2 = 2
D_POOL, D_CONV, CW = 512, 512, 31
IN2 = D_POOL + 2 * D_CONV
NPC = D_POOL // P
WINDOWS = (2, 4, 8, 16)
D_PLE = 256
FD = 2816
E2, F2 = 8, 3584
CAP2 = 128
SMALL = CAP2 // 2
ALPHA = float((2.0 * L2) ** 0.25)
LN_EPS = 1e-5

ROWS = {}
_at = 0
for _name, _n in (("mu", NF), ("w0", J), ("a0", J), ("k_k", J), ("k_a", J), ("r_k", J), ("g_cq", 2), ("g_ckv", 1),
                  ("g_mla", J), ("pool_scale", L2 * NPC), ("conv_b", L2 * NPC), ("ln_g", L2 * NPC), ("ln_b", L2 * NPC)):
    ROWS[_name] = _at
    _at += _n
NROWS = _at

PLACE = 4096
PLACES = 7
HALFP = PLACE // 2
HALVES = 12


class Steps:

    def __init__(self, sem, names):
        self.sem = sem
        self.value = {name: n + 1 for n, name in enumerate(names)}
        self.raised = 0

    def raise_by(self, instruction, name):
        self.raised += 1
        assert self.value[name] == self.raised, (name, self.raised)
        instruction.then_inc(self.sem, 1)

    def __call__(self, name):
        return self.sem, self.value[name]


STEPS = {
    "consts": [
        "ident", "all",
    ],
    "pe_front": [
        "cols", "xT 0 0", "xT 0 1", "xT 1 0", "xT 1 1", "c 0", "c 1", "feat 0", "feat 1", "c turned", "feat 2", "qkv 0",
        "feat 3", "feat 4", "qkv 1", "feat 5", "feat 6", "qkT 0", "qkT 1", "qkT 2", "qkT 3", "qkT 4", "qkT 5", "qkT 6",
        "qkT 7", "scores 0", "scores 1", "pT 0", "pT 1", "pv", "mlaT", "low rank", "kk sums", "w_o mla 0", "w_o mla 1",
        "turned 0 0", "turned 0 1", "bonus", "turned 1 0", "turned 1 1", "turned 2 0", "turned 2 1", "gram 0 0",
        "gram 0 1", "gram 1 0", "gram 1 1", "lx 0 0", "lx 0 1", "lx 1 0", "lx 1 1", "xlx 1 0", "xlxT 1 0", "xlx 1 1",
        "xlxT 1 1", "lx 2 0", "lx 2 1", "xlx 2 0", "xlxT 2 0", "xlx 2 1", "xlxT 2 1", "lx 3 0", "lx 3 1", "xlx 3 0",
        "xlxT 3 0", "xlx 3 1", "xlxT 3 1", "lx 4 0", "lx 4 1", "xlx 4 0", "xlxT 4 0", "xlx 4 1", "xlxT 4 1", "lx 5 0",
        "lx 5 1", "xlxT 5 0", "xlxT 5 1", "akv 0", "akv 1", "u 0", "state 0", "y 0", "kk s 1", "r s 1", "u 1",
        "state 1", "y 1", "kk s 2", "r s 2", "u 2", "state 2", "y 2", "kk s 3", "r s 3", "u 3", "y 3", "g", "yT",
        "w_o 0", "w_o 1",
    ],
    "act_front": [
        "x squares 0", "x squares 1", "x std", "c 0", "c 1", "c squares", "c std", "trig", "raw 0", "raw 1", "raw 2",
        "qk squares 0", "v 0", "qk std 0", "raw 3", "raw 4", "qk squares 1", "v 1", "qk std 1", "raw 5", "raw 6",
        "qkT 0", "qkT 1", "qkT 2", "qkT 3", "qkT 4", "qkT 5", "qkT 6", "qkT 7", "probs 0", "probs 1", "pT0", "pT1",
        "mla squares", "mla std", "tanh", "sig w", "sig a", "kk std", "d inv", "d inc", "d ex", "turned 0 0",
        "turned 0 1", "turned 1 0", "turned 1 1", "turned 2 0", "turned 2 1", "lx 1 0", "lx 1 1", "lx 2 0", "lx 2 1",
        "lx 3 0", "lx 3 1", "lx 4 0", "lx 4 1", "lx 5 0", "lx 5 1", "u 0", "u 1", "u 2", "u 3", "g", "y std",
    ],
    "dve_front": [
        "x var", "xn 0", "xn 1", "xT 0 0", "xT 0 1", "xT 1 0", "xT 1 1", "cols", "c var", "c normed", "cT", "qk var 0",
        "qk read 0", "qk var 1", "qk read 1", "qk", "mixed", "max 0", "max 1", "pT1", "mla", "mla var", "mla normed",
        "mla mixed", "kk squares", "kk var", "cum", "tilde", "x mla 0", "x mla 1", "bonus", "low 0 0", "low 0 1",
        "inv 0 0", "invT 0 0", "low 1 0", "inv 0 1", "invT 0 1", "low 1 1", "low 2 0", "low 2 1", "inv 1 0", "invT 1 0",
        "inv 1 1", "invT 1 1", "low 3 0", "low 3 1", "inv 2 0", "invT 2 0", "inv 2 1", "invT 2 1", "low 4 0", "low 4 1",
        "inv 3 0", "invT 3 0", "inv 3 1", "invT 3 1", "low 5 0", "low 5 1", "inv 4 0", "invT 4 0", "inv 4 1",
        "invT 4 1", "invT 5 0", "invT 5 1", "rn 0", "state 0", "y 0", "rn 1", "state 1", "y 1", "rn 2", "state 2",
        "y 2", "rn 3", "y 3", "y var", "y gated", "mixT", "x1 0", "x1 1",
    ],
    "moe1_pe": [
        "xT 0", "xT 1", "xT 2", "xT 3", "logits", "places",
    ],
    "moe1_act": [
        "squares 0", "squares 1", "std", "exp",
    ],
    "moe1_dve": [
        "var", "xn 0", "xn 1", "xT 0", "xT 1", "xT 2", "xT 3", "diffs", "mask", "over", "done",
    ],
    "block2_pe": [
        "xT mix 0 0", "xT mix 0 1", "xT mix 0 2", "xT mix 0 3", "taps 0", "conv in 0 0", "conv in 0 1", "conv in 0 2",
        "conv 3 0", "pool 0", "conv sum 0", "conv squares 0", "mix 0", "xT ffn 0 0", "xT ffn 0 1", "xT ffn 0 2",
        "xT ffn 0 3", "up 0", "hT 0 0", "hT 0 1", "up 1", "hT 1 0", "hT 1 1", "up 2", "hT 2 0", "hT 2 1", "up 3",
        "hT 3 0", "hT 3 1", "up 4", "hT 4 0", "hT 4 1", "up 5", "hT 5 0", "hT 5 1", "pT 0", "xT ple 0 0", "xT ple 0 1",
        "ple gate 0 0", "xT ple 0 2", "xT ple 0 3", "xT mix 1 0", "xT mix 1 1", "xT mix 1 2", "xT mix 1 3", "taps 1",
        "conv in 1 0", "conv in 1 1", "conv in 1 2", "conv 3 1", "pool 1", "conv sum 1", "conv squares 1", "mix 1",
        "xT ffn 1 0", "xT ffn 1 1", "xT ffn 1 2", "xT ffn 1 3", "logits", "places", "pT 1", "ple 1", "xT ple 1 0",
        "xT ple 1 1", "ple gate 1 0", "xT ple 1 2", "xT ple 1 3", "ple gate 1 1",
    ],
    "block2_act": [
        "xT mix 0 0", "xT mix 0 1", "xT mix 0 2", "xT mix 0 3", "gate 0 0", "gate 0 1", "gate 0 2", "diagonals 0",
        "gate 0 3", "pool in 0", "conv 3 0", "squares 0", "conv std 0", "silu 0", "conv out 0", "ln1 std 0 0",
        "ln1 std 0 1", "xT ffn 0 0", "xT ffn 0 1", "xT ffn 0 2", "xT ffn 0 3", "silu 0 0", "silu 0 1", "silu 1 0",
        "silu 1 1", "silu 2 0", "silu 2 1", "silu 3 0", "silu 3 1", "silu 4 0", "silu 4 1", "silu 5 0", "silu 5 1",
        "ln2 std 0 0", "pT 0", "ln2 std 0 1", "xT ple 0 0", "xT ple 0 1", "xT ple 0 2", "xT ple 0 3", "ple gate 0 0",
        "ple gate 0 1", "xT mix 1 0", "xT mix 1 1", "xT mix 1 2", "xT mix 1 3", "gate 1 0", "gate 1 1", "gate 1 2",
        "diagonals 1", "gate 1 3", "pool in 1", "conv 3 1", "squares 1", "conv std 1", "silu 1", "conv out 1",
        "ln1 std 1 0", "ln1 std 1 1", "xT ffn 1 0", "xT ffn 1 1", "xT ffn 1 2", "xT ffn 1 3", "x kept 0", "x kept 1",
        "exp", "ln2 std 1 0", "pT 1", "ln2 std 1 1", "xT ple 1 0", "xT ple 1 1", "xT ple 1 2", "xT ple 1 3",
        "ple gate 1 0", "ple gate 1 1",
    ],
    "block2_dve": [
        "pads 0", "taps 0", "conv in 0 0", "conv in 0 1", "conv in 0 2", "conv in 0 3", "conv 0", "pool out 0",
        "centred 0", "conv var 0", "conv normed 0", "ln1 var 0 0", "ln1 0 0", "ln1 var 0 1", "ln1 0 1", "hidden 0 0",
        "hT 0 0", "hidden 0 1", "hT 0 1", "hidden 1 0", "hT 1 0", "hidden 1 1", "hT 1 1", "hidden 2 0", "hT 2 0",
        "hidden 2 1", "hT 2 1", "hidden 3 0", "hT 3 0", "hidden 3 1", "hT 3 1", "hidden 4 0", "hT 4 0", "hidden 4 1",
        "hT 4 1", "hidden 5 0", "hT 5 0", "hidden 5 1", "hT 5 1", "ffn 0", "ln2 var 0 0", "ln2 0 0", "ln2 var 0 1",
        "ln2 0 1", "x 0 0", "x 0 1", "pads 1", "taps 1", "conv in 1 0", "conv in 1 1", "conv in 1 2", "conv in 1 3",
        "conv 1", "pool out 1", "centred 1", "conv var 1", "conv normed 1", "ln1 var 1 0", "ln1 1 0", "ln1 var 1 1",
        "ln1 1 1", "diffs", "mask", "over", "ffn 1", "ln2 var 1 0", "ln2 1 0", "ln2 var 1 1", "ln2 1 1", "x 1 0",
        "x 1 1",
    ],
}

def build(nc, x, positions, g_mix, w_in, g_cq, w_uq, g_ckv, w_uk, w_uv, g_qn, g_kn, g_mla_out, rw_mu, rw_w0, rw_w2,
          rw_a0, rw_a2, rw_g2, rw_k_k, rw_k_a, rw_r_k, rw_lnx_g, rw_lnx_b, w_o, g_ffn, w_group, b_group, w_expert,
          b_expert, w_gate, w_up, w_down, p_2, w_in_2, pool_w_2, pool_scale_2, conv_w_2, conv_b_2, conv_ln_g_2,
          conv_ln_b_2, conv_pw_2, w_out_2, ln1_g_2, ln1_b_2, dense_w1_2, dense_w3_2, dense_w2_2, router_w_2,
          exp_w1_2, exp_w3_2, exp_w2_2, ln2_g_2, ln2_b_2, ple_gate_w_2, ple_w_2, out):
    with ExitStack() as ctx:
        def sb(name, shape, dtype=F32):
            return ctx.enter_context(nc.sbuf_tensor(name, shape, dtype))

        def sem(name):
            return ctx.enter_context(nc.semaphore(name))

        def steps(name):
            return Steps(sem(name), STEPS[name])

        ring = sb("ring", [P, PLACES * PLACE])
        x_sb = sb("x_sb", [P, TT, D])
        xn = sb("xn", [P, TT, D])
        xT = sb("xT", [P, KD, S])
        work = sb("work", [P, 14368])
        c_sb = sb("c_sb", [P, TT, C_W])
        ident = sb("ident", [P, P])
        ones = sb("ones", [P, P])
        before = sb("before", [P, P])
        iota = sb("iota", [P, P])
        iota_q = sb("iota_q", [P, P])
        zero = sb("zero", [P, P // 2])
        thr = sb("thr", [P, 8])
        rows = sb("rows", [P, P])
        cols = sb("cols", [P, NROWS])
        sg = sb("sg", [P, S])
        st = sb("st", [P, J, N])
        st2 = sb("st2", [P, J, N])
        small = sb("small", [P, 512])
        pos_i = sb("pos_i", [P, TT], I32)
        gcol = sb("gcol", [P, 2, KD])
        ps = ctx.enter_context(nc.psum_tensor("ps", [P, 8, 512], F32))

        def cut(base, at, *shape):
            n = int(np.prod(shape))
            v = base[:, at:at + n]
            names = "abcde"[:len(shape)]
            if len(shape) == 1:
                return v
            return v.rearrange(f"p ({' '.join(names)}) -> p {' '.join(names)}", **dict(zip(names[1:], shape[1:])))

        def spread(v, axis, n):
            v = v.unsqueeze(axis)
            return v.to_broadcast([*v.shape[:axis], n, *v.shape[axis + 1:]])

        FC = 10 * HALFP
        w2a2 = cut(ring, FC, RW)
        g2w = cut(ring, FC + 512, RW)
        lnx = cut(ring, FC + 1024, 2, RW)
        cmask = cut(ring, FC + 2048, S)
        gqk = cut(ring, FC + 2304, 2, QK)
        lvl = cut(ring, FC + 2496, len(LVL), N)
        rst = cut(ring, FC + 2880, S)
        blk = cut(ring, FC + 3136, P)
        m_lt = cut(ring, FC + 3264, N)
        m_le = cut(ring, FC + 3328, N)
        idh = cut(ring, FC + 3392, N)
        hsel = cut(ring, FC + 3456, 2)
        w_in_sb = cut(ring, 0, KD, IN_W)
        w_uq_sb = cut(ring, 17664, 2, H * QK)
        w_uk_sb = cut(ring, 19200, H * NOPE)
        w_uv_sb = cut(ring, 19712, H * VD)
        w_o_a = cut(ring, 0, 4, D)
        w_o_b = cut(ring, 6 * PLACE, 4, D)

        raw = cut(work, 0, NF, S + 1)
        feat = cut(work, 3600, NF, S)
        cT = cut(work, 9744, 3, S)
        sq = cut(work, 7184, TT, H * QK + H * NOPE)
        qkT = cut(work, 7184, 2 * H, S)
        qk = cut(work, 11280, TT, 2 * H, QK)
        probs0 = cut(work, 11280, H, P)
        probs1 = cut(work, 12304, H, S)
        pT0 = cut(work, 0, H, P)
        pT1 = cut(work, 1024, 2 * H, P)
        mla = cut(work, 7184, TT, RW)
        vt = cut(xn[:, 0, :], 0, TT, H * VD)
        rope_t = cut(xn[:, 1, :], 0, 4, 512 // 2)
        r_f, k_f, v_f = (cut(work, 3600 + 1024 * n, J, S) for n in range(3))
        wa_f = cut(work, 3600 + 12 * S, S)
        gl_f = cut(work, 3600 + 13 * S, S)
        a_f = cut(work, 7184, J, S)
        sig_f = cut(work, 8208, J, S)
        cum = cut(work, 9232, J, S)
        d_inc = cut(work, 10256, J, S)
        d_inv = cut(work, 11280, J, S)
        d_ex = cut(work, 12304, J, S)
        tmp_f = cut(work, 13328, J, S)
        kk_f = cut(xn[:, 1, :], 0, J, S)
        bt_f, kt_f, rt_f = (cut(work, 1024 * n, J, S) for n in range(3))
        rk_f = a_f
        v_t, b_t, k_t = (cut(work, at, TT, RW) for at in (8208, 9232, 7184))
        gram = cut(work, 10256, TT, 2, 2, 2 * J * N)
        inv = cut(work, 3600, TT, 2 * J, N)
        invT = cut(work, 4624, TT, 2 * J, N)
        yy = cut(work, 5648, TT, 2 * J, N)
        low = cut(xn[:, 0, :], 0, TT, 2 * J, N)
        akv = yy
        u_t = inv
        rn = cut(xn[:, 0, :], 0, 2 * J, N)
        y_t = cut(work, 0, TT, RW)
        y_q = cut(work, 1024, TT, RW)
        gl_t = cut(work, 2048, TT, RW)
        mixT = xT
        at_small = [0]

        def tiny(*shape):
            at = at_small[0]
            at_small[0] += int(np.prod(shape))
            return cut(small, at, *shape)

        ss_x, rs_x = tiny(2), tiny(2)
        ss_c, rs_c = tiny(2, 2), tiny(2, 2)
        ss_qk, rs_qk, ss_kr = tiny(2, 16), tiny(2, 16), tiny(2)
        inv_freq, posf = tiny(HALF), tiny(2)
        ang, turn, trig = tiny(2, HALF), tiny(2, 2, HALF), tiny(2, 2, HALF)
        mx, den = tiny(2, H), tiny(2, H)
        bonus, d_end = tiny(2, H), tiny(J, NCH)
        mean, var = tiny(16), tiny(16)

        ld_x, ld_win, ld_rows, ld_front = sem("ld_x"), sem("ld_win"), sem("ld_rows"), sem("ld_front")
        ld_uq, ld_woa, ld_wob = sem("ld_uq"), sem("ld_woa"), sem("ld_wob")
        out_written = sem("out_written")
        pool_step, act_step, dve_step = sem("pool_step"), sem("act_step"), sem("dve_step")
        consts = steps("consts")
        pe_f, act_f, dve_f = steps("pe_front"), steps("act_front"), steps("dve_front")

        ga_sel = cut(work, 0, TT, P)
        sc_sel = cut(work, 256, TT, P)
        sc_T = cut(work, 512, TT, P)
        xg = cut(work, 768, KD, P)
        hs = cut(work, 1792, 2, 512)
        hh = cut(work, 2816, 2, 512)
        hT = cut(work, 3840, 4, P)
        yg = cut(work, 4352, D)
        RT = 7480
        at_rt = [RT]

        def rt(*shape):
            at = at_rt[0]
            at_rt[0] += int(np.prod(shape))
            return cut(work, at, *shape)

        glog, elog, gtop, etop = rt(2, 8), rt(2, E1), rt(2, 8), rt(2, 8)
        gtop_i, etop_i = rt(2, 8), rt(2, 8)
        gsel, esel = rt(2), rt(2, 2)
        g_one, e_one = rt(2, NG), rt(2, 2, 8)
        in_group, spread_g = rt(2, 8), rt(2, NG, 8)
        diffs, w2 = rt(2, 5), rt(2, 2)
        gp = rt(2)
        comb8, mask8 = rt(2, 8), rt(2, 8)
        comb, mask, slot = rt(2, E1), rt(2, E1), rt(2, E1)
        over, over8 = rt(1), rt(8)
        small_e = rt(E2)
        slot_hi = rt(2, E2 + 1)
        over_i = sb("over_i", [P, 1], I32)
        small_i = sb("small_i", [P, E2], I32)
        rtr = sb("rtr", [P, KD * (NG + E1) + NG + E1 + KD * E2])
        wg_sb = cut(rtr, 0, KD, NG)
        we_sb = cut(rtr, KD * NG, KD, E1)
        bg_sb = cut(rtr, KD * (NG + E1), NG)
        be_sb = cut(rtr, KD * (NG + E1) + NG, E1)
        w_router = cut(rtr, KD * (NG + E1) + NG + E1, KD, E2)

        up = cut(work, 0, NPC, 16 + S)
        sum_a = cut(work, 1088, NPC, 16 + S)
        sum_b = cut(work, 2176, NPC, 16 + S)
        pooled = cut(work, 3264, NPC, S)
        vp = cut(work, 4288, NPC, CW - 1 + S)
        yv = cut(work, 5432, NPC, S)
        sv = cut(work, 6456, NPC, S)
        mT = cut(work, 7480, KD, S)
        diag_a, diag_b = cut(xn[:, :, :].rearrange("p t n -> p (t n)"), 0, 16, P), cut(work, 7480, CW - 16, P)
        mean_b = cut(work, 9528, S)
        rstd_b = cut(work, 9784, S)
        lnp = cut(work, 10040, 4, D)
        c_flat = c_sb[:, :, :].rearrange("p t n -> p (t n)")
        conv_rows = cut(c_flat, 0, L2, P)
        cw = cut(c_flat, 2 * P, CW, NPC)
        rc = cut(c_flat, 2 * P + CW * NPC, NPC, 16)
        p_sb = (st[:, :, :].rearrange("p j n -> p (j n)"), st2[:, :, :].rearrange("p j n -> p (j n)"))
        pT = cut(work, 4864, 2, S)
        gate_s = cut(work, 0, TT, D)
        stats = cut(small, 300, TT, 2, 6)
        mv = cut(small, 324, TT, 2)
        rstd = cut(small, 328, TT)

        ld_rtr, ld_conv, ld_pool, ld_lnp, ld_p = sem("ld_rtr"), sem("ld_conv"), sem("ld_pool"), sem("ld_lnp"), sem("ld_p")
        m1 = {k: steps(f"moe1_{k}") for k in ("pe", "act", "dve")}
        piece1 = [sem(f"piece1_{n}") for n in range(HALVES)]
        used1 = sem("used1")
        q_sel, q_gath, q_xg, q_scT, q_silu, q_hid, q_hT, q_hTs, q_yg, q_scat, q_add, q_turn = (
            sem("q_" + n) for n in ("sel", "gathered", "xg", "scT", "silu", "hidden", "hT", "hTs", "yg", "scattered", "added",
                                    "turned"))
        landed = [sem(f"landed_{n}") for n in range(PLACES)]
        used = sem("used")
        bl = {k: steps(f"block2_{k}") for k in ("pe", "act", "dve")}
        e_sel, e_gath, e_xg, e_scT, e_turn, e_silu, e_hid, e_hT, e_hTs, e_yg, e_scat, e_add = (
            sem("e_" + n) for n in ("sel", "gathered", "xg", "scT", "turned", "silu", "hidden", "hT", "hTs", "yg", "scattered", "added"))
        more_done1, more_done2 = sem("more_done1"), sem("more_done2")
        q_sel_w, q_shift, e_sel_w, e_shift = sem("q_sel_w"), sem("q_shift"), sem("e_sel_w"), sem("e_shift")
        ld_gate_w, ld_ple_w, pooled_x = sem("ld_gate_w"), sem("ld_ple_w"), sem("pooled_x")

        NQ = E1 // 4
        UNITS = F2 // 512
        UD = [512] * (FD // 512) + [FD % 512]

        def half_place(i):
            return (i + 2) % HALVES

        def place(n):
            at = (n + 1) % PLACES * PLACE
            return ring[:, at:at + PLACE]

        def diag(tap):
            return diag_a[:, tap, :] if tap < 16 else diag_b[:, tap - 16, :]

        def chunked(v, width):
            return v[:, 0:KD * width].rearrange("p (k n) -> p k n", k=KD)

        def ffn_order(units):
            order = []
            for u in range(units):
                order += [("w1", u), ("w3", u)] + ([("w2", u - 1)] if u else [])
            return order + [("w2", units - 1)]

        MIX = [("in", 1), ("in", 2), ("in", 0), ("pw", 0), ("out", 0), ("out", 1)]
        PLE = [("ple", 0), ("pg", 0), ("pg", 1)]
        DENSE = [(what, u) for u in range(len(UD)) for what in ("w1", "w3", "w2")]
        MOE = ffn_order(UNITS)
        MIX0, DENSE0 = 0, len(MIX)
        PLE0 = DENSE0 + len(DENSE)
        MIX1 = PLE0 + len(PLE)
        MOE0 = MIX1 + len(MIX)
        PLE1 = MOE0 + E2 * len(MOE)

        def read(n):
            return used, n + 1

        def read_moe(what, u):
            return MOE0 + MOE.index((what, u)) + 1

        def read_dense(what, u):
            return read(DENSE0 + DENSE.index((what, u)))

        assert len(MOE) % PLACES == 0 and len(MOE) == 3 * UNITS

        block = ctx.enter_context(nc.Block())

        def row(v, n):
            return v.rearrange("(a n) -> a n", a=1).to_broadcast([P, n])

        @block.sync
        def _(sp):
            for t in range(TT):
                sp.dma_start(x_sb[:, t, :], x[0, t * P:(t + 1) * P, :]).then_inc(ld_x, 16)
            for k in range(KD):
                sp.dma_start(w_in_sb[:, k, :], w_in[0].rearrange("(p k) n -> p k n", k=KD)[:, k, :]).then_inc(ld_win, 16)
            sp.dma_start(w_uq_sb, w_uq[0].rearrange("(k p) h d -> p k (h d)", p=P)).then_inc(ld_uq, 16)
            sp.dma_start(w_uk_sb, w_uk[0].rearrange("p h d -> p (h d)")).then_inc(ld_uq, 16)
            sp.dma_start(w_uv_sb, w_uv[0].rearrange("p h d -> p (h d)")).then_inc(ld_uq, 16)
            wo_rows = w_o[0].rearrange("(k p) n -> p k n", p=P)
            sp.dma_start(w_o_b, wo_rows[:, 4:8, :]).then_inc(ld_wob, 16)
            sp.wait_ge(*pe_f("feat 6"))
            sp.dma_start(w_o_a, wo_rows[:, 0:4, :]).then_inc(ld_woa, 16)
            def quad(q, first, it):
                for i in range(HALVES):
                    j = i % 4
                    at = half_place(i) * HALFP
                    dst = ring[:, at:at + HALFP]
                    src = (w_gate, w_up, w_down)[i // 4]
                    src = src[0][bass.ds(q * 4 + j, 1)] if not first else src[0][j:j + 1]
                    if first:
                        if i == 6:
                            sp.wait_ge(*pe_f("qkv 1"))
                        if i == 8:
                            sp.wait_ge(*dve_f("y gated"))
                            sp.wait_ge(*pe_f("g"))
                        if i == 10:
                            sp.wait_ge(*pe_f("w_o 1"))
                    else:
                        sp.wait_ge(used1, (it - 1) * HALVES + i + 1)
                    src = src.rearrange("a (p k) n -> p (a k n)", p=P)
                    sp.dma_start(dst, src).then_inc(piece1[half_place(i)], 16)

            quad(0, True, 0)
            with sp.Fori(1, NQ) as q:
                quad(q, False, q)
            sp.wait_ge(*m1["dve"]("over"))
            extra = sp.value_load(over_i[0:1, 0:1], min_val=0, max_val=S // CAP1 - 1)
            with sp.If(extra > 0):
                with sp.Fori(1, extra + 1) as r:
                    with sp.Fori(0, NQ) as q:
                        quad(q, False, r * NQ + q)
                sp.wait_ge(more_done1, 1)

            def piece(n, src, slot_free=True):
                if n >= PLACES:
                    sp.wait_ge(used, n - PLACES + 1)
                elif (n + 1) % PLACES == 6:
                    sp.wait_ge(*pe_f("w_o 1"))
                else:
                    sp.wait_ge(used1, (NQ - 1) * HALVES + min(HALVES, 4 * (n // 2 + 1)))
                dst = place(n)
                dst = dst[:, 0:int(np.prod(src.shape[1:]))]
                if len(src.shape) == 3:
                    dst = dst.rearrange("p (a b) -> p a b", a=src.shape[1])
                sp.dma_start(dst, src).then_inc(landed[(n + 1) % PLACES], 16)

            def mixer_pieces(l, n0):
                w_i = w_in_2[l].rearrange("(p k) n -> p k n", k=KD)
                w_u = w_out_2[l].rearrange("(k p) n -> p k n", p=P)
                for n, (what, a) in enumerate(MIX):
                    if what == "in":
                        src = w_i[:, :, a * 512:(a + 1) * 512]
                    elif what == "pw":
                        src = conv_pw_2[l].rearrange("(k p) n -> p k n", p=P)
                    else:
                        src = w_u[:, 4 * a:4 * a + 4, :]
                    piece(n0 + n, src)
                    if what == "pw":
                        sp.dma_start(place(n0 + n)[:, 4 * 512:5 * 512].rearrange("p (g d) -> p g d", g=NPC),
                                     pool_w_2[l].rearrange("g c d -> c g d")).then_inc(ld_pool, 16)

            def ple_pieces(l, n0):
                w_g = ple_gate_w_2[l].rearrange("(p k) n -> p k n", k=KD)
                piece(n0, ple_w_2[l].rearrange("(k p) n -> p k n", p=P))
                piece(n0 + 1, w_g[:, 0:4, :])
                piece(n0 + 2, w_g[:, 4:8, :])

            mixer_pieces(0, MIX0)
            for n, (what, u) in enumerate(DENSE):
                f0, f = 512 * u, UD[u]
                if what == "w2":
                    src = dense_w2_2[0][f0:f0 + f, :].rearrange("(p c) n -> p c n", p=P)
                else:
                    src = (dense_w1_2 if what == "w1" else dense_w3_2)[0].rearrange("(p k) f -> p k f", k=KD)[:, :, f0:f0 + f]
                piece(DENSE0 + n, src)
            ple_pieces(0, PLE0)
            mixer_pieces(1, MIX1)

            def expert_pieces(e, it):
                for i, (what, u) in enumerate(MOE):
                    n = MOE0 + i
                    sp.wait_ge(used, it * len(MOE) + (n - PLACES + 1))
                    dst = place(n)
                    if what == "w2":
                        src = exp_w2_2[0][bass.ds(e, 1), u * 512:(u + 1) * 512, :].rearrange("a (p c) n -> p (a c n)", p=P)
                    else:
                        src = (exp_w1_2 if what == "w1" else exp_w3_2)[0][bass.ds(e, 1)]
                        src = src.rearrange("a (p k) f -> p (a k) f", k=KD)[:, :, u * 512:(u + 1) * 512]
                        dst = chunked(dst, 512)
                    sp.dma_start(dst, src).then_inc(landed[(n + 1) % PLACES], 16)

            with sp.Fori(0, E2) as e:
                expert_pieces(e, e)
            sp.wait_ge(*bl["dve"]("over"))
            extra2 = sp.value_load(over_i[0:1, 0:1], min_val=0, max_val=S // CAP2 - 1)
            with sp.If(extra2 > 0):
                with sp.Fori(E2, 2 * E2) as e:
                    expert_pieces(e - E2, e)
                sp.wait_ge(more_done2, 1)
            w_g = ple_gate_w_2[1].rearrange("(p k) n -> p k n", k=KD)
            for a in range(3):
                n = PLE1 + a
                sp.wait_ge(used, n - PLACES + 1)
                src = w_g[:, 4 * a - 4:4 * a, :] if a > 0 else ple_w_2[1].rearrange("(k p) n -> p k n", p=P)
                dst = place(n)[:, 0:src.shape[1] * D].rearrange("p (a b) -> p a b", b=D)
                sp.dma_start(dst, src).then_inc(ld_gate_w if a > 0 else ld_ple_w, 16)
            for t in range(TT):
                sp.wait_ge(*bl["dve"](f"x 1 {t}"))
                sp.dma_start(out[0, t * P:(t + 1) * P, :], x_sb[:, t, :]).then_inc(out_written, 16)
            sp.wait_ge(out_written, 16 * TT)

        @block.gpsimd
        def _(pool):
            count = [0]

            def link(ins):
                count[0] += 1
                ins.then_inc(pool_step, 1)
                pool.wait_ge(pool_step, count[0])

            link(pool.memset(ident[:, :], 0.0))
            consts.raise_by(pool.affine_select(out=ident[:, :], in_=ident[:, :], compare_op=ALU.not_equal, fill=1.0, base=0,
                                               pattern=[[-1, P]], channel_multiplier=1), "ident")
            link(pool.memset(ones[:, :], 1.0))
            link(pool.memset(zero[:, :], 0.0))
            link(pool.memset(raw[:, :, 0:1], 0.0))
            for n in range(HALF):
                f = float(np.float32(1.0) / np.float32(ROPE_THETA ** (n / HALF)))
                link(pool.memset(inv_freq[:, n:n + 1], f))
            link(pool.memset(cmask, 0.0))
            link(pool.affine_select(out=cmask[:, P:S], in_=cmask[:, P:S], compare_op=ALU.is_ge, fill=NEG, base=0,
                                    pattern=[[-1, P]], channel_multiplier=1))
            link(pool.affine_select(out=before[:, :], in_=ones[:, :], compare_op=ALU.is_gt, fill=0.0, base=0,
                                    pattern=[[1, P]], channel_multiplier=-1))
            link(pool.memset(blk, 0.0))
            link(pool.memset(hsel, 0.0))
            for h in range(2):
                half = slice(N * h, N * h + N)
                link(pool.memset(blk[half, N * h:N * h + N], 1.0))
                link(pool.memset(hsel[half, h:h + 1], 1.0))
            link(pool.memset(rst, 1.0))
            link(pool.memset(rst.rearrange("p (c t) -> p c t", t=N)[:, :, 0:1], 0.0))
            for h in range(2):
                half = slice(N * h, N * h + N)
                link(pool.affine_select(out=m_lt[half, :], in_=ones[half, 0:N], compare_op=ALU.is_gt, fill=0.0, base=0,
                                        pattern=[[1, N]], channel_multiplier=-1))
                link(pool.affine_select(out=m_le[half, :], in_=ones[half, 0:N], compare_op=ALU.is_ge, fill=0.0, base=0,
                                        pattern=[[1, N]], channel_multiplier=-1))
                link(pool.affine_select(out=idh[half, :], in_=ones[half, 0:N], compare_op=ALU.is_equal, fill=0.0, base=0,
                                        pattern=[[1, N]], channel_multiplier=-1))
            for n, m in enumerate(LVL):
                nb = N // (2 * m)
                for h in range(2):
                    half = slice(N * h, N * h + N)
                    v = lvl[half, n, :].rearrange("p (b u i) -> p b u i", u=2, i=m)
                    link(pool.memset(lvl[half, n, :], 0.0))
                    link(pool.memset(v[:, :, 1, :], 1.0))
                    link(pool.affine_select(out=v[:, :, 1, :], in_=v[:, :, 1, :], compare_op=ALU.is_ge, fill=0.0, base=0,
                                            pattern=[[-2 * m, nb], [0, m]], channel_multiplier=1))
                    link(pool.affine_select(out=v[:, :, 1, :], in_=v[:, :, 1, :], compare_op=ALU.is_gt, fill=0.0, base=m,
                                            pattern=[[2 * m, nb], [0, m]], channel_multiplier=-1))
            link(pool.iota(iota[:, :], pattern=[[1, P]], base=0, channel_multiplier=0,
                           allow_small_or_imprecise_dtypes=True))
            link(pool.iota(iota_q[:, :], pattern=[[0, 4], [1, CAP1]], base=0, channel_multiplier=0,
                           allow_small_or_imprecise_dtypes=True))
            consts.raise_by(pool.iota(thr[:, :], pattern=[[1, 8]], base=1, channel_multiplier=0,
                                      allow_small_or_imprecise_dtypes=True), "all")
            for dst, src in ((wg_sb, w_group[0].rearrange("(p k) n -> p k n", k=KD)),
                             (we_sb, w_expert[0].rearrange("(p k) n -> p k n", k=KD)),
                             (bg_sb, row(b_group[0], NG)), (be_sb, row(b_expert[0], E1)),
                             (w_router, router_w_2[0].rearrange("(p k) n -> p k n", k=KD))):
                pool.dma_start(dst, src).then_inc(ld_rtr, 16)
            ba, bd, bp = bl["act"], bl["dve"], bl["pe"]
            pool.wait_ge(*dve_f("qk"))
            pool.wait_ge(*act_f("c squares"))
            pool.dma_start(conv_rows[0:CW * NPC], conv_w_2.rearrange("l j (c b) -> (j c) l b", b=P)).then_inc(ld_conv, 16)
            pool.wait_ge(*dve_f("x1 1"))
            for l in range(L2):
                if l == 1:
                    pool.wait_ge(*bd("ln2 0 1"))
                    pool.wait_ge(*bp("pT 0"))
                for n, v in enumerate((ln1_g_2, ln1_b_2, ln2_g_2, ln2_b_2)):
                    pool.dma_start(lnp[:, n, :], row(v[l], D)).then_inc(ld_lnp, 16)
                for t in range(TT):
                    pool.dma_start(p_sb[t], p_2[l, 0, t * P:(t + 1) * P, :]).then_inc(ld_p, 16)
                pool.wait_ge(*ba(f"pool in {l}"))
                W = 16 + S
                add = pool.tensor_tensor
                link(add(sum_a[:, :, 1:W], up[:, :, 1:W], up[:, :, 0:W - 1], ALU.add))
                link(add(sum_b[:, 1:, 3:W], sum_a[:, 1:, 3:W], sum_a[:, 1:, 1:W - 2], ALU.add))
                link(add(sum_a[:, 2:, 7:W], sum_b[:, 2:, 7:W], sum_b[:, 2:, 3:W - 4], ALU.add))
                link(add(sum_b[:, 3:, 15:W], sum_a[:, 3:, 15:W], sum_a[:, 3:, 7:W - 8], ALU.add))
                for g, (w, src) in enumerate(zip(WINDOWS, (sum_a, sum_b, sum_a, sum_b))):
                    link(pool.tensor_scalar(pooled[:, g, 16:], src[:, g, 32:], 1.0 / w, None, ALU.mult))
                    link(add(pooled[:, g, 0:16], src[:, g, 16:32], rc[:, g, :], ALU.mult))
                add(pooled, pooled, up[:, :, 16:], ALU.subtract).then_inc(pooled_x, 1)

        @block.scalar
        def _(act):
            count = [0]

            def link(ins):
                count[0] += 1
                ins.then_inc(act_step, 1)
                act.wait_ge(act_step, count[0])

            def rowload(name, src, n):
                act.dma_start(rows[ROWS[name]:ROWS[name] + n, :], src).then_inc(ld_rows, 16)

            rowload("mu", rw_mu[0].rearrange("(a b) -> a b", b=P), NF)
            for name, v in (("w0", rw_w0), ("a0", rw_a0), ("k_k", rw_k_k), ("k_a", rw_k_a)):
                rowload(name, v[0].rearrange("(a b) -> a b", b=P), J)
            rowload("r_k", rw_r_k[0].rearrange("(a h) n -> a (h n)", h=2), J)
            rowload("g_cq", g_cq[0].rearrange("(a b) -> a b", b=P), 2)
            rowload("g_ckv", g_ckv[0].rearrange("(a b) -> a b", b=P), 1)
            rowload("g_mla", g_mla_out[0].rearrange("(a b) -> a b", b=P), J)
            for name, v in (("pool_scale", pool_scale_2), ("conv_b", conv_b_2), ("ln_g", conv_ln_g_2), ("ln_b", conv_ln_b_2)):
                rowload(name, v.rearrange("l (a b) -> (l a) b", b=P), L2 * NPC)
            front = [
                (gcol[:, 0, :], g_mix[0].rearrange("(p k) -> p k", k=KD)), (gcol[:, 1, :], g_ffn[0].rearrange("(p k) -> p k", k=KD)),
                (w2a2[0:N, :], rw_w2[0]), (w2a2[N:P, :], rw_a2[0]), (g2w, rw_g2[0]),
                (lnx[:, 0, :], row(rw_lnx_g[0], RW)), (lnx[:, 1, :], row(rw_lnx_b[0], RW)),
                (gqk[:, 0, :], row(g_qn[0], QK)), (gqk[:, 1, :], row(g_kn[0], QK)),
                (pos_i[:, 0:1], positions[0, 0:P].rearrange("(p a) -> p a", a=1)),
                (pos_i[:, 1:2], positions[0, P:S].rearrange("(p a) -> p a", a=1)),
            ]
            for dst, src in front:
                act.dma_start(dst, src).then_inc(ld_front, 16)

            for t in range(TT):
                act.wait_ge(ld_x, 16 * TT)
                act_f.raise_by(act.activation(xn[:, t, :], x_sb[:, t, :], ACT.Square, accum_out=ss_x[:, t:t + 1]), f"x squares {t}")
            act.wait_ge(*dve_f("x var"))
            act_f.raise_by(act.activation(rs_x, ss_x, ACT.Sqrt), "x std")

            for t in range(TT):
                act.wait_ge(*pe_f(f"c {t}"))
                act_f.raise_by(act.activation(c_sb[:, t, :], ps[:, t, 0:C_W], ACT.Copy), f"c {t}")
            act.wait_ge(*act_f("c 1"))
            for t in range(TT):
                act.activation(sq[:, 0, 0:Q_RANK], c_sb[:, t, 0:Q_RANK], ACT.Square, accum_out=ss_c[:, t, 0:1]).then_inc(act_step, 1)
                act.activation(rope_t[:, 0, 0:ROPE], c_sb[:, t, Q_RANK + KV_RANK:], ACT.Square,
                               accum_out=ss_kr[:, t:t + 1]).then_inc(act_step, 1)
                count[0] += 2
                ins = act.activation(sq[:, 1, 0:KV_RANK], c_sb[:, t, Q_RANK:Q_RANK + KV_RANK], ACT.Square,
                                     accum_out=ss_c[:, t, 1:2])
                if t == 0:
                    link(ins)
            act_f.raise_by(ins, "c squares")
            act.wait_ge(act_step, count[0])
            act.wait_ge(*act_f("c squares"))
            act.wait_ge(*dve_f("c var"))
            act_f.raise_by(act.activation(rs_c, ss_c, ACT.Sqrt), "c std")
            act_f.raise_by(act.activation(trig, turn, ACT.Sin), "trig")
            act.wait_ge(*consts("all"))

            def raw_in(i):
                act.wait_ge(*pe_f(f"feat {i}"))
                act_f.raise_by(act.activation(raw[:, 2 * i:2 * i + 2, 1:S + 1],
                                              ps[:, 4 + i % 4, :].rearrange("p (a t) -> p a t", a=2), ACT.Copy), f"raw {i}")

            def qkv_in(t):
                act.wait_ge(*pe_f(f"qkv {t}"))
                link(act.activation(sq[:, t, 0:H * QK].rearrange("p (a n) -> p a n", a=2), ps[:, 0:2, 0:384], ACT.Square))
                act_f.raise_by(act.activation(sq[:, t, H * QK:], ps[:, 2, :], ACT.Square), f"qk squares {t}")
                act_f.raise_by(act.activation(vt[:, t, :], ps[:, 3, :], ACT.Copy), f"v {t}")
                act.wait_ge(*dve_f(f"qk var {t}"))
                act_f.raise_by(act.activation(rs_qk[:, t, :], ss_qk[:, t, :], ACT.Sqrt), f"qk std {t}")

            for i in range(NF // 2):
                raw_in(i)
                if i in (2, 4):
                    qkv_in((i - 2) // 2)

            for g in range(8):
                t, a = g // 4, g % 4
                act.wait_ge(*pe_f(f"qkT {g}"))
                act_f.raise_by(act.activation(qkT[0:QK, 4 * a:4 * a + 4, t * P:(t + 1) * P],
                                              ps[0:QK, g, :].rearrange("p (a t) -> p a t", a=4), ACT.Copy), f"qkT {g}")
            for t, pr in ((0, probs0), (1, probs1)):
                act.wait_ge(*dve_f(f"max {t}"))
                for h in range(H):
                    ins = act.activation(pr[:, h, :], pr[:, h, :], ACT.Exp, bias=mx[:, t, h:h + 1], scale=QK ** -0.5,
                                         accum_out=den[:, t, h:h + 1])
                    if h < H - 1:
                        ins.then_inc(act_step, 1)
                        count[0] += 1
                act_f.raise_by(ins, f"probs {t}")
            act.wait_ge(*pe_f("pT 0"))
            act_f.raise_by(act.activation(pT0, ps[:, 6:8, :].rearrange("p b (a t) -> p (b a) t", a=4), ACT.Copy), "pT0")
            act.wait_ge(*pe_f("pT 1"))
            act_f.raise_by(act.activation(pT1[:, 0:8, :], ps[:, 0:2, :].rearrange("p b (a t) -> p (b a) t", a=4), ACT.Copy),
                           "pT1")
            act.wait_ge(*dve_f("mla"))
            link(act.activation(probs1[:, 0:2, :].rearrange("p a t -> p (a t)"), mla[:, 0, :], ACT.Square,
                                accum_out=ss_x[:, 0:1]))
            act_f.raise_by(act.activation(probs1[:, 0:2, :].rearrange("p a t -> p (a t)"), mla[:, 1, :], ACT.Square,
                                          accum_out=ss_x[:, 1:2]), "mla squares")
            act.wait_ge(*dve_f("mla var"))
            act_f.raise_by(act.activation(rs_x, ss_x, ACT.Sqrt), "mla std")

            act.wait_ge(*dve_f("mixed"))
            link(act.activation(sg[:, :], gl_f, ACT.Sigmoid))
            act_f.raise_by(act.activation(wa_f[0:N, :], wa_f[0:N, :], ACT.Tanh), "tanh")
            act.wait_ge(*pe_f("low rank"))
            act.wait_ge(*pe_f("mlaT"))
            for j in range(J):
                link(act.activation(sig_f[:, j, :], ps[:, j // 2, (j % 2) * S:(j % 2) * S + S], ACT.Sigmoid,
                                    bias=cols[:, ROWS["w0"] + j:ROWS["w0"] + j + 1]))
            act_f.raise_by(act.activation(a_f[:, 0, :], ps[:, 2, 0:S], ACT.Sigmoid, bias=cols[:, ROWS["a0"]:ROWS["a0"] + 1]),
                           "sig w")
            for j in range(1, J):
                ins = act.activation(a_f[:, j, :], ps[:, 2 + j // 2, (j % 2) * S:(j % 2) * S + S], ACT.Sigmoid,
                                     bias=cols[:, ROWS["a0"] + j:ROWS["a0"] + j + 1])
                if j < J - 1:
                    link(ins)
            act_f.raise_by(ins, "sig a")
            act.wait_ge(*dve_f("kk var"))
            act_f.raise_by(act.activation(tmp_f, tmp_f, ACT.Sqrt), "kk std")
            act.wait_ge(*dve_f("cum"))
            act_f.raise_by(act.activation(d_inv, cum, ACT.Exp, scale=DECAY), "d inv")
            act_f.raise_by(act.activation(d_inc, cum, ACT.Exp, scale=-DECAY), "d inc")
            act_f.raise_by(act.activation(d_ex, d_ex, ACT.Exp, scale=-DECAY), "d ex")
            for n, dst in enumerate((v_t, b_t, k_t)):
                for t in range(TT):
                    act.wait_ge(*pe_f(f"turned {n} {t}"))
                    act_f.raise_by(act.activation(dst[:, t, :], ps[:, 2 * n + t, :], ACT.Copy), f"turned {n} {t}")
            for n in range(1, len(LVL)):
                for t in range(TT):
                    act.wait_ge(*pe_f(f"lx {n} {t}"))
                    act_f.raise_by(act.activation(yy[:, t].rearrange("p h n -> p (h n)"), ps[:, 4 * t, :], ACT.Copy), f"lx {n} {t}")
            for c in range(NCH):
                half = slice(N * (c % 2), N * (c % 2) + N)
                act.wait_ge(*pe_f(f"u {c}"))
                act_f.raise_by(act.activation(u_t[half, c // 2].rearrange("p h n -> p (h n)"), ps[half, 2, :], ACT.Copy), f"u {c}")
            act.wait_ge(*pe_f("g"))
            act_f.raise_by(act.activation(gl_t, ps[:, 0:2, :], ACT.Copy), "g")
            act.wait_ge(*dve_f("y var"))
            act_f.raise_by(act.activation(var, var, ACT.Sqrt), "y std")
            m1a, m1d, m1p = m1["act"], m1["dve"], m1["pe"]
            ba, bd, bp = bl["act"], bl["dve"], bl["pe"]
            for t in range(TT):
                act.wait_ge(*dve_f("x1 1"))
                m1a.raise_by(act.activation(xn[:, t, :], x_sb[:, t, :], ACT.Square, accum_out=ss_x[:, t:t + 1]), f"squares {t}")
            act.wait_ge(*m1d("var"))
            m1a.raise_by(act.activation(rs_x, ss_x, ACT.Sqrt), "std")
            act.wait_ge(*m1d("diffs"))
            m1a.raise_by(act.activation(diffs, diffs, ACT.Exp), "exp")

            def quad_act(it):
                act.wait_ge(q_turn, it + 1)
                act.activation(sc_T, ps[:, 3, 256:512].rearrange("p (t n) -> p t n", t=TT), ACT.Copy).then_inc(q_scT, 1)
                act.wait_ge(used1, it * HALVES + 8)
                act.activation(hs[:, 0, 0:F1], ps[:, 2, 0:F1], ACT.Silu).then_inc(q_silu, 1)
                act.wait_ge(used1, it * HALVES + 12)
                act.activation(yg.rearrange("p (b n) -> p b n", b=2), ps[:, 4:6, :], ACT.Copy).then_inc(q_yg, 1)

            with act.Fori(0, NQ) as q:
                quad_act(q)
            extra = act.value_load(over_i[0:1, 0:1], min_val=0, max_val=S // CAP1 - 1)
            with act.If(extra > 0):
                with act.Fori(1, extra + 1) as r:
                    with act.Fori(0, NQ) as q:
                        quad_act(r * NQ + q)

            def turned_x(l, when):
                for b in range(4):
                    act.wait_ge(*bp(f"xT {when} {b}"))
                    t, g = b // 2, b % 2
                    ba.raise_by(act.activation(xT[:, 4 * g:4 * g + 4, t * P:(t + 1) * P],
                                               ps[:, b, :].rearrange("p (k t) -> p k t", k=4), ACT.Copy), f"xT {when} {b}")

            def mixer_act(l):
                turned_x(l, f"mix {l}")
                for i in range(NPC):
                    act.wait_ge(*(bp(f"conv in {l} {i}") if i < NPC - 1 else read((MIX0, MIX1)[l] + 1)))
                    ba.raise_by(act.activation(sv[:, i, :], ps[:, i, S:2 * S], ACT.Sigmoid), f"gate {l} {i}")
                    if i == 0:
                        act.wait_ge(*bd(f"taps {l}"))
                    for tap in range(11 * i, min(11 * i + 11, CW)):
                        ins = act.activation(diag(tap), ident[:, :], ACT.Copy, scale=cw[:, tap, NPC - 1:NPC])
                        if tap == CW - 1:
                            ba.raise_by(ins, f"diagonals {l}")
                act.wait_ge(*read((MIX0, MIX1)[l] + 2))
                act.wait_ge(*bd(f"pads {l}"))
                ba.raise_by(act.activation(up[:, :, 16:].rearrange("p (b a) t -> p b a t", b=2),
                                           ps[:, 4:6, :].rearrange("p b (a t) -> p b a t", a=2), ACT.Copy), f"pool in {l}")
                act.wait_ge(*bp(f"conv 3 {l}"))
                b = ROWS["conv_b"] + l * NPC + NPC - 1
                ba.raise_by(act.activation(yv[:, NPC - 1, :], ps[:, 0, 0:S], ACT.Identity, bias=cols[:, b:b + 1]), f"conv 3 {l}")
                act.wait_ge(*bd(f"centred {l}"))
                ba.raise_by(act.activation(sv, yv, ACT.Square), f"squares {l}")
                act.wait_ge(*bd(f"conv var {l}"))
                ba.raise_by(act.activation(rstd_b, rstd_b, ACT.Sqrt), f"conv std {l}")
                act.wait_ge(*bd(f"conv normed {l}"))
                for j in range(NPC):
                    g, b = ROWS["ln_g"] + l * NPC + j, ROWS["ln_b"] + l * NPC + j
                    ins = act.activation(sv[:, j, :], yv[:, j, :], ACT.Silu, bias=cols[:, b:b + 1], scale=cols[:, g:g + 1])
                    if j < NPC - 1:
                        link(ins)
                ba.raise_by(ins, f"silu {l}")
                act.wait_ge(*read((MIX0, MIX1)[l] + 3))
                ba.raise_by(act.activation(mT[:, 4:8, :].rearrange("p (b a) t -> p b (a t)", b=2), ps[:, 2:4, :], ACT.Copy),
                            f"conv out {l}")
                for t in range(TT):
                    act.wait_ge(*bd(f"ln1 var {l} {t}"))
                    ba.raise_by(act.activation(rstd[:, t:t + 1], rstd[:, t:t + 1], ACT.Sqrt), f"ln1 std {l} {t}")

            def tail_act(l):
                for t in range(TT):
                    act.wait_ge(*bd(f"ln2 var {l} {t}"))
                    ba.raise_by(act.activation(rstd[:, t:t + 1], rstd[:, t:t + 1], ACT.Sqrt), f"ln2 std {l} {t}")
                    if t == 0:
                        act.wait_ge(*bp(f"pT {l}"))
                        ba.raise_by(act.activation(pT, ps[:, 0, :].rearrange("p (k t) -> p k t", k=2), ACT.Copy), f"pT {l}")
                turned_x(l, f"ple {l}")
                for t in range(TT):
                    act.wait_ge(*(read(PLE0 + 2) if (l, t) == (0, 1) else bp(f"ple gate {l} {t}")))
                    ba.raise_by(act.activation(gate_s[:, t, :].rearrange("p (b n) -> p b n", b=2), ps[:, 2 * t:2 * t + 2, :],
                                               ACT.Sigmoid), f"ple gate {l} {t}")

            mixer_act(0)
            turned_x(0, "ffn 0")
            for u in range(len(UD)):
                for t in range(TT):
                    act.wait_ge(*(bp(f"up {u}") if t == 0 else read_dense("w3", u)))
                    if u > 0:
                        act.wait_ge(*bd(f"hidden {u - 1} {t}"))
                    ba.raise_by(act.activation(hs[:, t, 0:UD[u]], ps[:, t, 0:UD[u]], ACT.Silu), f"silu {u} {t}")
            tail_act(0)
            mixer_act(1)
            turned_x(1, "ffn 1")
            for t in range(TT):
                ba.raise_by(act.activation(xn[:, t, :], x_sb[:, t, :], ACT.Copy), f"x kept {t}")
            act.wait_ge(*bd("diffs"))
            ba.raise_by(act.activation(diffs, diffs, ACT.Exp), "exp")

            def expert_act(e, r):
                it = e + r * E2
                for u in range(UNITS):
                    b = u % 2
                    act.wait_ge(used, it * len(MOE) + read_moe("w1", u))
                    if u >= 2:
                        act.wait_ge(e_hid, it * UNITS + (u - 1))
                    act.activation(hs[:, b, :], ps[:, b, :], ACT.Silu).then_inc(e_silu, 1)
                    if u == 2:
                        act.wait_ge(e_turn, it + 1)
                        act.activation(sc_T, ps[:, 6, 0:2 * P].rearrange("p (t n) -> p t n", t=TT), ACT.Copy).then_inc(e_scT, 1)
                act.wait_ge(used, it * len(MOE) + read_moe("w2", UNITS - 1))
                act.activation(yg.rearrange("p (b n) -> p b n", b=2), ps[:, 4:6, :], ACT.Copy).then_inc(e_yg, 1)

            def pass_act(r):
                with act.Fori(0, E2) as e:
                    expert_act(e, r)

            pass_act(0)
            extra2 = act.value_load(over_i[0:1, 0:1], min_val=0, max_val=S // CAP2 - 1)
            with act.If(extra2 > 0):
                pass_act(1)
            tail_act(1)

        @block.tensor
        def _(pe):
            mm, turn_ = pe.matmul, pe.transpose

            pe.wait_ge(*consts("ident"))
            pe.wait_ge(ld_rows, 16 * 13)
            pe_f.raise_by(turn_(ps[:, 7, 0:NROWS], rows[0:NROWS, :], ident[0:NROWS, 0:NROWS]), "cols")
            for t in range(TT):
                pe.wait_ge(*dve_f(f"xn {t}"))
                for g in range(2):
                    for k in range(4):
                        ins = turn_(ps[:, 2 * t + g, k * P:(k + 1) * P],
                                    xn[:, t, :].rearrange("p (q k) -> p k q", k=KD)[:, 4 * g + k, :], ident[:, :])
                    pe_f.raise_by(ins, f"xT {t} {g}")
            pe.wait_ge(ld_win, 16 * KD)
            pe.wait_ge(*dve_f("xT 1 1"))
            for t in range(TT):
                for k in range(KD):
                    ins = mm(ps[:, t, 0:C_W], xT[:, k, t * P:(t + 1) * P], w_in_sb[:, k, 0:C_W], start=(k == 0), stop=(k == KD - 1))
                pe_f.raise_by(ins, f"c {t}")
            pe.wait_ge(*dve_f("cols"))

            def features(i):
                if i >= 4:
                    pe.wait_ge(*act_f(f"raw {i - 4}"))
                for u in range(2):
                    f0 = C_W + (2 * i + u) * P
                    for k in range(KD):
                        ins = mm(ps[:, 4 + i % 4, u * S:(u + 1) * S], w_in_sb[:, k, f0:f0 + P], xT[:, k, :],
                                 start=(k == 0), stop=(k == KD - 1))
                pe_f.raise_by(ins, f"feat {i}")

            def qkv(t):
                for a in range(2):
                    for k in range(2):
                        mm(ps[:, a, 0:384], cT[:, k, t * P:(t + 1) * P], w_uq_sb[:, k, 384 * a:384 * a + 384],
                           start=(k == 0), stop=(k == 1))
                mm(ps[:, 2, :], cT[:, 2, t * P:(t + 1) * P], w_uk_sb, start=True, stop=True)
                pe_f.raise_by(mm(ps[:, 3, :], cT[:, 2, t * P:(t + 1) * P], w_uv_sb, start=True, stop=True), f"qkv {t}")

            for i in range(NF // 2):
                features(i)
                if i == 1:
                    pe.wait_ge(*dve_f("c normed"))
                    pe.wait_ge(*act_f("c 1"))
                    for t in range(TT):
                        for j in range(3):
                            at = (j % 2) * S + t * P
                            ins = turn_(ps[:, j // 2, at:at + P], c_sb[:, t, j * P:(j + 1) * P], ident[:, :])
                    pe_f.raise_by(ins, "c turned")
                if i == 2:
                    pe.wait_ge(ld_uq, 48)
                    pe.wait_ge(*dve_f("cT"))
                    qkv(0)
                if i == 4:
                    pe.wait_ge(*act_f("v 0"))
                    pe.wait_ge(*dve_f("qk read 0"))
                    qkv(1)
            pe.wait_ge(*dve_f("qk"))
            pe.wait_ge(*act_f("v 1"))
            pe.wait_ge(*act_f("raw 6"))
            for t in range(TT):
                for g in range(4):
                    for a in range(4):
                        ins = turn_(ps[0:QK, 4 * t + g, a * P:(a + 1) * P], qk[:, t, 4 * g + a, :], ident[:, :])
                    pe_f.raise_by(ins, f"qkT {4 * t + g}")
            pe.wait_ge(*act_f("qkT 7"))
            for h in range(H):
                ins = mm(ps[:, h // 4, (h % 4) * P:(h % 4 + 1) * P], qkT[0:QK, h, 0:P], qkT[0:QK, H + h, 0:P], start=True, stop=True)
            pe_f.raise_by(ins, "scores 0")
            for h in range(H):
                ins = mm(ps[:, 2 + h // 2, (h % 2) * S:(h % 2 + 1) * S], qkT[0:QK, h, P:S], qkT[0:QK, H + h, :], start=True, stop=True)
            pe_f.raise_by(ins, "scores 1")
            pe.wait_ge(*act_f("probs 0"))
            for h in range(H):
                ins = turn_(ps[:, 6 + h // 4, (h % 4) * P:(h % 4 + 1) * P], probs0[:, h, :], ident[:, :])
            pe_f.raise_by(ins, "pT 0")
            pe.wait_ge(*act_f("probs 1"))
            for h in range(H):
                for b in range(2):
                    i = 2 * h + b
                    ins = turn_(ps[:, i // 4, (i % 4) * P:(i % 4 + 1) * P], probs1[:, h, b * P:(b + 1) * P], ident[:, :])
            pe_f.raise_by(ins, "pT 1")
            pe.wait_ge(*act_f("pT0"))
            for h in range(H):
                ins = mm(ps[:, 4, h * VD:(h + 1) * VD], pT0[:, h, :], vt[:, 0, h * VD:(h + 1) * VD], start=True, stop=True)
            pe.wait_ge(*act_f("pT1"))
            pe.wait_ge(*dve_f("pT1"))
            for h in range(H):
                for b in range(2):
                    ins = mm(ps[:, 5, h * VD:(h + 1) * VD], pT1[:, 2 * h + b, :], vt[:, b, h * VD:(h + 1) * VD],
                             start=(b == 0), stop=(b == 1))
            pe_f.raise_by(ins, "pv")
            pe.wait_ge(*dve_f("mla normed"))
            for t in range(TT):
                for j in range(J):
                    ins = turn_(ps[:, 6 + j // 2, (j % 2) * S + t * P:(j % 2) * S + (t + 1) * P], mla[:, t, j * P:(j + 1) * P],
                                ident[:, :])
            pe_f.raise_by(ins, "mlaT")

            pe.wait_ge(ld_front, 16 * 11)
            pe.wait_ge(*act_f("tanh"))
            for j in range(J):
                for n, half in enumerate((slice(0, N), slice(N, P))):
                    ins = mm(ps[:, 2 * n + j // 2, (j % 2) * S:(j % 2 + 1) * S], w2a2[half, j * P:(j + 1) * P], wa_f[half, :],
                             start=True, stop=True)
            pe_f.raise_by(ins, "low rank")
            pe.wait_ge(*dve_f("kk squares"))
            for b in range(2):
                ins = mm(ps[:, 4 + b, :], blk, tmp_f[:, 2 * b:2 * b + 2, :].rearrange("p a t -> p (a t)"), start=True, stop=True)
            pe_f.raise_by(ins, "kk sums")
            pe.wait_ge(ld_woa, 16)
            pe.wait_ge(*dve_f("mla mixed"))
            for t in range(TT):
                if t == 1:
                    pe.wait_ge(*dve_f("kk var"))
                for n in range(2):
                    for k in range(4):
                        ins = mm(ps[:, 6 - 2 * t + n, :], mixT[:, k, t * P:(t + 1) * P], w_o_a[:, k, n * 512:(n + 1) * 512],
                                 start=(k == 0), stop=(k == 3))
                pe_f.raise_by(ins, f"w_o mla {t}")
            pe.wait_ge(*act_f("sig a"))
            pe.wait_ge(*dve_f("tilde"))
            for n, src in enumerate((v_f, bt_f, kt_f)):
                if n == 2:
                    pe.wait_ge(*dve_f("x mla 1"))
                for t in range(TT):
                    for j in range(J):
                        ins = turn_(ps[:, 2 * n + t, j * P:(j + 1) * P], src[:, j, t * P:(t + 1) * P], ident[:, :])
                    pe_f.raise_by(ins, f"turned {n} {t}")
                if n == 0:
                    pe.wait_ge(*dve_f("x mla 0"))
                    for tt in range(TT):
                        for j in range(J):
                            ins = mm(ps[:, 6, tt * H + 2 * j:tt * H + 2 * j + 2], rk_f[:, j, tt * P:(tt + 1) * P], hsel,
                                     start=True, stop=True)
                    pe_f.raise_by(ins, "bonus")
            for t in range(TT):
                for m, rhs in enumerate((kk_f, rt_f)):
                    if t == 0 and m == 0:
                        pe.wait_ge(*act_f("turned 0 1"))
                    if t == 0 and m == 1:
                        pe.wait_ge(*act_f("turned 1 1"))
                    if t == 1 and m == 0:
                        pe.wait_ge(*act_f("turned 2 1"))
                    if t == 1 and m == 1:
                        pe.wait_ge(*dve_f("bonus"))
                    for h in range(H):
                        j, par = h // 2, h % 2
                        rows_h = slice(N * par, N * par + N)
                        for n, lhs in enumerate((bt_f, kt_f)):
                            for c in range(2):
                                tok = slice(t * P + c * N, t * P + c * N + N)
                                ins = mm(ps[c * N:(c + 1) * N, 4 * t + 2 * m + par, (n * J + j) * N:(n * J + j + 1) * N],
                                         lhs[rows_h, j, tok], rhs[rows_h, j, tok], start=True, stop=True)
                    pe_f.raise_by(ins, f"gram {t} {m}")

            def per_head(t, bank, left, right, **kw):
                for h in range(2 * J):
                    for c in range(2):
                        half = slice(N * c, N * c + N)
                        ins = mm(ps[half, bank, h * N:(h + 1) * N], left(half, h), right(half, h), **kw)
                return ins

            def natural(h):
                return slice((2 * (h % J) + h // J) * N, (2 * (h % J) + h // J + 1) * N)

            for n in range(len(LVL)):
                for t in range(TT):
                    pe.wait_ge(*dve_f(f"low {n} {t}"))
                    if n == 0:
                        pe_f.raise_by(per_head(t, 4 * t, lambda p_, h: low[p_, t, h, :], lambda p_, h: idh[p_, :], start=True,
                                               stop=True), f"lx {n} {t}")
                        continue
                    pe.wait_ge(*dve_f(f"inv {n - 1} {t}"))
                    pe_f.raise_by(per_head(t, 4 * t, lambda p_, h: low[p_, t, h, :], lambda p_, h: inv[p_, t, h, :], start=True,
                                           stop=True), f"lx {n} {t}")
                if n == 0:
                    continue
                for t in range(TT):
                    pe.wait_ge(*act_f(f"lx {n} {t}"))
                    pe.wait_ge(*dve_f(f"invT {n - 1} {t}"))
                    if n < len(LVL) - 1:
                        pe_f.raise_by(per_head(t, 4 * t + 1, lambda p_, h: invT[p_, t, h, :], lambda p_, h: yy[p_, t, h, :],
                                               start=True, stop=True), f"xlx {n} {t}")
                    pe_f.raise_by(per_head(t, 4 * t + 2, lambda p_, h: yy[p_, t, h, :], lambda p_, h: invT[p_, t, h, :], start=True,
                                           stop=True), f"xlxT {n} {t}")
            pe.wait_ge(*dve_f("invT 5 1"))
            for t in range(TT):
                pe_f.raise_by(per_head(t, 6 + t, lambda p_, h: gram[p_, t, 0, h // J, (J + h % J) * N:(J + h % J + 1) * N],
                                       lambda p_, h: v_t[p_, t, natural(h)], start=True, stop=True), f"akv {t}")

            for c in range(NCH):
                t, half = c // 2, slice(N * (c % 2), N * (c % 2) + N)
                tok = slice(c * N, c * N + N)
                if c > 0:
                    pe.wait_ge(*dve_f(f"state {c - 1}"))
                    for src, bank in ((kk_f, 0), (rt_f, 4)):
                        if bank == 4 and c >= 2:
                            pe.wait_ge(*dve_f(f"y {c - 1}"))
                        for h in range(2 * J):
                            par, j = h // J, h % J
                            rows_h = slice(N * par, N * par + N)
                            ins = mm(ps[half, bank + par, j * N:(j + 1) * N], src[rows_h, j, tok], st[rows_h, j, :], start=True,
                                     stop=True)
                        pe_f.raise_by(ins, f"kk s {c}" if bank == 0 else f"r s {c}")
                pe.wait_ge(*dve_f(f"rn {c}"))
                for h in range(2 * J):
                    ins = mm(ps[half, 2, h * N:(h + 1) * N], invT[half, t, h, :], rn[half, h, :], start=True, stop=True)
                pe_f.raise_by(ins, f"u {c}")
                pe.wait_ge(*act_f(f"u {c}"))
                if c < NCH - 1:
                    for h in range(2 * J):
                        par, j = h // J, h % J
                        o = ps[N * par:N * par + N, 3, j * N:(j + 1) * N]
                        mm(o, b_t[half, t, natural(h)], u_t[half, t, h, :], start=True, stop=False)
                        ins = mm(o, k_t[half, t, natural(h)], v_t[half, t, natural(h)], start=False, stop=True)
                    pe_f.raise_by(ins, f"state {c}")
                for h in range(2 * J):
                    par, j = h // J, h % J
                    o = ps[half, 6, h * N:(h + 1) * N]
                    mm(o, gram[half, t, 1, par, j * N:(j + 1) * N], u_t[half, t, h, :], start=True, stop=False)
                    ins = mm(o, gram[half, t, 1, par, (J + j) * N:(J + j + 1) * N], v_t[half, t, natural(h)], start=False,
                             stop=True)
                pe_f.raise_by(ins, f"y {c}")
            pe.wait_ge(*dve_f("rn 3"))
            for t in range(TT):
                ins = mm(ps[:, t, :], sg[:, t * P:(t + 1) * P], g2w, start=True, stop=True)
            pe_f.raise_by(ins, "g")
            pe.wait_ge(*dve_f("y gated"))
            for t in range(TT):
                for j in range(J):
                    ins = turn_(ps[:, 6 + j // 2, (j % 2) * S + t * P:(j % 2) * S + (t + 1) * P], y_t[:, t, j * P:(j + 1) * P],
                                ident[:, :])
            pe_f.raise_by(ins, "yT")
            pe.wait_ge(ld_wob, 16)
            pe.wait_ge(*dve_f("mixT"))
            for t in range(TT):
                for n in range(2):
                    for k in range(4):
                        ins = mm(ps[:, 2 * t + n, :], mixT[:, 4 + k, t * P:(t + 1) * P], w_o_b[:, k, n * 512:(n + 1) * 512],
                                 start=(k == 0), stop=(k == 3))
                pe_f.raise_by(ins, f"w_o {t}")
            m1a, m1d, m1p = m1["act"], m1["dve"], m1["pe"]
            ba, bd, bp = bl["act"], bl["dve"], bl["pe"]

            def by8(v):
                return v.rearrange("p (q k) -> p k q", k=KD)

            def turn_tile(src, stage, name, t, waits):
                for w in waits:
                    pe.wait_ge(*w)
                for g in range(2):
                    for k in range(4):
                        ins = turn_(ps[:, 2 * t + g, k * P:(k + 1) * P], by8(src[:, t, :])[:, 4 * g + k, :], ident[:, :])
                    stage.raise_by(ins, f"{name} {2 * t + g}")

            def turn_x(src, stage, name, waits):
                for t in range(TT):
                    turn_tile(src, stage, name, t, waits(t))

            def logits(experts, w, at):
                for t in range(TT):
                    for k in range(KD):
                        ins = mm(ps[:, 4 + t, at:at + experts], xT[:, k, t * P:(t + 1) * P], w[:, k, :], start=(k == 0),
                                 stop=(k == KD - 1))
                return ins

            def places(stage, n):
                mm(ps[:, 6, 0:n], before[:, :], mask[:, 0, 0:n], start=True, stop=True)
                mm(ps[:, 6, n:2 * n], ones[:, :], mask[:, 0, 0:n], start=True, stop=False)
                mm(ps[:, 6, n:2 * n], before[:, :], mask[:, 1, 0:n], start=False, stop=True)
                mm(ps[:, 6, 2 * n:3 * n], ones[:, :], mask[:, 0, 0:n], start=True, stop=False)
                stage.raise_by(mm(ps[:, 6, 2 * n:3 * n], ones[:, :], mask[:, 1, 0:n], start=False, stop=True), "places")

            turn_x(xn, m1p, "xT", lambda t: [m1d(f"xn {t}"), dve_f("x1 1")])
            pe.wait_ge(ld_rtr, 16 * 5)
            pe.wait_ge(*m1d("xT 3"))
            logits(NG, wg_sb, 0)
            m1p.raise_by(logits(E1, we_sb, 8), "logits")
            pe.wait_ge(*m1d("mask"))
            places(m1p, E1)

            def quad_pe(it):
                pe.wait_ge(q_sel, it + 1)
                for k in range(KD):
                    for t in range(TT):
                        ins = mm(ps[:, k // 4, (k % 4) * P:(k % 4 + 1) * P], by8(xn[:, t, :])[:, k, :], ga_sel[:, t, :],
                                 start=(t == 0), stop=(t == TT - 1))
                ins.then_inc(q_gath, 1)
                for t in range(TT):
                    ins = turn_(ps[:, 3, 256 + t * P:256 + (t + 1) * P], sc_sel[:, t, :], ident[:, :])
                ins.then_inc(q_turn, 1)
                pe.wait_ge(q_xg, it + 1)
                for n in range(2):
                    for j in range(4):
                        pe.wait_ge(piece1[half_place(4 * n + j)], (it + 1) * 16)
                    for k in range(KD):
                        for j in range(4):
                            at = half_place(4 * n + j) * HALFP
                            ins = mm(ps[32 * j:32 * j + 32, 2, n * F1:(n + 1) * F1], xg[:, k, 32 * j:32 * j + 32],
                                     ring[:, at + k * F1:at + (k + 1) * F1], start=(k == 0), stop=(k == KD - 1),
                                     tile_position=(0, 32 * j))
                    ins.then_inc(used1, 4)
                pe.wait_ge(q_hid, it + 1)
                for c in range(2):
                    ins = turn_(ps[:, 3, c * P:(c + 1) * P], hh[:, 0, 0:F1].rearrange("p (q c) -> p c q", c=2)[:, c, :], ident[:, :])
                ins.then_inc(q_hT, 1)
                pe.wait_ge(q_hTs, it + 1)
                for j in range(4):
                    pe.wait_ge(piece1[half_place(8 + j)], (it + 1) * 16)
                for n in range(2):
                    for c in range(2):
                        for j in range(4):
                            at = half_place(8 + j) * HALFP + c * D + n * 512
                            ins = mm(ps[32 * j:32 * j + 32, 4 + n, :], hT[:, c, 32 * j:32 * j + 32], ring[:, at:at + 512],
                                     start=(c == 0), stop=(c == 1), tile_position=(0, 32 * j))
                ins.then_inc(used1, 4)
                pe.wait_ge(q_yg, it + 1)
                pe.wait_ge(q_scT, it + 1)
                for t in range(TT):
                    if t == 1:
                        pe.wait_ge(q_add, 2 * it + 2)
                    for n in range(2):
                        ins = mm(ps[:, 6 + n, :], sc_T[:, t, :], yg[:, n * 512:(n + 1) * 512], start=True, stop=True)
                    ins.then_inc(q_scat, 1)

            with pe.Fori(0, NQ) as q:
                quad_pe(q)
            extra = pe.value_load(over_i[0:1, 0:1], min_val=0, max_val=S // CAP1 - 1)
            with pe.If(extra > 0):
                with pe.Fori(1, extra + 1) as r:
                    with pe.Fori(0, NQ) as q:
                        quad_pe(r * NQ + q)
                pe.drain().then_inc(more_done1, 1)

            def has(n):
                pe.wait_ge(landed[(n + 1) % PLACES], 16 * (n // PLACES + 1))

            def mixer_pe(l, n0):
                turn_x(x_sb, bp, f"xT mix {l}", lambda t: [m1d("done") if l == 0 else bd(f"x 0 {t}")])
                if l == 0:
                    pe.wait_ge(ld_conv, 16)
                ins = turn_(ps[:, 6, 0:CW * NPC], conv_rows[0:CW * NPC, l, :], ident[0:CW * NPC, 0:CW * NPC])
                bp.raise_by(ins, f"taps {l}")
                has(n0)
                has(n0 + 1)
                pe.wait_ge(*ba(f"xT mix {l} 3"))

                def project(n, i, bank, half):
                    w = chunked(place(n0 + n), 512)
                    for k in range(KD):
                        ins = mm(ps[:, bank, half * S:(half + 1) * S], w[:, k, i * P:(i + 1) * P], xT[:, k, :], start=(k == 0),
                                 stop=(k == KD - 1))
                    return ins

                for i in range(NPC):
                    project(0, i, i, 0)
                    ins = project(1, i, i, 1)
                    if i < NPC - 1:
                        bp.raise_by(ins, f"conv in {l} {i}")
                    else:
                        ins.then_inc(used, 2)
                has(n0 + 2)
                for i in range(NPC):
                    ins = project(2, i, 4 + i // 2, i % 2)
                ins.then_inc(used, 1)
                pe.wait_ge(*ba(f"diagonals {l}"))
                pe.wait_ge(*bd(f"conv in {l} {NPC - 1}"))
                for tap in range(CW):
                    ins = mm(ps[:, 0, 0:S], diag(tap), vp[:, NPC - 1, tap:tap + S], start=(tap == 0), stop=(tap == CW - 1))
                bp.raise_by(ins, f"conv 3 {l}")
                has(n0 + 3)
                pe.wait_ge(ld_pool, 16 * (l + 1))
                pe.wait_ge(pooled_x, l + 1)
                for g in range(NPC):
                    w = place(n0 + 3)[:, 4 * 512 + g * P:4 * 512 + (g + 1) * P]
                    ins = mm(ps[:, 6 + g // 2, (g % 2) * S:(g % 2 + 1) * S], w, pooled[:, g, :], start=True, stop=True)
                bp.raise_by(ins, f"pool {l}")
                pe.wait_ge(*bd(f"conv {l}"))
                pe.wait_ge(*ba(f"conv 3 {l}"))
                for j in range(NPC):
                    ins = mm(ps[:, 5, 0:S], ones[:, :], yv[:, j, :], start=(j == 0), stop=(j == NPC - 1))
                bp.raise_by(ins, f"conv sum {l}")
                pe.wait_ge(*ba(f"squares {l}"))
                for j in range(NPC):
                    ins = mm(ps[:, 5, S:2 * S], ones[:, :], sv[:, j, :], start=(j == 0), stop=(j == NPC - 1))
                bp.raise_by(ins, f"conv squares {l}")
                pe.wait_ge(*ba(f"silu {l}"))
                pw = place(n0 + 3)[:, 0:4 * 512].rearrange("p (k n) -> p k n", k=4)
                for j in range(NPC):
                    for k in range(NPC):
                        ins = mm(ps[:, 2 + j // 2, (j % 2) * S:(j % 2 + 1) * S], pw[:, k, j * P:(j + 1) * P], sv[:, k, :],
                                 start=(k == 0), stop=(k == NPC - 1))
                ins.then_inc(used, 1)
                pe.wait_ge(*bd(f"pool out {l}"))
                pe.wait_ge(*ba(f"conv out {l}"))
                has(n0 + 4)
                has(n0 + 5)
                wo = [place(n0 + 4 + a).rearrange("p (k n) -> p k n", k=4) for a in range(2)]
                for t in range(TT):
                    for n in range(2):
                        for k in range(KD):
                            ins = mm(ps[:, 4 + 2 * t + n, :], mT[:, k, t * P:(t + 1) * P],
                                     wo[k // 4][:, k % 4, n * 512:(n + 1) * 512], start=(k == 0), stop=(k == KD - 1))
                    if t == 0:
                        bp.raise_by(ins, f"mix {l}")
                    else:
                        ins.then_inc(used, 2)

            def ple_pe(l, n0, last):
                pe.wait_ge(ld_p, 16 * TT * (l + 1))
                pe.wait_ge(*bd(f"ffn {l}"))
                for k in range(2):
                    for t in range(TT):
                        ins = turn_(ps[:, 0, k * S + t * P:k * S + (t + 1) * P], p_sb[t][:, k * P:(k + 1) * P], ident[:, :])
                bp.raise_by(ins, f"pT {l}")
                if last:
                    pe.wait_ge(ld_ple_w, 16)
                else:
                    has(n0)
                wp = place(n0)[:, 0:2 * D].rearrange("p (k n) -> p k n", k=2)
                pe.wait_ge(*ba(f"pT {l}"))
                for t in range(TT):
                    for n in range(2):
                        for k in range(2):
                            ins = mm(ps[:, 4 + 2 * t + n, :], pT[:, k, t * P:(t + 1) * P], wp[:, k, n * 512:(n + 1) * 512],
                                     start=(k == 0), stop=(k == 1))
                if last:
                    bp.raise_by(ins, f"ple {l}")
                else:
                    ins.then_inc(used, 1)
                if last:
                    pe.wait_ge(ld_gate_w, 16 * 2)
                else:
                    has(n0 + 1)
                    has(n0 + 2)
                wg = [place(n0 + 1 + a).rearrange("p (k n) -> p k n", k=4) for a in range(2)]
                for t in range(TT):
                    turn_tile(x_sb, bp, f"xT ple {l}", t, [bd(f"ln2 {l} {t}")])
                    pe.wait_ge(*ba(f"xT ple {l} {2 * t + 1}"))
                    for n in range(2):
                        for k in range(KD):
                            ins = mm(ps[:, 2 * t + n, :], xT[:, k, t * P:(t + 1) * P], wg[k // 4][:, k % 4, n * 512:(n + 1) * 512],
                                     start=(k == 0), stop=(k == KD - 1))
                    if last or t == 0:
                        bp.raise_by(ins, f"ple gate {l} {t}")
                    else:
                        ins.then_inc(used, 2)

            mixer_pe(0, MIX0)
            turn_x(x_sb, bp, "xT ffn 0", lambda t: [bd(f"ln1 0 {t}")])
            pe.wait_ge(*ba("xT ffn 0 3"))

            def dense_down(u, t):
                n_c = UD[u] // P
                n2 = DENSE0 + DENSE.index(("w2", u))
                if t == 0:
                    has(n2)
                pe.wait_ge(*bd(f"hT {u} {t}"))
                w = place(n2)[:, 0:n_c * D].rearrange("p (c n) -> p c n", c=n_c)
                for n in range(2):
                    for c in range(n_c):
                        ins = mm(ps[:, 4 + 2 * t + n, :], hT[:, c, :], w[:, c, n * 512:(n + 1) * 512], start=(u == 0 and c == 0),
                                 stop=(u == len(UD) - 1 and c == n_c - 1))
                if t == 1:
                    ins.then_inc(used, 1)

            def dense_turn(u, t):
                n_c = UD[u] // P
                pe.wait_ge(*bd(f"hidden {u} {t}"))
                v = hh[:, t, 0:UD[u]].rearrange("p (q c) -> p c q", c=n_c)
                for c in range(n_c):
                    ins = turn_(ps[:, 3, c * P:(c + 1) * P], v[:, c, :], ident[:, :])
                bp.raise_by(ins, f"hT {u} {t}")

            before_ = None
            for u in range(len(UD)):
                n1, n3 = DENSE0 + DENSE.index(("w1", u)), DENSE0 + DENSE.index(("w3", u))
                has(n1)
                has(n3)
                for t in range(TT):
                    if u > 0:
                        pe.wait_ge(*ba(f"silu {u - 1} {t}"))
                    for k in range(KD):
                        ins = mm(ps[:, t, 0:UD[u]], xT[:, k, t * P:(t + 1) * P], chunked(place(n1), UD[u])[:, k, :],
                                 start=(k == 0), stop=(k == KD - 1))
                    if t == 1:
                        ins.then_inc(used, 1)
                    if before_:
                        dense_turn(*before_)
                    for k in range(KD):
                        ins = mm(ps[:, 2, 0:UD[u]], xT[:, k, t * P:(t + 1) * P], chunked(place(n3), UD[u])[:, k, :],
                                 start=(k == 0), stop=(k == KD - 1))
                    if t == 0:
                        bp.raise_by(ins, f"up {u}")
                    else:
                        ins.then_inc(used, 1)
                    if before_:
                        dense_down(*before_)
                    before_ = (u, t)
            dense_turn(*before_)
            dense_down(*before_)
            ple_pe(0, PLE0, False)
            mixer_pe(1, MIX1)
            turn_x(x_sb, bp, "xT ffn 1", lambda t: [bd(f"ln1 1 {t}")])
            pe.wait_ge(*ba("xT ffn 1 3"))
            bp.raise_by(logits(E2, w_router, 8), "logits")
            pe.wait_ge(*bd("mask"))
            places(bp, E2)

            def gather(n):
                pe.wait_ge(e_sel, n)
                for k in range(KD):
                    for t in range(TT):
                        ins = mm(ps[:, 6 + k // 4, (k % 4) * P:(k % 4 + 1) * P], by8(xn[:, t, :])[:, k, :], ga_sel[:, t, :],
                                 start=(t == 0), stop=(t == TT - 1))
                ins.then_inc(e_gath, 1)

            def scatter(n, t):
                if t == 0:
                    pe.wait_ge(e_scT, n)
                    pe.wait_ge(e_yg, n)
                else:
                    pe.wait_ge(e_add, 2 * n)
                for h in range(2):
                    ins = mm(ps[:, 6 + h, :], sc_T[:, t, :], yg[:, h * 512:(h + 1) * 512], start=True, stop=True)
                ins.then_inc(e_scat, 1)

            def expert_pe(e, r, halves):
                it, n9 = e + r * E2, e + (r * (E2 + 1) + 1)
                fh, slots_h = 512 // halves, P // halves
                pe.wait_ge(e_xg, n9)

                def has_piece(what, u):
                    n = MOE0 + MOE.index((what, u))
                    pe.wait_ge(landed[(n + 1) % PLACES], it * (16 * len(MOE) // PLACES) + 16 * (n // PLACES + 1))
                    return place(n)

                def side(j):
                    return slice(slots_h * j, slots_h * (j + 1)), dict(tile_position=(0, slots_h * j)) if halves > 1 else {}

                def rows_of(what, u, bank):
                    w = chunked(has_piece(what, u), 512)
                    w = w.rearrange("p k (q c) -> p k q c", c=4)
                    n_c = 4 // halves
                    for k in range(KD):
                        for j in range(halves):
                            cols_j, tile = side(j)
                            ins = mm(ps[cols_j, bank, 0:fh], xg[:, k, cols_j], w[:, k, :, n_c * j:n_c * (j + 1)], start=(k == 0),
                                     stop=(k == KD - 1), **tile)
                    ins.then_inc(used, 1)

                def turn_hidden(u):
                    pe.wait_ge(e_hid, it * UNITS + (u + 1))
                    v = hh[:, u % 2, 0:fh].rearrange("p (q c) -> p c q", q=P)
                    for c in range(4 // halves):
                        ins = turn_(ps[:, 3, c * P:(c + 1) * P], v[:, c, :], ident[:, :])
                    ins.then_inc(e_hT, 1)

                def down(u):
                    w = has_piece("w2", u).rearrange("p (c n) -> p c n", c=4)
                    pe.wait_ge(e_hTs, it * UNITS + (u + 1))
                    first, final = u == 0, u == UNITS - 1
                    if halves == 1:
                        for n in range(2):
                            for c in range(4):
                                ins = mm(ps[:, 4 + n, :], hT[:, c, :], w[:, c, n * 512:(n + 1) * 512], start=(first and c == 0),
                                         stop=(final and c == 3))
                    else:
                        for c in range(4):
                            for n in range(2):
                                rows_n, tile = side(n)
                                ins = mm(ps[rows_n, 4 + n, :], hT[:, c % 2, side(c // 2)[0]], w[:, c, n * 512:(n + 1) * 512],
                                         start=(first and c == 0), stop=(final and c == 3), **tile)
                    ins.then_inc(used, 1)

                for u in range(UNITS):
                    rows_of("w1", u, u % 2)
                    if u > 0:
                        turn_hidden(u - 1)
                    if u == 1:
                        scatter(n9, 1)
                    rows_of("w3", u, 2)
                    if u == 0:
                        scatter(n9, 0)
                        if halves > 1:
                            for n in range(2):
                                rows_n, tile = side(1 - n)
                                mm(ps[rows_n, 4 + n, :], zero[:, 0:slots_h], spread(ones[:, :], 1, 4), start=True, stop=True, **tile)
                    if u > 0:
                        down(u - 1)
                    if u == 2:
                        pe.wait_ge(e_add, 2 * n9 + 1)
                        for t in range(TT):
                            ins = turn_(ps[:, 6, t * P:(t + 1) * P], sc_sel[:, t, :], ident[:, :])
                        ins.then_inc(e_turn, 1)
                gather(n9 + 1)
                turn_hidden(UNITS - 1)
                down(UNITS - 1)

            def pass_end(r):
                n = (r + 1) * (E2 + 1)
                pe.wait_ge(e_xg, n)
                for t in range(TT):
                    scatter(n, t)

            gather(1)
            with pe.Fori(0, E2) as e:
                small_one = pe.value_load(small_i[0:1, bass.ds(e, 1)], min_val=0, max_val=1)
                with pe.If(small_one > 0):
                    expert_pe(e, 0, 2)
                with pe.If(small_one < 1):
                    expert_pe(e, 0, 1)
            pass_end(0)
            extra2 = pe.value_load(over_i[0:1, 0:1], min_val=0, max_val=S // CAP2 - 1)
            with pe.If(extra2 > 0):
                gather(E2 + 2)
                with pe.Fori(0, E2) as e:
                    expert_pe(e, 1, 1)
                pass_end(1)
                pe.drain().then_inc(more_done2, 1)
            ple_pe(1, PLE1, True)

        @block.vector
        def _(dve):
            count = [0]
            tt, ts, stt, red, rec, cp = (dve.tensor_tensor, dve.tensor_scalar, dve.scalar_tensor_tensor, dve.tensor_reduce,
                                         dve.reciprocal, dve.tensor_copy)

            def link(ins):
                count[0] += 1
                ins.then_inc(dve_step, 1)
                dve.wait_ge(dve_step, count[0])

            def mark(stage, ins, name):
                stage.raise_by(ins, name)
                dve.wait_ge(*stage(name))

            dve.wait_ge(*act_f("x squares 1"))
            mark(dve_f, ts(ss_x, ss_x, 1.0 / D, EPS, ALU.mult, ALU.add), "x var")
            dve.wait_ge(*act_f("x std"))
            link(rec(rs_x, rs_x))
            for t in range(TT):
                mark(dve_f, ts(xn[:, t, :], x_sb[:, t, :], rs_x[:, t:t + 1], None, ALU.mult), f"xn {t}")
            dve.wait_ge(ld_front, 16 * 11)
            for t in range(TT):
                for g in range(2):
                    dve.wait_ge(*pe_f(f"xT {t} {g}"))
                    mark(dve_f, tt(xT[:, 4 * g:4 * g + 4, t * P:(t + 1) * P], ps[:, 2 * t + g, :].rearrange("p (k t) -> p k t", k=4),
                                   spread(gcol[:, 0, 4 * g:4 * g + 4], 2, P), ALU.mult), f"xT {t} {g}")
            mark(dve_f, cp(cols[:, :], ps[:, 7, 0:NROWS]), "cols")
            link(cp(posf, pos_i[:, :]))
            dve.wait_ge(*consts("all"))
            link(tt(ang, spread(inv_freq, 1, 2), spread(posf, 2, HALF), ALU.mult))
            magic = 12582912.0
            for n in range(2):
                link(ts(turn[:, n], ang, 1.0 / TWO_PI, 0.25 * n, ALU.mult, ALU.add))
                link(ts(turn[:, n], turn[:, n], magic, None, ALU.add))
                link(ts(trig[:, n], turn[:, n], -magic, None, ALU.add))
                link(stt(turn[:, n], trig[:, n], -6.28125, ang, ALU.mult, ALU.add))
                link(stt(turn[:, n], trig[:, n], -0.0019350051879882812, turn[:, n], ALU.mult, ALU.add))
                link(stt(turn[:, n], trig[:, n], -(TWO_PI - 6.28125 - 0.0019350051879882812), turn[:, n], ALU.mult, ALU.add))
                if n == 1:
                    link(ts(turn[:, n], turn[:, n], TWO_PI / 4, None, ALU.add))
                link(ts(turn[:, n], turn[:, n], 3.1415925, -3.1415925, ALU.min, ALU.max))
            dve.wait_ge(*act_f("c squares"))
            link(ts(ss_c[:, :, 0:1], ss_c[:, :, 0:1], 1.0 / Q_RANK, EPS, ALU.mult, ALU.add))
            mark(dve_f, ts(ss_c[:, :, 1:2], ss_c[:, :, 1:2], 1.0 / KV_RANK, EPS, ALU.mult, ALU.add), "c var")
            dve.wait_ge(*act_f("c std"))
            link(rec(rs_c, rs_c))
            for t in range(TT):
                link(ts(c_sb[:, t, 0:Q_RANK], c_sb[:, t, 0:Q_RANK], rs_c[:, t, 0:1], None, ALU.mult))
                ins = ts(c_sb[:, t, Q_RANK:Q_RANK + KV_RANK], c_sb[:, t, Q_RANK:Q_RANK + KV_RANK], rs_c[:, t, 1:2], None, ALU.mult)
                if t == 0:
                    link(ins)
            mark(dve_f, ins, "c normed")
            dve.wait_ge(*pe_f("c turned"))
            for i in range(3):
                g = ROWS["g_cq"] + i
                ins = ts(cT[:, i, :], ps[:, i // 2, (i % 2) * S:(i % 2 + 1) * S], cols[:, g:g + 1], None, ALU.mult)
                if i < 2:
                    link(ins)
            mark(dve_f, ins, "cT")
            for t in range(TT):
                dve.wait_ge(*act_f(f"qk squares {t}"))
                link(red(ss_qk[:, t, 0:H], sq[:, t, 0:H * QK].rearrange("p (h d) -> p h d", h=H), AX_X, ALU.add))
                link(red(ss_qk[:, t, H:], sq[:, t, H * QK:].rearrange("p (h d) -> p h d", h=H), AX_X, ALU.add))
                link(ts(ss_qk[:, t, H:], ss_qk[:, t, H:], ss_kr[:, t:t + 1], None, ALU.add))
                mark(dve_f, ts(ss_qk[:, t, :], ss_qk[:, t, :], 1.0 / QK, EPS, ALU.mult, ALU.add), f"qk var {t}")
                dve.wait_ge(*act_f(f"qk std {t}"))
                link(rec(rs_qk[:, t, :], rs_qk[:, t, :]))
                heads = rs_qk[:, t, 0:H].rearrange("p (a b) -> p a b", a=2)
                link(tt(qk[:, t, 0:H, :].rearrange("p (a b) d -> p a b d", a=2),
                        ps[:, 0:2, 0:384].rearrange("p a (b d) -> p a b d", b=4), spread(heads, 3, QK), ALU.mult))
                mark(dve_f, tt(qk[:, t, H:, 0:NOPE], ps[:, 2, :].rearrange("p (h d) -> p h d", h=H),
                               spread(rs_qk[:, t, H:], 2, NOPE), ALU.mult), f"qk read {t}")
                link(tt(qk[:, t, H:, NOPE:], spread(c_sb[:, t, Q_RANK + KV_RANK:], 1, H), spread(rs_qk[:, t, H:], 2, ROPE),
                        ALU.mult))
                link(tt(qk[:, t].rearrange("p (a h) d -> p a h d", a=2), qk[:, t].rearrange("p (a h) d -> p a h d", a=2),
                        spread(gqk, 2, H), ALU.mult))
                dve.wait_ge(*act_f("trig"))
                x1, x2 = qk[:, t, :, NOPE:NOPE + HALF], qk[:, t, :, NOPE + HALF:]
                prod = [rope_t[:, n, :].rearrange("p (h d) -> p h d", h=2 * H) for n in range(4)]
                sin, cos = spread(trig[:, 0, t, :], 1, 2 * H), spread(trig[:, 1, t, :], 1, 2 * H)
                link(tt(prod[0], x1, cos, ALU.mult))
                link(tt(prod[1], x2, sin, ALU.mult))
                link(tt(prod[2], x2, cos, ALU.mult))
                link(tt(prod[3], x1, sin, ALU.mult))
                link(tt(x1, prod[0], prod[1], ALU.subtract))
                ins = tt(x2, prod[2], prod[3], ALU.add)
                if t == 0:
                    link(ins)
            mark(dve_f, ins, "qk")
            dve.wait_ge(*act_f("raw 6"))
            for f in range(NF):
                link(tt(feat[:, f, :], raw[:, f, 0:S], raw[:, f, 1:S + 1], ALU.subtract))
                ins = stt(feat[:, f, :], feat[:, f, :], cols[:, ROWS["mu"] + f:ROWS["mu"] + f + 1], raw[:, f, 1:S + 1],
                          ALU.mult, ALU.add)
                if f < NF - 1:
                    link(ins)
            mark(dve_f, ins, "mixed")
            for t, pr, banks in ((0, probs0, ps[:, 0:2, :]), (1, probs1, ps[:, 2:6, :])):
                n = P * (t + 1)
                dve.wait_ge(*pe_f(f"scores {t}"))
                link(tt(pr, banks.rearrange("p b (a k) -> p (b a) k", k=n), spread(cmask[:, S - n:], 1, H), ALU.add))
                link(red(mx[:, t, :], pr, AX_X, ALU.max))
                mark(dve_f, ts(mx[:, t, :], mx[:, t, :], -(QK ** -0.5), None, ALU.mult), f"max {t}")
            dve.wait_ge(*act_f("probs 1"))
            link(rec(den, den))
            dve.wait_ge(*pe_f("pT 1"))
            mark(dve_f, cp(pT1[:, 8:16, :], ps[:, 2:4, :].rearrange("p b (a t) -> p (b a) t", a=4)), "pT1")
            dve.wait_ge(*pe_f("pv"))
            mark(dve_f, tt(mla.rearrange("p t (h d) -> p t h d", h=H), ps[:, 4:6, :].rearrange("p t (h d) -> p t h d", h=H),
                           spread(den, 3, VD), ALU.mult), "mla")
            dve.wait_ge(*act_f("mla squares"))
            mark(dve_f, ts(ss_x, ss_x, 1.0 / RW, EPS, ALU.mult, ALU.add), "mla var")
            dve.wait_ge(*act_f("mla std"))
            link(rec(rs_x, rs_x))
            link(ts(mla[:, 0, :], mla[:, 0, :], rs_x[:, 0:1], None, ALU.mult))
            mark(dve_f, ts(mla[:, 1, :], mla[:, 1, :], rs_x[:, 1:2], None, ALU.mult), "mla normed")
            dve.wait_ge(*pe_f("mlaT"))
            for b in range(2):
                g = ROWS["g_mla"] + 2 * b
                ins = tt(mixT[:, 2 * b:2 * b + 2, :], ps[:, 6 + b, :].rearrange("p (a t) -> p a t", a=2),
                         spread(cols[:, g:g + 2], 2, S), ALU.mult)
                if b == 0:
                    link(ins)
            mark(dve_f, ins, "mla mixed")

            def col(name):
                return cols[:, ROWS[name]:ROWS[name] + J]

            link(tt(kk_f, k_f, spread(col("k_k"), 2, S), ALU.mult))
            mark(dve_f, tt(tmp_f, kk_f, kk_f, ALU.mult), "kk squares")
            dve.wait_ge(*pe_f("kk sums"))
            mark(dve_f, ts(tmp_f.rearrange("p (b a) t -> p b (a t)", b=2), ps[:, 4:6, :], 1e-12, None, ALU.add), "kk var")
            dve.wait_ge(*act_f("sig w"))
            for j in range(J):
                link(dve.tensor_tensor_scan(cum[:, j, :], rst, sig_f[:, j, :], 0.0, ALU.mult, ALU.add))
            mark(dve_f, tt(d_ex, cum, sig_f, ALU.subtract), "cum")
            dve.wait_ge(*act_f("kk std"))
            link(rec(tmp_f, tmp_f))
            link(tt(kk_f, kk_f, tmp_f, ALU.mult))
            dve.wait_ge(*act_f("sig a"))
            link(stt(tmp_f, a_f, -1.0, spread(col("k_a"), 2, S), ALU.add, ALU.mult))
            link(stt(k_f, tmp_f, 1.0, k_f, ALU.add, ALU.mult))
            link(tt(tmp_f, kk_f, a_f, ALU.mult))
            link(tt(rk_f, r_f, k_f, ALU.mult))
            link(tt(rk_f, rk_f, spread(col("r_k"), 2, S), ALU.mult))
            dve.wait_ge(*act_f("d inv"))
            link(tt(bt_f, tmp_f, d_inv, ALU.mult))
            link(tt(kt_f, k_f, d_inv, ALU.mult))
            dve.wait_ge(*act_f("d inc"))
            link(tt(rt_f, r_f, d_inc, ALU.mult))
            link(cp(d_end, d_inc.rearrange("p j (c t) -> p j c t", t=N)[:, :, :, N - 1]))
            dve.wait_ge(*act_f("d ex"))
            mark(dve_f, tt(kk_f, kk_f, d_ex, ALU.mult), "tilde")
            for t in range(TT):
                dve.wait_ge(*pe_f(f"w_o mla {t}"))
                x_t = x_sb[:, t, :].rearrange("p (b n) -> p b n", b=2)
                mark(dve_f, tt(x_t, x_t, ps[:, 6 - 2 * t:8 - 2 * t, :], ALU.add), f"x mla {t}")
            dve.wait_ge(*pe_f("bonus"))
            mark(dve_f, cp(bonus, ps[:, 6, 0:2 * H].rearrange("p (t h) -> p t h", t=2)), "bonus")
            for t in range(TT):
                for m, kept in enumerate((m_lt, m_le)):
                    dve.wait_ge(*pe_f(f"gram {t} {m}"))
                    link(tt(gram[:, t, m].rearrange("p a (h n) -> p a h n", n=N),
                            ps[:, 4 * t + 2 * m:4 * t + 2 * m + 2, :].rearrange("p a (h n) -> p a h n", n=N),
                            spread(spread(kept, 1, 2 * J), 1, 2), ALU.mult))

            def a_part(t):
                return gram[:, t, 0, :, 0:J * N].rearrange("p a (j n) -> p a j n", n=N)

            def parity(v):
                return v.rearrange("p (a j) n -> p a j n", a=2)

            def flat(v):
                return v.rearrange("p h n -> p (h n)")

            dve.wait_ge(*act_f("turned 2 1"))
            def low_blocks(n, t):
                mark(dve_f, tt(parity(low[:, t]), a_part(t), spread(spread(lvl[:, n, :], 1, J), 1, 2), ALU.mult), f"low {n} {t}")

            for t in range(TT):
                low_blocks(0, t)
            for n in range(len(LVL)):
                for t in range(TT):
                    dve.wait_ge(*pe_f(f"lx {n} {t}"))
                    if n == 0:
                        mark(dve_f, stt(inv[:, t], ps[:, 4 * t, :].rearrange("p (h n) -> p h n", n=N), -1.0,
                                        spread(idh, 1, 2 * J), ALU.mult, ALU.add), f"inv 0 {t}")
                        mark(dve_f, stt(invT[:, t], low[:, t], -1.0, spread(idh, 1, 2 * J), ALU.mult, ALU.add), f"invT 0 {t}")
                    if n < len(LVL) - 1:
                        low_blocks(n + 1, t)
                for t in range(TT) if n > 0 else ():
                    if n < len(LVL) - 1:
                        dve.wait_ge(*pe_f(f"xlx {n} {t}"))
                        mark(dve_f, tt(flat(inv[:, t]), flat(inv[:, t]), ps[:, 4 * t + 1, :], ALU.subtract), f"inv {n} {t}")
                    dve.wait_ge(*pe_f(f"xlxT {n} {t}"))
                    mark(dve_f, tt(flat(invT[:, t]), flat(invT[:, t]), ps[:, 4 * t + 2, :], ALU.subtract), f"invT {n} {t}")
            for t in range(TT):
                dve.wait_ge(*pe_f(f"akv {t}"))
                link(cp(flat(akv[:, t]), ps[:, 6 + t, :]))
            for c in range(NCH):
                t, half = c // 2, slice(N * (c % 2), N * (c % 2) + N)
                if c == 0:
                    mark(dve_f, ts(rn[half], akv[half, t], -1.0, None, ALU.mult), "rn 0")
                else:
                    dve.wait_ge(*pe_f(f"kk s {c}"))
                    mark(dve_f, stt(rn[half].rearrange("p (a j) n -> p a (j n)", a=2), ps[half, 0:2, 0:J * N], -1.0,
                                    akv[half, t].rearrange("p (a j) n -> p a (j n)", a=2), ALU.mult, ALU.subtract), f"rn {c}")
                if c < NCH - 1:
                    dve.wait_ge(*pe_f(f"state {c}"))
                    new = ps[:, 3, 0:J * N].rearrange("p (j n) -> p j n", n=N)
                    end = spread(d_end[:, :, c], 2, N)
                    if c == 0:
                        mark(dve_f, tt(st[:, :, :], new, end, ALU.mult), "state 0")
                    else:
                        link(tt(st2[:, :, :], new, st[:, :, :], ALU.add))
                        dve.wait_ge(*pe_f(f"r s {c}"))
                        mark(dve_f, tt(st[:, :, :], st2[:, :, :], end, ALU.mult), f"state {c}")
                dve.wait_ge(*pe_f(f"y {c}"))
                y_c = y_t[half, t].rearrange("p (j a n) -> p a j n", j=J, a=2)
                ins = cp(y_c, ps[half, 6, :].rearrange("p (a j n) -> p a j n", a=2, n=N))
                if c > 0:
                    link(ins)
                    dve.wait_ge(*pe_f(f"r s {c}"))
                    ins = tt(y_c, y_c, ps[half, 4:6, 0:J * N].rearrange("p a (j n) -> p a j n", n=N), ALU.add)
                mark(dve_f, ins, f"y {c}")
            y_h = y_t.rearrange("p t (h n) -> p (t h) n", n=N)
            q_h = y_q.rearrange("p t (h n) -> p (t h) n", n=N)
            link(red(mean, y_h, AX_X, ALU.add))
            link(ts(mean, mean, 1.0 / N, None, ALU.mult))
            link(tt(y_h, y_h, spread(mean, 2, N), ALU.subtract))
            link(tt(q_h, y_h, y_h, ALU.mult))
            link(red(var, q_h, AX_X, ALU.add))
            mark(dve_f, ts(var, var, 1.0 / N, LNX_EPS, ALU.mult, ALU.add), "y var")
            link(tt(q_h, v_t.rearrange("p t (h n) -> p (t h) n", n=N), spread(bonus.rearrange("p t h -> p (t h)"), 2, N), ALU.mult))
            dve.wait_ge(*act_f("y std"))
            link(rec(var, var))
            link(tt(y_h, y_h, spread(var, 2, N), ALU.mult))
            link(tt(y_t, y_t, spread(lnx[:, 0, :], 1, TT), ALU.mult))
            link(tt(y_t, y_t, spread(lnx[:, 1, :], 1, TT), ALU.add))
            link(tt(y_t, y_t, y_q, ALU.add))
            dve.wait_ge(*act_f("g"))
            mark(dve_f, tt(y_t, y_t, gl_t, ALU.mult), "y gated")
            dve.wait_ge(*pe_f("yT"))
            mark(dve_f, cp(mixT[:, 4:8, :].rearrange("p (b a) t -> p b (a t)", b=2), ps[:, 6:8, :]), "mixT")
            for t in range(TT):
                dve.wait_ge(*pe_f(f"w_o {t}"))
                x_t = x_sb[:, t, :].rearrange("p (b n) -> p b n", b=2)
                mark(dve_f, tt(x_t, x_t, ps[:, 2 * t:2 * t + 2, :], ALU.add), f"x1 {t}")
            m1a, m1d, m1p = m1["act"], m1["dve"], m1["pe"]
            ba, bd, bp = bl["act"], bl["dve"], bl["pe"]

            def top_two(stage, acts, values, n_pad):
                for t in range(TT):
                    link(dve.max(etop[:, t, :], values[:, t, :]))
                    link(dve.max_index(etop_i[:, t, :].bitcast(U32), etop[:, t, :], values[:, t, :]))
                link(cp(esel, etop_i.bitcast(U32)[:, :, 0:2]))
                mark(stage, tt(diffs[:, :, 4:5], etop[:, :, 1:2], etop[:, :, 0:1], ALU.subtract), "diffs")
                dve.wait_ge(*acts("exp"))
                link(ts(w2[:, :, 0:1], diffs[:, :, 4:5], 1.0, None, ALU.add))
                link(rec(w2[:, :, 0:1], w2[:, :, 0:1]))
                link(tt(w2[:, :, 1:2], diffs[:, :, 4:5], w2[:, :, 0:1], ALU.mult))
                link(tt(e_one, spread(spread(iota[:, 0:8], 1, 2), 1, TT), spread(esel, 3, 8), ALU.is_equal))

            def slots(stage, n, cap):
                link(stt(slot[:, :, 0:n], stage_ps(n), 1.0, mask[:, :, 0:n], ALU.add, ALU.mult))
                link(ts(slot[:, :, 0:n], slot[:, :, 0:n], -1.0, None, ALU.add))
                link(red(over, ps[:, 6, 2 * n:3 * n], AX_X, ALU.max))
                link(ts(over8, thr[:, :], float(cap), over, ALU.mult, ALU.is_lt))
                link(red(over, over8, AX_X, ALU.add))
                mark(stage, cp(over_i[:, :], over), "over")

            def stage_ps(n):
                return ps[:, 6, 0:2 * n].rearrange("p (t e) -> p t e", t=TT)

            dve.wait_ge(*m1a("squares 1"))
            mark(m1d, ts(ss_x, ss_x, 1.0 / D, EPS, ALU.mult, ALU.add), "var")
            dve.wait_ge(*m1a("std"))
            link(rec(rs_x, rs_x))
            for t in range(TT):
                mark(m1d, ts(xn[:, t, :], x_sb[:, t, :], rs_x[:, t:t + 1], None, ALU.mult), f"xn {t}")
            for b in range(4):
                t, g = b // 2, b % 2
                dve.wait_ge(*m1p(f"xT {b}"))
                mark(m1d, tt(xT[:, 4 * g:4 * g + 4, t * P:(t + 1) * P], ps[:, b, :].rearrange("p (k t) -> p k t", k=4),
                             spread(gcol[:, 1, 4 * g:4 * g + 4], 2, P), ALU.mult), f"xT {b}")
            link(dve.memset(glog, 2 * NEG))
            dve.wait_ge(*m1p("logits"))
            dve.wait_ge(ld_rtr, 16 * 5)
            link(tt(glog[:, :, 0:NG], ps[:, 4:6, 0:NG], spread(bg_sb, 1, TT), ALU.add))
            link(tt(elog, ps[:, 4:6, 8:8 + E1], spread(be_sb, 1, TT), ALU.add))
            for t in range(TT):
                link(dve.max(gtop[:, t, :], glog[:, t, :]))
                link(dve.max_index(gtop_i[:, t, :].bitcast(U32), gtop[:, t, :], glog[:, t, :]))
            link(cp(gsel, gtop_i.bitcast(U32)[:, :, 0]))
            link(tt(g_one, spread(iota[:, 0:NG], 1, TT), spread(gsel, 2, NG), ALU.is_equal))
            link(tt(spread_g, elog.rearrange("p t (g e) -> p t g e", g=NG), spread(g_one, 3, EG), ALU.mult))
            link(red(in_group, spread_g.rearrange("p t g e -> p t e g"), AX_X, ALU.add))
            link(tt(diffs[:, :, 0:NG], glog[:, :, 0:NG], gtop[:, :, 0:1].to_broadcast([P, TT, NG]), ALU.subtract))
            top_two(m1d, m1a, in_group, 0)
            link(red(gp, diffs[:, :, 0:NG], AX_X, ALU.add))
            link(rec(gp, gp))
            link(tt(w2, w2, spread(gp, 2, 2), ALU.mult))
            link(tt(mask8, e_one[:, :, 0, :], e_one[:, :, 1, :], ALU.add))
            link(tt(e_one, e_one, spread(w2, 3, 8), ALU.mult))
            link(tt(comb8, e_one[:, :, 0, :], e_one[:, :, 1, :], ALU.add))
            link(tt(comb.rearrange("p t (g e) -> p t g e", g=NG), spread(g_one, 3, EG), spread(comb8, 2, NG), ALU.mult))
            mark(m1d, tt(mask.rearrange("p t (g e) -> p t g e", g=NG), spread(g_one, 3, EG), spread(mask8, 2, NG), ALU.mult), "mask")
            dve.wait_ge(*m1p("places"))
            slots(m1d, E1, CAP1)
            dve.memset(over8, 0.0).then_inc(q_add, 1)

            def quad_dve(q, it, shifted=None):
                k4 = bass.ds(dve.snap(q * 4), 4)
                dve.wait_ge(q_add, it * 2 + 1)
                if shifted is not None:
                    dve.wait_ge(q_shift, shifted)
                sel4 = ga_sel.rearrange("p t (j s) -> p t j s", j=4)
                dve.tensor_tensor(sel4, spread(iota_q[:, :].rearrange("p (j s) -> p j s", j=4), 1, TT),
                                  spread(slot[:, :, k4], 3, CAP1), ALU.is_equal).then_inc(q_sel_w, 1)
                dve.wait_ge(q_sel_w, it + 1)
                dve.tensor_tensor(sc_sel.rearrange("p t (j s) -> p t j s", j=4), sel4, spread(comb[:, :, k4], 3, CAP1),
                                  ALU.mult).then_inc(q_sel, 1)
                dve.wait_ge(q_gath, it + 1)
                dve.tensor_tensor(xg[:, :, :], ps[:, 0:2, :].rearrange("p b (k s) -> p (b k) s", k=4), spread(gcol[:, 1, :], 2, P),
                                  ALU.mult).then_inc(q_xg, 1)
                dve.wait_ge(q_silu, it + 1)
                dve.tensor_tensor(hh[:, 0, 0:F1], hs[:, 0, 0:F1], ps[:, 2, F1:2 * F1], ALU.mult).then_inc(q_hid, 1)
                dve.wait_ge(q_hT, it + 1)
                dve.tensor_copy(hT[:, 0:2, :], ps[:, 3, 0:2 * P].rearrange("p (c s) -> p c s", c=2)).then_inc(q_hTs, 1)
                for t in range(TT):
                    dve.wait_ge(q_scat, it * 2 + (t + 1))
                    x_t = x_sb[:, t, :].rearrange("p (b n) -> p b n", b=2)
                    dve.tensor_tensor(x_t, x_t, ps[:, 6:8, :], ALU.add).then_inc(q_add, 1)

            with dve.Fori(0, NQ) as q:
                quad_dve(q, q)
            extra = dve.value_load(over_i[0:1, 0:1], min_val=0, max_val=S // CAP1 - 1)
            with dve.If(extra > 0):
                with dve.Fori(1, extra + 1) as r:
                    dve.tensor_scalar(slot[:, :, :], slot[:, :, :], -float(CAP1), None, ALU.add).then_inc(q_shift, 1)
                    with dve.Fori(0, NQ) as q:
                        quad_dve(q, r * NQ + q, r)
            dve.wait_ge(q_add, 2 * NQ + 1)
            for g, w in enumerate(WINDOWS):
                link(ts(rc[:, g, :], iota[:, 0:16], 1.0, float(w), ALU.add, ALU.min))
            link(rec(rc, rc))
            mark(m1d, dve.memset(up[:, :, 0:16], 0.0), "done")

            def layer_norm(l, which, gain, bias, t):
                x_t = x_sb[:, t, :]
                for b in range(2):
                    link(dve.bn_stats(stats[:, t, b, :], x_sb[:, t, b * 512:(b + 1) * 512]))
                link(dve.bn_aggr(mv[:, t, :], stats[:, t].rearrange("p b n -> p (b n)")))
                mark(bd, ts(rstd[:, t:t + 1], mv[:, t, 1:2], LN_EPS, None, ALU.add), f"{which} var {l} {t}")
                if t == 0:
                    dve.wait_ge(ld_lnp, 16 * 4 * (l + 1))
                link(stt(x_t, x_t, mv[:, t, 0:1], lnp[:, gain, :], ALU.subtract, ALU.mult))
                dve.wait_ge(*ba(f"{which} std {l} {t}"))
                link(rec(rstd[:, t:t + 1], rstd[:, t:t + 1]))
                mark(bd, stt(x_t, x_t, rstd[:, t:t + 1], lnp[:, gain + 1, :], ALU.mult, ALU.add), f"{which} {l} {t}")

            def mixer_dve(l):
                if l > 0:
                    link(dve.memset(up[:, :, 0:16], 0.0))
                mark(bd, dve.memset(vp[:, :, 0:CW - 1], 0.0), f"pads {l}")
                dve.wait_ge(*bp(f"taps {l}"))
                mark(bd, cp(cw.rearrange("p j c -> p (j c)"), ps[:, 6, 0:CW * NPC]), f"taps {l}")

                def conv_in(j):
                    dve.wait_ge(*ba(f"gate {l} {j}"))
                    mark(bd, tt(vp[:, j, CW - 1:], sv[:, j, :], ps[:, j, 0:S], ALU.mult), f"conv in {l} {j}")

                for n, (j, tap) in enumerate((j, tap) for j in range(NPC - 1) for tap in range(CW)):
                    if n % 13 == 0 and n // 13 < NPC:
                        conv_in(n // 13)
                    b = ROWS["conv_b"] + l * NPC + j
                    if tap == 0:
                        link(ts(yv[:, j, :], vp[:, j, 0:S], cw[:, 0, j:j + 1], cols[:, b:b + 1], ALU.mult, ALU.add))
                    else:
                        ins = stt(yv[:, j, :], vp[:, j, tap:tap + S], cw[:, tap, j:j + 1], yv[:, j, :], ALU.mult, ALU.add)
                        if (j, tap) < (NPC - 2, CW - 1):
                            link(ins)
                        else:
                            mark(bd, ins, f"conv {l}")
                dve.wait_ge(*bp(f"pool {l}"))
                g = ROWS["pool_scale"] + l * NPC
                mark(bd, tt(mT[:, 0:4, :].rearrange("p (b a) t -> p b a t", b=2), ps[:, 6:8, :].rearrange("p b (a t) -> p b a t", a=2),
                            spread(cols[:, g:g + 4].rearrange("p (b a) -> p b a", b=2), 3, S), ALU.mult), f"pool out {l}")
                dve.wait_ge(*ba(f"conv 3 {l}"))
                dve.wait_ge(*bp(f"conv sum {l}"))
                link(ts(mean_b, ps[:, 5, 0:S], 1.0 / D_CONV, None, ALU.mult))
                mark(bd, tt(yv, yv, spread(mean_b, 1, NPC), ALU.subtract), f"centred {l}")
                dve.wait_ge(*bp(f"conv squares {l}"))
                mark(bd, ts(rstd_b, ps[:, 5, S:2 * S], 1.0 / D_CONV, LN_EPS, ALU.mult, ALU.add), f"conv var {l}")
                dve.wait_ge(*ba(f"conv std {l}"))
                link(rec(rstd_b, rstd_b))
                mark(bd, tt(yv, yv, spread(rstd_b, 1, NPC), ALU.mult), f"conv normed {l}")
                for t in range(TT):
                    dve.wait_ge(*(bp(f"mix {l}") if t == 0 else read((MIX0, MIX1)[l] + 5)))
                    b = 4 + 2 * t
                    x_t = x_sb[:, t, :].rearrange("p (b n) -> p b n", b=2)
                    link(stt(x_t, x_t, ALPHA, ps[:, b:b + 2, :], ALU.mult, ALU.add))
                    layer_norm(l, "ln1", 0, 1, t)

            def tail_dve(l):
                for t in range(TT):
                    layer_norm(l, "ln2", 2, 3, t)
                dve.wait_ge(*(read(PLE0) if l == 0 else bp("ple 1")))
                for t in range(TT):
                    dve.wait_ge(*ba(f"ple gate {l} {t}"))
                    g_t = gate_s[:, t, :].rearrange("p (b n) -> p b n", b=2)
                    link(tt(g_t, g_t, ps[:, 4 + 2 * t:6 + 2 * t, :], ALU.mult))
                    mark(bd, tt(x_sb[:, t, :], x_sb[:, t, :], gate_s[:, t, :], ALU.add), f"x {l} {t}")

            mixer_dve(0)
            for u in range(len(UD)):
                for t in range(TT):
                    dve.wait_ge(*ba(f"silu {u} {t}"))
                    mark(bd, tt(hh[:, t, 0:UD[u]], hs[:, t, 0:UD[u]], ps[:, 2, 0:UD[u]], ALU.mult), f"hidden {u} {t}")
                    dve.wait_ge(*bp(f"hT {u} {t}"))
                    n_c = UD[u] // P
                    mark(bd, cp(hT[:, 0:n_c, :].rearrange("p c s -> p (c s)"), ps[:, 3, 0:UD[u]]), f"hT {u} {t}")
            dve.wait_ge(*read_dense("w2", len(UD) - 1))
            for t in range(TT):
                x_t = x_sb[:, t, :].rearrange("p (b n) -> p b n", b=2)
                ins = stt(x_t, x_t, ALPHA, ps[:, 4 + 2 * t:6 + 2 * t, :], ALU.mult, ALU.add)
                if t == 0:
                    link(ins)
            mark(bd, ins, "ffn 0")
            tail_dve(0)
            mixer_dve(1)
            dve.wait_ge(*bp("logits"))
            link(cp(in_group, ps[:, 4:6, 8:8 + E2]))
            link(dve.memset(diffs[:, :, 0:4], 0.0))
            top_two(bd, ba, in_group, 0)
            mark(bd, tt(mask[:, :, 0:E2], e_one[:, :, 0, :], e_one[:, :, 1, :], ALU.add), "mask")
            link(tt(e_one, e_one, spread(w2, 3, 8), ALU.mult))
            link(tt(comb[:, :, 0:E2], e_one[:, :, 0, :], e_one[:, :, 1, :], ALU.add))
            dve.wait_ge(*bp("places"))
            slots(bd, E2, CAP2)
            link(ts(small_e, ps[:, 6, 2 * E2:3 * E2], float(SMALL), None, ALU.is_le))
            link(cp(small_i[:, :], small_e))
            link(dve.memset(slot[:, :, E2:E2 + 1], -1.0))
            link(dve.memset(comb[:, :, E2:E2 + 1], 0.0))
            link(dve.memset(slot_hi, -1.0))
            link(stt(slot_hi[:, :, 0:E2], spread(small_e, 1, TT), float(SMALL), slot[:, :, 0:E2], ALU.mult, ALU.add))
            dve.wait_ge(*ba("x kept 1"))
            ts(x_sb[:, :, :], x_sb[:, :, :], ALPHA, None, ALU.mult).then_inc(e_add, 1)

            def select(k, n):
                for half, of in ((slice(0, SMALL), slot), (slice(SMALL, P), slot_hi)):
                    dve.tensor_tensor(ga_sel[:, :, half], spread(iota[:, half], 1, TT),
                                      of[:, :, k].to_broadcast([P, TT, SMALL]), ALU.is_equal).then_inc(e_sel_w, 1)
                dve.wait_ge(e_sel_w, 2 * n)
                dve.tensor_tensor(sc_sel, ga_sel, comb[:, :, k].to_broadcast([P, TT, P]), ALU.mult).then_inc(e_sel, 1)

            def take_x(n):
                dve.wait_ge(e_gath, n)
                dve.tensor_copy(xg[:, :, :].rearrange("p (b k) s -> p b (k s)", b=2), ps[:, 6:8, :]).then_inc(e_xg, 1)

            def add_y(n, t):
                dve.wait_ge(e_scat, 2 * n + (t - 1))
                x_t = x_sb[:, t, :].rearrange("p (b n) -> p b n", b=2)
                dve.tensor_tensor(x_t, x_t, ps[:, 6:8, :], ALU.add).then_inc(e_add, 1)

            def expert_dve(e, r):
                it, n9 = e + r * E2, e + (r * (E2 + 1) + 1)
                k_next = bass.ds(dve.snap(e + 1), 1)
                for u in range(UNITS):
                    b = u % 2
                    dve.wait_ge(used, it * len(MOE) + read_moe("w3", u))
                    dve.wait_ge(e_silu, it * UNITS + (u + 1))
                    dve.tensor_tensor(hh[:, b, :], hs[:, b, :], ps[:, 2, :], ALU.mult).then_inc(e_hid, 1)
                    if u == 0:
                        add_y(n9, 0)
                    if u == UNITS - 1:
                        take_x(n9 + 1)
                    dve.wait_ge(e_hT, it * UNITS + (u + 1))
                    dve.tensor_copy(hT[:, :, :].rearrange("p c s -> p (c s)"), ps[:, 3, :]).then_inc(e_hTs, 1)
                    if u == 0:
                        add_y(n9, 1)
                    if u == 3:
                        dve.wait_ge(e_turn, it + 1)
                        select(k_next, n9 + 1)

            def pass_dve(r):
                dve.memset(sc_T, 0.0).then_inc(e_scT, 1)
                dve.memset(yg, 0.0).then_inc(e_yg, 1)
                select(slice(0, 1), r * (E2 + 1) + 1)
                take_x(r * (E2 + 1) + 1)
                with dve.Fori(0, E2) as e:
                    expert_dve(e, r)
                for t in range(TT):
                    add_y((r + 1) * (E2 + 1), t)

            pass_dve(0)
            extra2 = dve.value_load(over_i[0:1, 0:1], min_val=0, max_val=S // CAP2 - 1)
            with dve.If(extra2 > 0):
                for shifted in (slot_hi, slot):
                    dve.tensor_scalar(shifted[:, :, 0:E2], slot[:, :, 0:E2], -float(CAP2), None, ALU.add).then_inc(e_shift, 1)
                dve.wait_ge(e_shift, 2)
                dve.wait_ge(e_add, 2 * (E2 + 1) + 1)
                pass_dve(1)
            dve.wait_ge(e_add, 2 * (E2 + 1) + 1)
            mark(bd, dve.memset(stats, 0.0), "ffn 1")
            tail_dve(1)


INPUTS = ["x", "positions", "g_mix", "w_in", "g_cq", "w_uq", "g_ckv", "w_uk", "w_uv", "g_qn", "g_kn", "g_mla_out", "rw_mu",
          "rw_w0", "rw_w2", "rw_a0", "rw_a2", "rw_g2", "rw_k_k", "rw_k_a", "rw_r_k", "rw_lnx_g", "rw_lnx_b", "w_o", "g_ffn",
          "w_group", "b_group", "w_expert", "b_expert", "w_gate", "w_up", "w_down", "p_2", "w_in_2", "pool_w_2",
          "pool_scale_2", "conv_w_2", "conv_b_2", "conv_ln_g_2", "conv_ln_b_2", "conv_pw_2", "w_out_2", "ln1_g_2", "ln1_b_2",
          "dense_w1_2", "dense_w3_2", "dense_w2_2", "router_w_2", "exp_w1_2", "exp_w3_2", "exp_w2_2", "ln2_g_2", "ln2_b_2",
          "ple_gate_w_2", "ple_w_2"]


def kernel(**inputs):
    import concourse.bacc as bacc
    from concourse.bass_utils import run_bass_kernel_spmd

    nc = bacc.Bacc("TRN2", target_bir_lowering=False, num_devices=1)
    arrays, args = {}, {}
    for name in INPUTS:
        a = np.ascontiguousarray(inputs[name])
        arrays[f"in_{name}"] = a
        args[name] = nc.dram_tensor(f"in_{name}", a.shape, mybir.dt.from_np(a.dtype), kind="ExternalInput").ap()
    out = nc.dram_tensor("out_0", (1, S, D), F32, kind="ExternalOutput").ap()
    build(nc, out=out, **args)
    r = run_bass_kernel_spmd(nc, [arrays], core_ids=[0])
    return r.results[0]["out_0"]
```
